# Optimizing a Trainium2 kernel written in Bass

```python
import jax, jax.numpy as jnp
from jax import lax
import numpy as np

D_MODEL = 1024
BATCH = 1
SEQ = 128
DEPTH = 2
DEC_BATCH = 1
DEC_SEQ = 256
PAST_LEN = 128

GRID_W = 64
N_EVEN = (DEPTH + 1) // 2
N_ODD = DEPTH // 2
EPS = 1e-6
GLA_HEADS = 4
GLA_DK = 64
GLA_DV = 128
GLA_LOWRANK = 16
GLA_GATE_TEMP = 16.0
GLA_CHUNK = 64
ATT_HEADS = 8
ATT_KV_HEADS = 2
ATT_GROUP = ATT_HEADS // ATT_KV_HEADS
ATT_HD = 64
WINDOW = 128
ATT_BLOCK = 128
ROPE_BASE = 10000.0
ROPE_AXIS_DIMS = ATT_HD // 2
NEG = -1e30
IN_WIDTHS = (GLA_HEADS * GLA_DK, GLA_HEADS * GLA_DK, GLA_HEADS * GLA_DV, GLA_HEADS * GLA_DV,
             ATT_HEADS * ATT_HD, ATT_KV_HEADS * ATT_HD, ATT_KV_HEADS * ATT_HD, 2 * GLA_LOWRANK)
IN_WIDTH = sum(IN_WIDTHS)
IN_SPLITS = tuple(int(v) for v in np.cumsum(IN_WIDTHS)[:-1])
MIX_WIDTH = GLA_HEADS * GLA_DV + ATT_HEADS * ATT_HD
RWKV_HEAD = 64
RWKV_HEADS = D_MODEL // RWKV_HEAD
W_LORA = 64
A_LORA = 64
G_LORA = 128
RWKV_LN_EPS = 64e-5
N_GROUPS = 4
EXP_PER_GROUP = 4
N_EXPERTS = N_GROUPS * EXP_PER_GROUP
TOP_K = 2
D_EXPERT = 512

kernel_name = "hybrid_diffusion_gla_swa_rwkv7_hmoe_step"

f32 = jnp.float32

def rmsnorm(x, w):
    xf = x.astype(f32)
    y = xf * lax.rsqrt(jnp.mean(xf * xf, axis=-1, keepdims=True) + EPS)
    return (y * w.astype(f32)).astype(x.dtype)

def ada_mod(cond, w, b):
    mod = jax.nn.silu(cond) @ w + b
    return [m[:, None, :] for m in jnp.split(mod, 6, axis=-1)]

def modulate(x, shift, scale):
    return x * (1.0 + scale) + shift

def rope_tables(row_pos, col_pos):
    freqs = ROPE_BASE ** (-jnp.arange(0, ROPE_AXIS_DIMS, 2, dtype=f32) / ROPE_AXIS_DIMS)
    ang_r = row_pos.astype(f32)[:, None] * freqs[None, :]
    ang_c = col_pos.astype(f32)[:, None] * freqs[None, :]
    return jnp.cos(ang_r), jnp.sin(ang_r), jnp.cos(ang_c), jnp.sin(ang_c)

def rotate(x, cos, sin):
    x1, x2 = jnp.split(x, 2, axis=-1)
    cos = cos[None, :, None, :].astype(x.dtype)
    sin = sin[None, :, None, :].astype(x.dtype)
    return jnp.concatenate([x1 * cos - x2 * sin, x1 * sin + x2 * cos], axis=-1)

def apply_axial_rope(x, tables):
    cr, sr, cc, sc = tables
    xr, xc = jnp.split(x, 2, axis=-1)
    return jnp.concatenate([rotate(xr, cr, sr), rotate(xc, cc, sc)], axis=-1)

def gla_scan(q, k, v, logdecay, s0):
    B, L, H, _ = q.shape
    n = L // GLA_CHUNK

    def to_chunks(a):
        return a.reshape(B, n, GLA_CHUNK, H, a.shape[-1]).transpose(1, 0, 3, 2, 4).astype(f32)

    qc, kc, vc, gc = to_chunks(q), to_chunks(k), to_chunks(v), to_chunks(logdecay)
    causal = jnp.tril(jnp.ones((GLA_CHUNK, GLA_CHUNK), bool))

    def step(s, inp):
        qi, ki, vi, gi = inp
        b = jnp.cumsum(gi, axis=-2)
        b_last = b[..., -1:, :]
        q_e = qi * jnp.exp(b)
        att = jnp.einsum('bhik,bhjk->bhij', q_e, ki * jnp.exp(-b))
        att = jnp.where(causal, att, 0.0)
        o = jnp.einsum('bhik,bhkv->bhiv', q_e, s) + jnp.einsum('bhij,bhjv->bhiv', att, vi)
        s_new = jnp.exp(b_last[..., 0, :])[..., None] * s + jnp.einsum('bhjk,bhjv->bhkv', ki * jnp.exp(b_last - b), vi)
        return s_new, o

    s_fin, o = lax.scan(step, s0.astype(f32), (qc, kc, vc, gc))
    o = o.transpose(1, 0, 3, 2, 4).reshape(B, L, H, v.shape[-1])
    return o.astype(q.dtype), s_fin

def gla_bidir(q, k, v, ld_f, ld_b, s_f0, s_b0):
    o_f, s_f = gla_scan(q, k, v, ld_f, s_f0)
    o_b, s_b = gla_scan(q[:, ::-1], k[:, ::-1], v[:, ::-1], ld_b[:, ::-1], s_b0)
    return o_f + o_b[:, ::-1], s_f, s_b

def ctx_attn(q, k, v, sink):
    B, L = q.shape[:2]
    nb = L // ATT_BLOCK
    scale = ATT_HD ** -0.5
    qb = q.reshape(B, nb, ATT_BLOCK, ATT_KV_HEADS, ATT_GROUP, ATT_HD).transpose(1, 0, 2, 3, 4, 5)
    sink_b = sink.reshape(ATT_KV_HEADS, ATT_GROUP)[None, :, :, None, None].astype(f32)

    def block(q_blk):
        s = jnp.einsum('bqhgd,bkhd->bhgqk', q_blk, k).astype(f32) * scale
        s_sink = jnp.broadcast_to(sink_b, s.shape[:-1] + (1,))
        p = jax.nn.softmax(jnp.concatenate([s_sink, s], axis=-1), axis=-1)[..., 1:].astype(v.dtype)
        return jnp.einsum('bhgqk,bkhd->bqhgd', p, v).reshape(B, ATT_BLOCK, ATT_HEADS * ATT_HD)

    o = lax.map(block, qb)
    return o.transpose(1, 0, 2, 3).reshape(B, L, ATT_HEADS * ATT_HD)

def window_attn_latent(q, k, v, k_ctx, v_ctx, sink):
    B, S = q.shape[:2]
    nb = S // ATT_BLOCK
    Lc = k_ctx.shape[1]
    scale = ATT_HD ** -0.5
    qb = q.reshape(B, nb, ATT_BLOCK, ATT_KV_HEADS, ATT_GROUP, ATT_HD).transpose(1, 0, 2, 3, 4, 5)
    pad = ((0, 0), (ATT_BLOCK, ATT_BLOCK), (0, 0), (0, 0))
    kp = jnp.pad(k, pad)
    vp = jnp.pad(v, pad)
    sink_b = sink.reshape(ATT_KV_HEADS, ATT_GROUP)[None, :, :, None, None].astype(f32)
    offs_q = jnp.arange(ATT_BLOCK)
    offs_k = jnp.arange(3 * ATT_BLOCK) - ATT_BLOCK

    def block(args):
        bi, q_blk = args
        k_band = lax.dynamic_slice_in_dim(kp, bi * ATT_BLOCK, 3 * ATT_BLOCK, axis=1)
        v_band = lax.dynamic_slice_in_dim(vp, bi * ATT_BLOCK, 3 * ATT_BLOCK, axis=1)
        qpos = bi * ATT_BLOCK + offs_q
        kpos = bi * ATT_BLOCK + offs_k
        valid = (jnp.abs(qpos[:, None] - kpos[None, :]) <= WINDOW) & (kpos >= 0)[None, :] & (kpos < S)[None, :]
        s_lat = jnp.einsum('bqhgd,bkhd->bhgqk', q_blk, k_band).astype(f32) * scale
        s_lat = jnp.where(valid, s_lat, NEG)
        s_ctx = jnp.einsum('bqhgd,bchd->bhgqc', q_blk, k_ctx).astype(f32) * scale
        s_sink = jnp.broadcast_to(sink_b, s_ctx.shape[:-1] + (1,))
        p = jax.nn.softmax(jnp.concatenate([s_sink, s_ctx, s_lat], axis=-1), axis=-1).astype(v.dtype)
        o = (jnp.einsum('bhgqc,bchd->bqhgd', p[..., 1:1 + Lc], v_ctx)
             + jnp.einsum('bhgqk,bkhd->bqhgd', p[..., 1 + Lc:], v_band))
        return o.reshape(B, ATT_BLOCK, ATT_HEADS * ATT_HD)

    o = lax.map(block, (jnp.arange(nb), qb))
    return o.transpose(1, 0, 2, 3).reshape(B, S, ATT_HEADS * ATT_HD)

def even_projections(h, w_in, dec_w, dec_b):
    B, L, _ = h.shape
    gq, gk, gv, gg, aq, ak, av, lr = jnp.split(h @ w_in, IN_SPLITS, axis=-1)
    gq = gq.reshape(B, L, GLA_HEADS, GLA_DK) * (GLA_DK ** -0.5)
    gk = gk.reshape(B, L, GLA_HEADS, GLA_DK)
    gv = gv.reshape(B, L, GLA_HEADS, GLA_DV)
    lr_f, lr_b = jnp.split(lr, 2, axis=-1)

    def logdecay(lr_d, w, b):
        return (jax.nn.log_sigmoid((lr_d @ w + b).astype(f32)) / GLA_GATE_TEMP).reshape(B, L, GLA_HEADS, GLA_DK)

    ld_f = logdecay(lr_f, dec_w[0], dec_b[0])
    ld_b = logdecay(lr_b, dec_w[1], dec_b[1])
    aq = aq.reshape(B, L, ATT_HEADS, ATT_HD)
    ak = ak.reshape(B, L, ATT_KV_HEADS, ATT_HD)
    av = av.reshape(B, L, ATT_KV_HEADS, ATT_HD)
    return gq, gk, gv, gg, ld_f, ld_b, aq, ak, av

def even_output(o_gla, gg, o_att, gla_norm, w_out):
    B, L = o_gla.shape[:2]
    o_gla = rmsnorm(o_gla, gla_norm).reshape(B, L, GLA_HEADS * GLA_DV) * jax.nn.silu(gg)
    return jnp.concatenate([o_gla, o_att.astype(o_gla.dtype)], axis=-1) @ w_out

def even_mixer_ctx(h, w_in, w_out, dec_w, dec_b, gla_norm, sink):
    gq, gk, gv, gg, ld_f, ld_b, aq, ak, av = even_projections(h, w_in, dec_w, dec_b)
    zero = jnp.zeros((h.shape[0], GLA_HEADS, GLA_DK, GLA_DV), f32)
    o_gla, s_f, s_b = gla_bidir(gq, gk, gv, ld_f, ld_b, zero, zero)
    o_att = ctx_attn(aq, ak, av, sink)
    return even_output(o_gla, gg, o_att, gla_norm, w_out), ak, av, s_f, s_b

def even_mixer_lat(h, w_in, w_out, dec_w, dec_b, gla_norm, sink, rope, k_ctx, v_ctx, s_f0, s_b0):
    gq, gk, gv, gg, ld_f, ld_b, aq, ak, av = even_projections(h, w_in, dec_w, dec_b)
    o_gla, _, _ = gla_bidir(gq, gk, gv, ld_f, ld_b, s_f0, s_b0)
    o_att = window_attn_latent(apply_axial_rope(aq, rope), apply_axial_rope(ak, rope), av,
                               k_ctx.astype(aq.dtype), v_ctx.astype(av.dtype), sink)
    return even_output(o_gla, gg, o_att, gla_norm, w_out)

def centred_shift(x):
    xp = jnp.pad(x, ((0, 0), (1, 1), (0, 0)))
    return 0.5 * (xp[:, :-2] + xp[:, 2:])

def rwkv_scan(r, w, k, v, kk, a, s0):
    def step(s, inp):
        r_t, w_t, k_t, v_t, kk_t, a_t = inp
        sa = jnp.einsum('bhvk,bhk->bhv', s, -kk_t)
        s = s * w_t[:, :, None, :] + sa[..., None] * (kk_t * a_t)[:, :, None, :] + v_t[..., None] * k_t[:, :, None, :]
        return s, jnp.einsum('bhvk,bhk->bhv', s, r_t)

    xs = tuple(t.transpose(1, 0, 2, 3) for t in (r, w, k, v, kk, a))
    s_fin, out = lax.scan(step, s0.astype(f32), xs)
    return out.transpose(1, 0, 2, 3), s_fin

def rwkv_mix(h, mu, wr, wk, wv, wo, w0, w1, w2, a0, a1, a2, g1, g2, k_k, k_a, r_k, lnx_w, lnx_b, s_f0, s_b0):
    B, L, D = h.shape
    H, N = RWKV_HEADS, RWKV_HEAD
    xx = centred_shift(h) - h
    xr, xw, xk, xv, xa, xg = [h + xx * mu[j] for j in range(6)]
    r = (xr @ wr).reshape(B, L, H, N).astype(f32)
    k = (xk @ wk).reshape(B, L, H, N).astype(f32)
    v = (xv @ wv).reshape(B, L, H, N).astype(f32)
    g = jax.nn.sigmoid(xg @ g1) @ g2
    kk = k * k_k.reshape(H, N).astype(f32)
    kk = kk * lax.rsqrt(jnp.sum(kk * kk, axis=-1, keepdims=True) + 1e-12)

    def direction(d, flip, s0):
        w_raw = -jax.nn.softplus(-(w0[d] + jnp.tanh(xw @ w1[d]) @ w2[d]).astype(f32)) - 0.5
        decay = jnp.exp(-jnp.exp(w_raw)).reshape(B, L, H, N)
        a = jax.nn.sigmoid((a0[d] + (xa @ a1[d]) @ a2[d]).astype(f32)).reshape(B, L, H, N)
        k_d = k * (1.0 + (a - 1.0) * k_a.reshape(H, N).astype(f32))
        seqs = (r, decay, k_d, v, kk, a)
        if flip:
            seqs = tuple(t[:, ::-1] for t in seqs)
        o, s = rwkv_scan(*seqs, s0)
        if flip:
            o = o[:, ::-1]
        return o, s, k_d

    o_f, s_f, k_f = direction(0, False, s_f0)
    o_b, s_b, k_b = direction(1, True, s_b0)
    o = o_f + o_b
    m = jnp.mean(o, axis=-1, keepdims=True)
    var = jnp.mean(jnp.square(o - m), axis=-1, keepdims=True)
    o = (o - m) * lax.rsqrt(var + RWKV_LN_EPS) * lnx_w.reshape(H, N).astype(f32) + lnx_b.reshape(H, N).astype(f32)
    bonus = jnp.sum(r * 0.5 * (k_f + k_b) * r_k.astype(f32), axis=-1, keepdims=True) * v
    o = (o + bonus).reshape(B, L, D).astype(h.dtype)
    return (o * g) @ wo, s_f, s_b

def hier_moe(h, w_grp, b_grp, w_exp, b_exp, w_gate, w_up, w_down):
    B, L, D = h.shape
    t = h.reshape(-1, D)
    grp_logits = (t @ w_grp + b_grp).astype(f32)
    grp_prob = jax.nn.softmax(grp_logits, axis=-1)
    g_top = jnp.argmax(grp_logits, axis=-1)
    p_g = jnp.take_along_axis(grp_prob, g_top[:, None], axis=1)
    exp_logits = (t @ w_exp + b_exp).astype(f32).reshape(-1, N_GROUPS, EXP_PER_GROUP)
    sel = jnp.take_along_axis(exp_logits, g_top[:, None, None], axis=1)[:, 0]
    top_v, top_i = lax.top_k(sel, TOP_K)
    wts = p_g * jax.nn.softmax(top_v, axis=-1)
    idx = g_top[:, None] * EXP_PER_GROUP + top_i
    gates = jnp.sum(jax.nn.one_hot(idx, N_EXPERTS, dtype=f32) * wts[..., None], axis=1)
    hid = jax.nn.silu(jnp.einsum('td,edf->tef', t, w_gate)) * jnp.einsum('td,edf->tef', t, w_up)
    hid = hid * gates[..., None].astype(hid.dtype)
    return jnp.einsum('tef,efd->td', hid, w_down).reshape(B, L, D)

def setup_inputs(seed: int = 0) -> dict:
    key = jax.random.key(seed)
    ks = iter(jax.random.split(key, 64))
    D = D_MODEL

    def nrm(shape, scale=1.0):
        return jax.random.normal(next(ks), shape, f32) * scale

    def gain(shape):
        return 1.0 + nrm(shape, 0.05)

    return {
        "x_prompt": nrm((BATCH, SEQ, D)),
        "x_sample": nrm((DEC_BATCH, DEC_SEQ, D)),
        "c": nrm((DEC_BATCH, D)),
        "cache_attn_k": nrm((DEC_BATCH, N_EVEN, PAST_LEN, ATT_KV_HEADS, ATT_HD)),
        "cache_attn_v": nrm((DEC_BATCH, N_EVEN, PAST_LEN, ATT_KV_HEADS, ATT_HD)),
        "state_gla": nrm((DEC_BATCH, N_EVEN, 2, GLA_HEADS, GLA_DK, GLA_DV), 0.5),
        "state_rwkv": nrm((DEC_BATCH, N_ODD, 2, RWKV_HEADS, RWKV_HEAD, RWKV_HEAD), 0.3),
        "c_ctx": nrm((D,)),
        "ada_w": nrm((DEPTH, D, 6 * D), 0.5 * D ** -0.5),
        "ada_b": nrm((DEPTH, 6 * D), 0.02),
        "norm_mix": gain((DEPTH, D)),
        "norm_ffn": gain((DEPTH, D)),
        "norm_out": gain((D,)),
        "ev_w_in": nrm((N_EVEN, D, IN_WIDTH), D ** -0.5),
        "ev_w_out": nrm((N_EVEN, MIX_WIDTH, D), MIX_WIDTH ** -0.5),
        "gla_dec_w": nrm((N_EVEN, 2, GLA_LOWRANK, GLA_HEADS * GLA_DK), GLA_LOWRANK ** -0.5),
        "gla_dec_b": nrm((N_EVEN, 2, GLA_HEADS * GLA_DK), 0.5),
        "gla_norm": gain((N_EVEN, GLA_DV)),
        "att_sink": nrm((N_EVEN, ATT_HEADS), 0.5),
        "rw_mu": jax.random.uniform(next(ks), (N_ODD, 6, D), f32),
        "rw_wr": nrm((N_ODD, D, D), D ** -0.5),
        "rw_wk": nrm((N_ODD, D, D), D ** -0.5),
        "rw_wv": nrm((N_ODD, D, D), D ** -0.5),
        "rw_wo": nrm((N_ODD, D, D), D ** -0.5),
        "rw_w0": -1.0 + nrm((N_ODD, 2, D), 0.5),
        "rw_w1": nrm((N_ODD, 2, D, W_LORA), D ** -0.5),
        "rw_w2": nrm((N_ODD, 2, W_LORA, D), 0.5 * W_LORA ** -0.5),
        "rw_a0": nrm((N_ODD, 2, D), 0.5),
        "rw_a1": nrm((N_ODD, 2, D, A_LORA), D ** -0.5),
        "rw_a2": nrm((N_ODD, 2, A_LORA, D), 0.5 * A_LORA ** -0.5),
        "rw_g1": nrm((N_ODD, D, G_LORA), D ** -0.5),
        "rw_g2": nrm((N_ODD, G_LORA, D), G_LORA ** -0.5),
        "rw_kk": 0.85 + nrm((N_ODD, D), 0.05),
        "rw_ka": 1.0 + nrm((N_ODD, D), 0.05),
        "rw_rk": nrm((N_ODD, RWKV_HEADS, RWKV_HEAD), 0.1),
        "rw_lnx_w": gain((N_ODD, D)),
        "rw_lnx_b": nrm((N_ODD, D), 0.02),
        "moe_w_grp": nrm((DEPTH, D, N_GROUPS), D ** -0.5),
        "moe_b_grp": nrm((DEPTH, N_GROUPS), 0.01),
        "moe_w_exp": nrm((DEPTH, D, N_EXPERTS), D ** -0.5),
        "moe_b_exp": nrm((DEPTH, N_EXPERTS), 0.01),
        "moe_w_gate": nrm((DEPTH, N_EXPERTS, D, D_EXPERT), D ** -0.5),
        "moe_w_up": nrm((DEPTH, N_EXPERTS, D, D_EXPERT), D ** -0.5),
        "moe_w_down": nrm((DEPTH, N_EXPERTS, D_EXPERT, D), D_EXPERT ** -0.5),
    }

def reference(x_prompt, x_sample, c, cache_attn_k, cache_attn_v, state_gla, state_rwkv, c_ctx,
              ada_w, ada_b, norm_mix, norm_ffn, norm_out, ev_w_in, ev_w_out, gla_dec_w, gla_dec_b, gla_norm,
              att_sink, rw_mu, rw_wr, rw_wk, rw_wv, rw_wo, rw_w0, rw_w1, rw_w2, rw_a0, rw_a1, rw_a2, rw_g1, rw_g2,
              rw_kk, rw_ka, rw_rk, rw_lnx_w, rw_lnx_b, moe_w_grp, moe_b_grp, moe_w_exp, moe_b_exp,
              moe_w_gate, moe_w_up, moe_w_down):
    n_lat = x_sample.shape[1]
    rows = n_lat // GRID_W
    row_pos = jnp.repeat(jnp.arange(rows), GRID_W)
    col_pos = jnp.tile(jnp.arange(GRID_W), rows)
    rope = rope_tables(row_pos, col_pos)

    xc, xl = x_prompt, x_sample
    cond_ctx = c_ctx[None, :]
    ks_out, vs_out, gla_out, rwkv_out = [], [], [], []
    for l in range(DEPTH):
        sc1, scl1, gc1, sc2, scl2, gc2 = ada_mod(cond_ctx, ada_w[l], ada_b[l])
        sl1, sll1, gl1, sl2, sll2, gl2 = ada_mod(c, ada_w[l], ada_b[l])
        hc = modulate(rmsnorm(xc, norm_mix[l]), sc1, scl1)
        hl = modulate(rmsnorm(xl, norm_mix[l]), sl1, sll1)
        i = l // 2
        if l % 2 == 0:
            oc, k_c, v_c, s_f, s_b = even_mixer_ctx(hc, ev_w_in[i], ev_w_out[i], gla_dec_w[i], gla_dec_b[i],
                                                    gla_norm[i], att_sink[i])
            ol = even_mixer_lat(hl, ev_w_in[i], ev_w_out[i], gla_dec_w[i], gla_dec_b[i], gla_norm[i], att_sink[i],
                                rope, cache_attn_k[:, i], cache_attn_v[:, i], state_gla[:, i, 0], state_gla[:, i, 1])
            ks_out.append(k_c)
            vs_out.append(v_c)
            gla_out.append(jnp.stack([s_f, s_b], axis=1))
        else:
            rw = (rw_mu[i], rw_wr[i], rw_wk[i], rw_wv[i], rw_wo[i], rw_w0[i], rw_w1[i], rw_w2[i], rw_a0[i],
                  rw_a1[i], rw_a2[i], rw_g1[i], rw_g2[i], rw_kk[i], rw_ka[i], rw_rk[i], rw_lnx_w[i], rw_lnx_b[i])
            zero = jnp.zeros((xc.shape[0], RWKV_HEADS, RWKV_HEAD, RWKV_HEAD), f32)
            oc, s_f, s_b = rwkv_mix(hc, *rw, zero, zero)
            ol, _, _ = rwkv_mix(hl, *rw, state_rwkv[:, i, 0], state_rwkv[:, i, 1])
            rwkv_out.append(jnp.stack([s_f, s_b], axis=1))
        xc = xc + gc1 * oc
        xl = xl + gl1 * ol
        moe = (moe_w_grp[l], moe_b_grp[l], moe_w_exp[l], moe_b_exp[l], moe_w_gate[l], moe_w_up[l], moe_w_down[l])
        xc = xc + gc2 * hier_moe(modulate(rmsnorm(xc, norm_ffn[l]), sc2, scl2), *moe)
        xl = xl + gl2 * hier_moe(modulate(rmsnorm(xl, norm_ffn[l]), sl2, sll2), *moe)

    y_prompt = rmsnorm(xc, norm_out)
    y_sample = rmsnorm(xl, norm_out)
    new_attn_k = jnp.stack(ks_out, axis=1)
    new_attn_v = jnp.stack(vs_out, axis=1)
    new_gla = jnp.stack(gla_out, axis=1)
    new_rwkv = jnp.stack(rwkv_out, axis=1)
    return (y_prompt, y_sample, new_attn_k, new_attn_v, new_gla, new_rwkv)


_drawn_inputs = setup_inputs


def setup_inputs(seed=0):
    import zlib

    import numpy as np

    out = dict(_drawn_inputs(seed))
    spreads = {}
    factors = {'cache_attn_k': 3.119,
     'cache_attn_v': 2.917,
     'state_gla': 8.0,
     'state_rwkv': 6.185,
     'gla_norm': 5.076,
     'att_sink': 23.476,
     'rw_lnx_w': 7.11,
     'rw_lnx_b': 29.63,
     'moe_b_grp': 16.535,
     'moe_b_exp': 31.257,
     'norm_ffn': 2.84,
     'rw_rk': 2.768}
    for name, (base, spread) in spreads.items():
        noise = np.random.default_rng([zlib.crc32(name.encode()), seed]).standard_normal(out[name].shape)
        drawn = base * np.exp(spread * noise) if base else spread * noise
        out[name] = __import__('jax').numpy.asarray(drawn.astype(out[name].dtype))
    for name, factor in factors.items():
        out[name] = (out[name] * factor).astype(out[name].dtype)
    return out
```

```python
from contextlib import ExitStack

import numpy as np

import concourse.bass as bass
from concourse import mybir

F32 = mybir.dt.float32
I32 = mybir.dt.int32
ALU = mybir.AluOpType
ACT = mybir.ActivationFunctionType
AX = mybir.AxisListType.X

P = 128
D = 1024
KC = D // P
CTX, LAT = 128, 256
T = CTX + LAT
STREAMS = ((0, 0, CTX), (1, CTX, T))
TILE = 2048
RING = 6
MC = 6 * KC
HD = 64
CH = 64
NCH = T // CH
GH, GV = 4, 128
AH, AKV = 8, 2
LR = 16
IN_W = 2336
NE, NG, EPG, FE = 16, 4, 4, 512
CAP = 96
EPS = 1e-6
LN_EPS = 64e-5
HALF_DECAY = float(np.exp(-0.5))

N_ADA = 2 * MC // 2
N_IN = 10
N_OUT = 4
N_MOE = NE * 6
AT_ADA = 0
AT_IN = AT_ADA + N_ADA
AT_OUT = AT_IN + N_IN
AT_MOE0 = AT_OUT + N_OUT
AT_RKV = AT_MOE0 + N_MOE
AT_LORA = AT_RKV + 12
AT_GATE = AT_LORA + 1
AT_WO = AT_GATE + 1
AT_MOE1 = AT_WO + 4
N_TILES = AT_MOE1 + N_MOE

V_COND = 0
V_ADA_B = V_COND + 2 * KC
V_NMIX = V_ADA_B + 2 * MC
V_NFFN = V_NMIX + 2 * KC
V_NOUT = V_NFFN + 2 * KC
V_MU = V_NOUT + KC
V_PAIR = V_MU + 6 * KC
PAIR_VECS = 9
V_GNORM = V_PAIR + PAIR_VECS * KC
V_DECB = V_GNORM + 1
V_EPS = V_DECB + 4
V_LNEPS = V_EPS + 1
V_N = V_LNEPS + 1

LEVELS = (1, 2, 4, 8, 16, 32)
C_ID = 0
C_ONES = C_ID + P
C_HEADS = C_ONES + P
C_INCL = C_HEADS + P
C_STRICT = C_INCL + 2 * CH
C_LEV = C_STRICT + 2 * CH
C_LEV1T = C_LEV + len(LEVELS) * 2 * CH
C_I64 = C_LEV1T + 2 * CH
C_KEEP = C_I64 + CH
C_MASK = C_KEEP + T
C_COS = C_MASK + 2 * T
C_SIN = C_COS + LAT
C_PERM = C_SIN + LAT
C_N = C_PERM + HD


def constants():
    c = np.zeros((P, C_N), np.float32)
    c[:, C_ID:C_ID + P] = np.eye(P)
    c[:, C_ONES:C_ONES + P] = 1.0
    c[:64, C_HEADS:C_HEADS + 64] = 1.0
    c[64:, C_HEADS + 64:C_HEADS + 128] = 1.0
    p = np.arange(CH)[:, None]
    f = np.arange(CH)[None, :]

    def put(at, m):
        c[:64, at:at + CH] = m
        c[64:, at:at + CH] = m

    put(C_INCL, p <= f)
    put(C_INCL + CH, p >= f)
    put(C_STRICT, p < f)
    put(C_STRICT + CH, p > f)
    for n, s in enumerate(LEVELS):
        lower = (p // (2 * s) == f // (2 * s)) & (p % (2 * s) >= s) & (f % (2 * s) < s)
        put(C_LEV + 2 * n * CH, lower)
        put(C_LEV + (2 * n + 1) * CH, lower.T)
        if s == 1:
            put(C_LEV1T, lower.T)
            put(C_LEV1T + CH, lower)
    put(C_I64, p == f)
    c[:, C_KEEP:C_KEEP + T] = np.arange(T) % CH != 0
    for b in range(2):
        q = b * P + np.arange(P)[:, None]
        k = np.arange(LAT)[None, :]
        c[:, C_MASK + b * T + CTX:C_MASK + (b + 1) * T] = np.where(np.abs(q - k) <= 128, 0.0, -1e30)
    freqs = (np.float32(10000.0) ** (-np.arange(0, 32, 2, dtype=np.float32) / np.float32(32))).astype(np.float32)
    t = np.arange(LAT)
    row = (t // 64).astype(np.float32)[None, :] * freqs[:, None]
    col = (t % 64).astype(np.float32)[None, :] * freqs[:, None]
    ang = np.concatenate([row, row, col, col], 0)
    put_at = slice(0, HD)
    c[put_at, C_COS:C_COS + LAT] = np.cos(ang)
    c[put_at, C_SIN:C_SIN + LAT] = np.sin(ang)
    perm = np.zeros((HD, HD), np.float32)
    for half in (0, 32):
        for i in range(16):
            perm[half + 16 + i, half + i] = -1.0
            perm[half + i, half + 16 + i] = 1.0
    c[:HD, C_PERM:C_PERM + HD] = perm
    return c


def router_constants():
    c = np.zeros((P, CAP + P), np.float32)
    c[:, :CAP] = np.arange(CAP)
    c[:, CAP:] = np.arange(P)[:, None] < np.arange(P)[None, :]
    return c


class Order:

    def __init__(self, eng, sem):
        self.eng, self.sem, self.n, self.at = eng, sem, 0, 0

    def __call__(self, ins):
        self.inc(ins)
        self.wait()

    def inc(self, ins):
        ins.then_inc(self.sem, 1)
        self.n += 1

    def wait(self):
        self.eng.wait_ge(self.sem, self.at + self.n)

    def enter(self, i, per):
        self.start, self.per = self.n, per
        self.at = i * per

    def leave(self, turns):
        assert self.n - self.start == self.per, self.n - self.start
        self.n = self.start + self.per * turns
        self.at = 0


def build(nc, xT, cst, rcst, vec, sinkr, ckT, cv, zgla, zrwkv, wrt, brt, dec2, wa2, wstream,
          yT, kT_out, vT_out, gla_out, rwkv_out):
    ctx = ExitStack()

    def sb(name, words):
        return ctx.enter_context(nc.sbuf_tensor(name, [P, words], F32))

    def sem(name):
        return ctx.enter_context(nc.semaphore(name))

    with ctx:
        ring = sb("ring", RING * TILE)
        XT_ = sb("XT", KC * T)
        HT_ = sb("HT", KC * T)
        C = sb("consts", C_N)
        V = sb("vecs", V_N)
        MOD = sb("mod", 2 * MC * 2)
        GAIN = sb("gain", 2 * 2 * KC * 2)
        SINK = sb("sink", AH)
        A = sb("arena", 30880)
        ps = ctx.enter_context(nc.psum_tensor("ps", [P, 8 * 512], F32))

        XT = XT_[:, :].rearrange("p (k t) -> p k t", k=KC)
        HT = HT_[:, :].rearrange("p (k t) -> p k t", k=KC)
        mod = MOD[:, :].rearrange("p (l a k c) -> p l a k c", l=2, a=6, k=KC)
        gain = GAIN[:, :].rearrange("p (l w k c) -> p l w k c", l=2, w=2, k=KC)
        ident = C[:, C_ID:C_ID + P]
        ones = C[:, C_ONES:C_ONES + P]
        heads = C[:, C_HEADS:C_HEADS + P]

        def bank(b, cols=T, at=0):
            return ps[:, b * 512 + at:b * 512 + at + cols]

        def area(at, words, **dims):
            v = A[:, at:at + words]
            if not dims:
                return v
            names = " ".join(dims)
            return v.rearrange(f"p ({names}) -> p {names}", **dims)

        w_in = [sem(f"weight_tile_in_slot{i}") for i in range(RING)]
        w_used = sem("weight_tiles_used")
        out_sem = sem("outputs_written")
        n_out = [0]

        issued = [0]

        def stream(sp, end):
            n = issued[0]
            while n < end:
                if n >= RING and n + RING <= end:
                    turns = (end - n) // RING
                    with sp.Fori(0, turns) as i:
                        for j in range(RING):
                            m = n + j
                            sp.wait_ge(w_used, i * RING + (m - RING + 1))
                            sp.dma_start(ring[:, m % RING * TILE:(m % RING + 1) * TILE],
                                         wstream[bass.ds(i * RING + m, 1)].rearrange("a p n -> (a p) n")
                                         ).then_inc(w_in[m % RING], 16)
                    n += turns * RING
                    continue
                if n >= RING:
                    sp.wait_ge(w_used, n - RING + 1)
                sp.dma_start(ring[:, n % RING * TILE:(n % RING + 1) * TILE], wstream[n]).then_inc(w_in[n % RING], 16)
                n += 1
            issued[0] = n

        def tile_in(pe, n, i=0):
            pe.wait_ge(w_in[n % RING], i * 16 + 16 * (n // RING + 1))

        def tile(n, **dims):
            names = " ".join(dims)
            return ring[:, n % RING * TILE:(n % RING + 1) * TILE].rearrange(f"p ({names}) -> p {names}", **dims)

        def linear(pe, at, chunks, rhs, ready, freed, rhs_wait=None, last_of=2, first=0):
            if rhs_wait is not None:
                pe.wait_ge(*rhs_wait)
            for m in chunks:
                n = at + m // 2
                if m % 2 == 0:
                    tile_in(pe, n)
                if m - first >= 8:
                    pe.wait_ge(freed, m - 7)
                w = tile(n, k=KC, c=256)
                for k in range(KC):
                    mm = pe.matmul(bank(m % 8), w[:, k, m % 2 * P:m % 2 * P + P], rhs[:, k, :],
                                   start=k == 0, stop=k == KC - 1)
                mm.then_inc(ready, 1)
                if m % 2 == 1:
                    pe.wait_ge(ready, m + 1)
                    pe.sem_inc(w_used, 1)

        s_small, s_state = sem("small_inputs_in"), sem("x_in")
        s_cond, s_ada, s_ada_ev = sem("cond_silu_ready"), sem("ada_products_ready"), sem("ada_chunks_stored")
        s_dve, s_act, s_pool = sem("dve_order"), sem("act_order"), sem("pool_order")
        dve_o, act_o = Order(nc.vector, s_dve), Order(nc.scalar, s_act)
        SC = area(0, 2 * KC, k=KC, c=2)
        PER_ADA = 2 * RING
        with nc.Block() as block:
            @block.sync
            def _(sp):
                stream(sp, AT_IN + RING)

            @block.scalar
            def _(act):
                act.dma_start(V[:, :], vec).then_inc(s_small, 16)
                act.dma_start(C[:, :], cst).then_inc(s_small, 16)
                act.dma_start(SINK[:, :], sinkr.partition_broadcast(P)).then_inc(s_small, 16)
                act.dma_start(XT_[:, :], xT).then_inc(s_state, 16)
                act.wait_ge(s_small, 48)
                act.activation(SC, V[:, V_COND:V_COND + 2 * KC].rearrange("p (k c) -> p k c", c=2),
                               ACT.Silu).then_inc(s_cond, 1)
                act.wait_ge(s_state, 16)

            @block.tensor
            def _(pe):
                pe.wait_ge(s_cond, 1)
                with pe.Fori(0, N_ADA // RING) as i:
                    pe.wait_ge(s_ada_ev, i + 1)
                    for j in range(RING):
                        tile_in(pe, j, i)
                        w = tile(j, k=KC, c=256)
                        for m in range(2):
                            o = bank(0, 2, 2 * (2 * j + m))
                            for k in range(KC):
                                mm = pe.matmul(o, w[:, k, m * P:m * P + P], SC[:, k, :],
                                               start=k == 0, stop=k == KC - 1)
                        mm.then_inc(w_used, 1)
                    pe.wait_ge(w_used, (i + 1) * RING)
                    pe.sem_inc(s_ada, 1)

            @block.vector
            def _(dve):
                dve.wait_ge(s_small, 48)
                dve.sem_inc(s_ada_ev, 1)
                with dve.Fori(0, N_ADA // RING) as i:
                    dve.wait_ge(s_ada, i + 1)
                    dst = MOD[:, bass.ds(i * (2 * PER_ADA), 2 * PER_ADA)].rearrange("p (m c) -> p m c", c=2)
                    b = V[:, bass.ds(i * PER_ADA + V_ADA_B, PER_ADA)].unsqueeze(2).broadcast_to([P, PER_ADA, 2])
                    dve.tensor_tensor(dst, bank(0, 2 * PER_ADA).rearrange("p (m c) -> p m c", c=2), b,
                                      ALU.add).then_inc(s_ada_ev, 1)
                dve.wait_ge(s_ada_ev, N_ADA // RING + 1)
                for l in range(2):
                    for w, vn in ((0, V_NMIX), (1, V_NFFN)):
                        nw = V[:, vn + l * KC:vn + (l + 1) * KC].unsqueeze(2).broadcast_to([P, KC, 2])
                        last = dve.scalar_tensor_tensor(out=gain[:, l, w], in0=mod[:, l, 3 * w + 1], scalar=1.0,
                                                        in1=nw, op0=ALU.add, op1=ALU.mult)
                        dve_o(last)

        s_sq, s_ss, s_var, s_sd, s_rs, s_xn = (sem("squares_ready"), sem("square_sums_ready"), sem("variance_ready"),
                                               sem("std_ready"), sem("rstd_ready"), sem("normalised_ready"))
        norms = [0]

        def norm_block(l, w, end, save=None):
            n = norms[0]
            norms[0] += 1
            RS, VAR = area(0, T), area(T, T)
            with nc.Block() as block:
                @block.sync
                def _(sp):
                    stream(sp, end)

                @block.scalar
                def _(act):
                    act.activation(HT_[:, :], XT_[:, :], ACT.Square).then_inc(s_sq, 1)
                    act.wait_ge(s_var, n + 1)
                    act.activation(VAR, VAR, ACT.Sqrt).then_inc(s_sd, 1)
                    for k in range(KC):
                        act.wait_ge(s_xn, n * KC + k + 1)
                        if l is None:
                            act_o(act.activation(HT[:, k, :], HT[:, k, :], ACT.Copy,
                                                 scale=V[:, V_NOUT + k:V_NOUT + k + 1]))
                            continue
                        for c, a, b in STREAMS:
                            act_o.inc(act.activation(HT[:, k, a:b], HT[:, k, a:b], ACT.Identity,
                                                     bias=mod[:, l, 3 * w, k, c:c + 1],
                                                     scale=gain[:, l, w, k, c:c + 1]))
                    act_o.wait()
                    if l is None:
                        act.dma_start(yT, HT_[:, :]).then_inc(out_sem, 16)
                        n_out[0] += 16
                        act.wait_ge(out_sem, n_out[0])

                @block.tensor
                def _(pe):
                    pe.wait_ge(s_sq, n + 1)
                    for k in range(KC):
                        mm = pe.matmul(bank(0), ones, HT[:, k, :], start=k == 0, stop=k == KC - 1)
                    mm.then_inc(s_ss, 1)

                @block.vector
                def _(dve):
                    dve.wait_ge(s_ss, n + 1)
                    dve.tensor_scalar(VAR, bank(0), 1.0 / D, EPS, ALU.mult, ALU.add).then_inc(s_var, 1)
                    dve.wait_ge(s_sd, n + 1)
                    dve_o(dve.reciprocal(RS, VAR))
                    for k in range(KC):
                        dve.tensor_tensor(HT[:, k, :], XT[:, k, :], RS, ALU.mult).then_inc(s_xn, 1)

        norm_block(0, 0, AT_IN + RING)

        a_ = [0]

        def take(words):
            a_[0] += words
            return a_[0] - words

        QG = area(take(2 * T), 2 * T, c=2, t=T)
        KG = area(take(2 * T), 2 * T, c=2, t=T)
        GVT = area(take(4 * T), 4 * T, h=4, t=T)
        SG = area(take(4 * T), 4 * T, h=4, t=T)
        at_aq = take(8 * T)
        AQK = area(at_aq, 8 * T, h=8, t=T)
        AK = area(take(2 * T), 2 * T, h=2, t=T)
        AVT = area(take(T), T)
        LRT = area(take(T), T)
        VR = area(take(T), T, a=3, d=P)
        GVR = area(take(2 * NCH * GV), 2 * NCH * GV, r=2, n=NCH, v=GV)
        LD = area(take(4 * T), 4 * T, r=2, d=2, t=T)
        CK = area(take(2 * P), 2 * P, h=2, t=P)
        CV = area(take(P), P, h=2, e=HD)
        DEC = area(take(4 * P), 4 * P)
        at_tmp = a_[0]
        OT = HT
        s_in, s_in_ev, s_side = sem("projection_ready"), sem("projection_stored"), sem("side_inputs_in")
        with nc.Block() as block:
            @block.sync
            def _(sp):
                sp.dma_start(CK[0:HD], ckT).then_inc(s_side, 16)
                sp.dma_start(CV, cv).then_inc(s_side, 16)
                sp.dma_start(DEC[0:2 * LR, :], dec2).then_inc(s_side, 16)
                stream(sp, AT_OUT + N_OUT)
                sp.wait_ge(s_side, 48)

            @block.tensor
            def _(pe):
                linear(pe, AT_IN, range(18), HT, s_in, s_in_ev)
                tile_in(pe, AT_IN + 9)
                pe.wait_ge(s_in_ev, 11)
                w = tile(AT_IN + 9, k=KC, c=256)
                for k in range(KC):
                    mm = pe.matmul(bank(2)[0:2 * LR, :], w[:, k, 0:2 * LR], HT[:, k, :], start=k == 0, stop=k == KC - 1)
                mm.then_inc(s_in, 1)
                pe.wait_ge(s_in, 19)
                pe.sem_inc(w_used, 1)

            @block.scalar
            def _(act):
                for m in range(19):
                    act.wait_ge(s_in, m + 1)
                    o = bank(m % 8)
                    if m < 2:
                        last = act.activation(QG[:, m, :], o, ACT.Copy, scale=HD ** -0.5)
                    elif m < 4:
                        last = act.activation(KG[:, m - 2, :], o, ACT.Copy)
                    elif m < 8:
                        last = act.activation(GVT[:, m - 4, :], o, ACT.Copy)
                    elif m < 12:
                        last = act.activation(SG[:, m - 8, :], o, ACT.Silu)
                    elif m < 16:
                        h = 2 * (m - 12)
                        act.activation(AQK[0:HD, h, :], o[0:HD], ACT.Copy, scale=HD ** -0.5)
                        last = act.activation(AQK[0:HD, h + 1, :], o[HD:P], ACT.Copy, scale=HD ** -0.5)
                    elif m == 16:
                        act.activation(AK[0:HD, 0, :], o[0:HD], ACT.Copy)
                        last = act.activation(AK[0:HD, 1, :], o[HD:P], ACT.Copy)
                    elif m == 17:
                        last = act.activation(AVT, o, ACT.Copy)
                    else:
                        last = act.activation(LRT[0:2 * LR, :], o[0:2 * LR], ACT.Copy)
                    last.then_inc(s_in_ev, 1)

        ROT = area(at_tmp, 10 * LAT, h=10, t=LAT)
        Z_ = area(at_tmp + 10 * LAT, 4 * T, r=2, d=2, t=T)
        E_ = area(at_tmp + 10 * LAT + 4 * T, 4 * T, r=2, d=2, t=T)
        assert at_tmp + 10 * LAT + 8 * T <= 30880
        s_rows, s_ldp, s_rope, s_free = sem("value_rows_ready"), sem("decay_products_ready"), sem("rotated_ready"), sem("rope_banks_read")
        s_z, s_l = sem("decay_argument_ready"), sem("decay_log_ready")
        with nc.Block() as block:
            @block.scalar
            def _(act):
                act.dma_start(kT_out, AK[0:HD, :, 0:CTX]).then_inc(out_sem, 16)
                act.dma_start(vT_out, AVT[:, 0:CTX]).then_inc(out_sem, 16)
                n_out[0] += 32
                for r in range(2):
                    act.wait_ge(s_rows, r + 1)
                    act_o.inc(act.activation(GVR[:, r], ps[:, 1024 * r:1024 * r + NCH * GV].rearrange(
                        "p (n v) -> p n v", v=GV), ACT.Copy))
                act.wait_ge(s_rows, 3)
                act_o(act.activation(VR, bank(4).rearrange("p (a d) -> p a d", d=P), ACT.Copy))
                act.sem_inc(s_free, 1)
                for r in range(2):
                    for d in range(2):
                        u = 2 * r + d
                        act.wait_ge(s_ldp, u + 1)
                        o = bank(5 + u) if u < 3 else bank(4)
                        act_o.inc(act.activation(Z_[:, r, d, :], o, ACT.Identity,
                                                 bias=V[:, V_DECB + u:V_DECB + u + 1]))
                        if u == 0:
                            act_o.wait()
                            act.sem_inc(s_free, 1)
                act_o.wait()
                act.sem_inc(s_z, 1)
                zf, ef = Z_.rearrange("p r d t -> p (r d t)"), E_.rearrange("p r d t -> p (r d t)")
                act_o(act.activation(ef, zf, ACT.Abs))
                act_o(act.activation(ef, ef, ACT.Exp, scale=-1.0))
                act.activation(ef, ef, ACT.Ln, bias=1.0).then_inc(s_l, 1)

            @block.tensor
            def _(pe):
                for r in range(2):
                    for n in range(NCH):
                        for hp in range(2):
                            mm = pe.matmul(ps[HD * hp:HD * hp + HD, 1024 * r + GV * n:1024 * r + GV * (n + 1)],
                                           GVT[:, 2 * r + hp, CH * n:CH * (n + 1)], ident, start=True, stop=True)
                    mm.then_inc(s_rows, 1)
                for a in range(3):
                    mm = pe.matmul(bank(4, P, P * a), AVT[:, P * a:P * a + P], ident, start=True, stop=True)
                mm.then_inc(s_rows, 1)
                for u in range(4):
                    if u == 3:
                        pe.wait_ge(s_free, 1)
                    r, d = divmod(u, 2)
                    pe.matmul(bank(5 + u) if u < 3 else bank(4), DEC[0:2 * LR, 256 * d + P * r:256 * d + P * r + P],
                              LRT[0:2 * LR, :], start=True, stop=True).then_inc(s_ldp, 1)
                for h in range(10):
                    if h == 8:
                        pe.wait_ge(s_free, 2)
                    src = AQK[0:HD, h, CTX:T] if h < 8 else AK[0:HD, h - 8, CTX:T]
                    b = h // 2 if h < 8 else 5
                    mm = pe.matmul(bank(b, LAT, LAT * (h % 2))[0:HD], C[0:HD, C_PERM:C_PERM + HD], src,
                                   start=True, stop=True)
                    mm.then_inc(s_rope, 1)

            @block.gpsimd
            def _(pool):
                pass

            @block.vector
            def _(dve):
                cos = C[0:HD, C_COS:C_COS + LAT]
                sin = C[0:HD, C_SIN:C_SIN + LAT]
                for h in range(10):
                    dve.wait_ge(s_rope, h // 2 * 2 + 2)
                    b = h // 2 if h < 8 else 5
                    x = AQK[0:HD, h, CTX:T] if h < 8 else AK[0:HD, h - 8, CTX:T]
                    dve.tensor_tensor(ROT[0:HD, h, :], bank(b, LAT, LAT * (h % 2))[0:HD], sin, ALU.mult)
                    dve_o(dve.tensor_tensor(x, x, cos, ALU.mult))
                    dve_o.inc(dve.tensor_tensor(x, x, ROT[0:HD, h, :], ALU.add))
                dve_o.wait()
                dve.wait_ge(s_l, 1)
                zf, ef, lf = (v.rearrange("p r d t -> p (r d t)") for v in (Z_, E_, LD))
                dve_o(dve.tensor_scalar(zf, zf, 0.0, 1.0 / 16.0, ALU.min, ALU.mult))
                dve_o(dve.scalar_tensor_tensor(out=lf, in0=ef, scalar=-1.0 / 16.0, in1=zf,
                                               op0=ALU.mult, op1=ALU.add))

        units = [(h, -1) for h in range(AH)] + [(h, b) for h in range(AH) for b in range(2)]
        NU = len(units)
        S = area(at_tmp, 3 * T, b=3, t=T)
        PR = area(at_tmp + 3 * T, 2 * T, b=2, t=T)
        PTR = area(at_tmp + 5 * T, 2 * T, b=2, t=T)
        ST = area(at_tmp + 7 * T, 8 * NU, u=NU, v=8)
        s_sc, s_scr, s_nm, s_p, s_pn = (sem("scores_ready"), sem("scores_read"), sem("row_max_ready"), sem("probs_ready"),
                                        sem("probs_normalised"))
        s_pt, s_ptc, s_ao, s_aoc = sem("probs_turned"), sem("turned_probs_stored"), sem("attention_ready"), sem("attention_stored")
        with nc.Block() as block:
            def keys(b):
                return CTX if b < 0 else T

            @block.tensor
            def _(pe):
                def scores(u):
                    h, b = units[u]
                    kv = h // (AH // AKV)
                    if u >= 3:
                        pe.wait_ge(s_scr, u - 2)
                    if b < 0:
                        mm = pe.matmul(bank(u % 3, CTX), AQK[0:HD, h, 0:CTX], AK[0:HD, kv, 0:CTX], start=True, stop=True)
                    else:
                        q = AQK[0:HD, h, CTX + P * b:CTX + P * b + P]
                        pe.matmul(bank(u % 3, P), q, CK[0:HD, kv, :], start=True, stop=True)
                        mm = pe.matmul(bank(u % 3, LAT, P), q, AK[0:HD, kv, CTX:T], start=True, stop=True)
                    mm.then_inc(s_sc, 1)

                def turn(u):
                    pe.wait_ge(s_pn, u + 1)
                    if u >= 2:
                        pe.wait_ge(s_ptc, u - 1)
                    for a in range(keys(units[u][1]) // P):
                        mm = pe.transpose(bank(3 + u % 2, P, P * a), PR[:, u % 2, P * a:P * a + P], ident)
                    mm.then_inc(s_pt, 1)

                def mix(u):
                    h, b = units[u]
                    kv = h // (AH // AKV)
                    pe.wait_ge(s_ptc, u + 1)
                    if u >= 2:
                        pe.wait_ge(s_aoc, u - 1)
                    vs = [VR[:, 0, HD * kv:HD * kv + HD]] if b < 0 else \
                        [CV[:, kv, :], VR[:, 1, HD * kv:HD * kv + HD], VR[:, 2, HD * kv:HD * kv + HD]]
                    o = bank(5 + u % 2, P)[HD * (h % 2):HD * (h % 2) + HD]
                    for a, v in enumerate(vs):
                        mm = pe.matmul(o, v, PTR[:, u % 2, P * a:P * a + P], start=a == 0, stop=a == len(vs) - 1)
                    mm.then_inc(s_ao, 1)

                scores(0)
                for u in range(NU):
                    if u + 1 < NU:
                        scores(u + 1)
                    turn(u)
                    if u >= 1:
                        mix(u - 1)
                mix(NU - 1)

            @block.scalar
            def _(act):
                def exps(u):
                    h, b = units[u]
                    n = keys(b)
                    act.wait_ge(s_nm, u + 1)
                    if u >= 2:
                        act.wait_ge(s_pt, u - 1)
                    act.activation(ST[:, u, 3:4], SINK[:, h:h + 1], ACT.Exp, bias=ST[:, u, 1:2])
                    act.activation(PR[:, u % 2, 0:n], S[:, u % 3, 0:n], ACT.Exp, bias=ST[:, u, 1:2],
                                   accum_out=ST[:, u, 2:3]).then_inc(s_p, 1)

                def store_turned(u):
                    n = keys(units[u][1])
                    act.wait_ge(s_pt, u + 1)
                    if u >= 2:
                        act.wait_ge(s_ao, u - 1)
                    act.activation(PTR[:, u % 2, 0:n], bank(3 + u % 2, n), ACT.Copy).then_inc(s_ptc, 1)

                def store_out(u):
                    h, b = units[u]
                    act.wait_ge(s_ao, u + 1)
                    p0, t0 = HD * (h % 2), 0 if b < 0 else CTX + P * b
                    act.activation(OT[p0:p0 + HD, 4 + h // 2, t0:t0 + P], bank(5 + u % 2, P)[p0:p0 + HD],
                                   ACT.Copy).then_inc(s_aoc, 1)

                for u in range(NU + 2):
                    if u < NU:
                        exps(u)
                    if 1 <= u <= NU:
                        store_turned(u - 1)
                    if u >= 2:
                        store_out(u - 2)

            @block.vector
            def _(dve):
                def front(u):
                    h, b = units[u]
                    n = keys(b)
                    dve.wait_ge(s_sc, u + 1)
                    if u >= 3:
                        dve.wait_ge(s_p, u - 2)
                    if b < 0:
                        dve.tensor_copy(S[:, u % 3, 0:n], bank(u % 3, n)).then_inc(s_scr, 1)
                    else:
                        dve.tensor_tensor(S[:, u % 3, :], bank(u % 3), C[:, C_MASK + T * b:C_MASK + T * (b + 1)],
                                          ALU.add).then_inc(s_scr, 1)
                    dve.wait_ge(s_scr, u + 1)
                    dve_o(dve.reduce_max(ST[:, u, 0:1], S[:, u % 3, 0:n], AX))
                    dve.tensor_scalar(ST[:, u, 1:2], ST[:, u, 0:1], SINK[:, h:h + 1], -1.0,
                                      ALU.max, ALU.mult).then_inc(s_nm, 1)

                def back(u):
                    n = keys(units[u][1])
                    dve.wait_ge(s_p, u + 1)
                    dve_o(dve.tensor_tensor(ST[:, u, 4:5], ST[:, u, 2:3], ST[:, u, 3:4], ALU.add))
                    dve_o(dve.reciprocal(ST[:, u, 5:6], ST[:, u, 4:5]))
                    dve.tensor_scalar(PR[:, u % 2, 0:n], PR[:, u % 2, 0:n], ST[:, u, 5:6], None,
                                      ALU.mult).then_inc(s_pn, 1)

                front(0)
                for u in range(NU):
                    if u + 1 < NU:
                        front(u + 1)
                    back(u)

        a_[0] = at_aq
        B = area(take(4 * T), 4 * T, r=2, d=2, t=T)
        QE = area(take(4 * T), 4 * T, r=2, d=2, t=T)
        assert a_[0] <= at_aq + 8 * T
        a_[0] = at_tmp
        KN = area(take(4 * T), 4 * T, r=2, d=2, t=T)
        KD = area(take(4 * T), 4 * T, r=2, d=2, t=T)
        KDR = area(take(4 * T), 4 * T, r=2, d=2, n=NCH, k=HD)
        AT = area(take(4 * T), 4 * T, r=2, d=2, n=NCH, k=CH)
        TOT = area(take(4 * NCH), 4 * NCH, r=2, d=2, n=NCH)
        EBT = area(take(4 * NCH), 4 * NCH, r=2, d=2, n=NCH)
        ZG = area(take(8 * GV), 8 * GV, r=2, a=4, v=GV)
        OF = area(take(8 * T), 8 * T, d=2, h=4, t=T)
        assert a_[0] <= 30880
        LANES = ((0, (2, 3, 4, 5)), (1, (5, 4, 3, 2)), (0, (0, 1)), (1, (1, 0)))

        def lanes_at(s):
            return [(a, d, n[s]) for a, (d, n) in enumerate(LANES) if s < len(n)]

        s_tot, s_b, s_e, s_qk, s_am, s_ams, s_zin = (
            sem("gla_totals_ready"), sem("gla_cumulated_ready"), sem("gla_exps_ready"), sem("gla_operands_ready"),
            sem("gla_matrices_ready"), sem("gla_matrices_stored"), sem("gla_state_in"))
        s_go, s_gz, s_goc, s_gzc = (sem("gla_chunk_ready"), sem("gla_state_products_ready"), sem("gla_chunk_stored"),
                                    sem("gla_state_updated"))
        with nc.Block() as block:
            def flat(v):
                return v.rearrange("p r d t -> p (r d t)")

            @block.sync
            def _(sp):
                for r in range(2):
                    sp.dma_start(ZG[:, r, 0:2], zgla[r]).then_inc(s_zin, 16)
                sp.wait_ge(s_zin, 32)

            @block.vector
            def _(dve):
                dve_o.inc(dve.memset(ZG[:, :, 2:4], 0.0))
                for r in range(2):
                    for d in range(2):
                        dve_o.inc(dve.tensor_tensor_scan(B[:, r, d, :], C[:, C_KEEP:C_KEEP + T], LD[:, r, d, :], 0.0,
                                                         ALU.mult, ALU.add))
                dve_o.wait()
                Bc = B.rearrange("p r d (n i) -> p r d n i", i=CH)
                for r in range(2):
                    dve_o.inc(dve.tensor_copy(TOT[:, r], Bc[:, r, :, :, CH - 1]))
                dve_o.wait()
                dve.sem_inc(s_tot, 1)
                for r in range(2):
                    dve_o(dve.scalar_tensor_tensor(out=B[:, r, 1, :], in0=B[:, r, 1, :], scalar=-1.0,
                                                   in1=LD[:, r, 1, :], op0=ALU.mult, op1=ALU.add))
                    dve_o.inc(dve.tensor_tensor(Bc[:, r, 1], Bc[:, r, 1],
                                                TOT[:, r, 1].unsqueeze(2).broadcast_to([P, NCH, CH]), ALU.add))
                dve_o.wait()
                for r in range(2):
                    kd = KD[:, r].rearrange("p d (n i) -> p d n i", i=CH)
                    dve_o.inc(dve.scalar_tensor_tensor(
                        out=KD[:, r].rearrange("p d (n i) -> p (d n) i", i=CH),
                        in0=B[:, r].rearrange("p d (n i) -> p (d n) i", i=CH), scalar=-1.0,
                        in1=TOT[:, r].rearrange("p d n -> p (d n)").unsqueeze(2).broadcast_to([P, 2 * NCH, CH]),
                        op0=ALU.mult, op1=ALU.add))
                dve_o.wait()
                dve.sem_inc(s_b, 1)
                dve.wait_ge(s_e, 1)
                for dst, src in ((QE, QG), (KN, KG), (KD, KG)):
                    for r in range(2):
                        dve_o.inc(dve.tensor_tensor(dst[:, r], dst[:, r], src[:, r].unsqueeze(1).broadcast_to([P, 2, T]),
                                                    ALU.mult))
                dve_o.wait()
                dve.sem_inc(s_qk, 1)
                for r in range(2):
                    dve.wait_ge(s_am, r + 1)
                    m = C[:, C_INCL:C_INCL + 2 * CH].rearrange("p (d i) -> p d i", d=2).unsqueeze(2)
                    dve.tensor_tensor(AT[:, r], ps[:, 1024 * r:1024 * r + 2 * T].rearrange("p (d n i) -> p d n i", d=2, n=NCH),
                                      m.broadcast_to([P, 2, NCH, CH]), ALU.mult).then_inc(s_ams, 1)
                    dve.tensor_copy(KDR[:, r], ps[:, 2048 + 1024 * r:2048 + 1024 * r + 2 * T].rearrange(
                        "p (d n i) -> p d n i", d=2, n=NCH)).then_inc(s_ams, 1)
                for s in range(4):
                    dve.wait_ge(s_gz, s + 1)
                    for r in range(2):
                        for a, d, n in lanes_at(s):
                            z = bank(2 + r, GV, a * GV)
                            dve_o.inc(dve.scalar_tensor_tensor(out=ZG[:, r, a], in0=ZG[:, r, a],
                                                               scalar=EBT[:, r, d, n:n + 1], in1=z,
                                                               op0=ALU.mult, op1=ALU.add))
                    dve_o.wait()
                    dve.sem_inc(s_gzc, 1)

            @block.scalar
            def _(act):
                act.wait_ge(s_tot, 1)
                act.activation(EBT.rearrange("p r d n -> p (r d n)"), TOT.rearrange("p r d n -> p (r d n)"), ACT.Exp)
                act.wait_ge(s_b, 1)
                act.activation(flat(QE), flat(B), ACT.Exp)
                act.activation(flat(KN), flat(B), ACT.Exp, scale=-1.0)
                act_o(act.activation(flat(KD), flat(KD), ACT.Exp))
                act.sem_inc(s_e, 1)
                for s in range(4):
                    act.wait_ge(s_go, s + 1)
                    for a, d, n in lanes_at(s):
                        src = ps[:, 0:1024].rearrange("p (x r a i) -> p r x a i", x=2, r=2, a=4)[:, :, :, a, :]
                        dst = OF[:, d].rearrange("p (r x) t -> p r x t", r=2)[:, :, :, CH * n:CH * n + CH]
                        act_o.inc(act.activation(dst, src, ACT.Copy))
                    act_o.wait()
                    act.sem_inc(s_goc, 1)
                act.wait_ge(s_gzc, 4)
                for r in range(2):
                    act.dma_start(gla_out[r], ZG[:, r, 2:4]).then_inc(out_sem, 16)
                n_out[0] += 32
                act.wait_ge(out_sem, n_out[0])

            @block.tensor
            def _(pe):
                pe.wait_ge(s_qk, 1)
                for r in range(2):
                    for which in range(2):
                        for d in range(2):
                            for n in range(NCH):
                                for hp in range(2):
                                    h = slice(HD * hp, HD * hp + HD)
                                    i = slice(CH * n, CH * n + CH)
                                    c = 1024 * r + 2048 * which + T * d + CH * n
                                    o = ps[h, c:c + CH]
                                    if which == 0:
                                        mm = pe.matmul(o, KN[h, r, d, i], QE[h, r, d, i], start=True, stop=True)
                                    else:
                                        mm = pe.matmul(o, KD[h, r, d, i], C[h, C_I64:C_I64 + CH], start=True, stop=True)
                    mm.then_inc(s_am, 1)
                pe.wait_ge(s_ams, 4)
                pe.wait_ge(s_zin, 32)
                for s in range(4):
                    if s:
                        pe.wait_ge(s_gzc, s)
                        pe.wait_ge(s_goc, s)
                    for r in range(2):
                        for hp in range(2):
                            h = slice(HD * hp, HD * hp + HD)
                            for a, d, n in lanes_at(s):
                                c = ((2 * hp + r) * 4 + a) * CH
                                o = ps[:, c:c + CH]
                                pe.matmul(o, ZG[h, r, a], QE[h, r, d, CH * n:CH * n + CH], start=True, stop=False)
                                mm = pe.matmul(o, GVR[h, r, n], AT[h, r, d, n], start=False, stop=True)
                    mm.then_inc(s_go, 1)
                    for r in range(2):
                        for hp in range(2):
                            h = slice(HD * hp, HD * hp + HD)
                            for a, d, n in lanes_at(s):
                                mm = pe.matmul(bank(2 + r, GV, a * GV)[h], KDR[h, r, d, n], GVR[h, r, n],
                                               start=True, stop=True)
                    mm.then_inc(s_gz, 1)

        s_go2, s_gsq, s_gss, s_gv, s_gsd = (sem("gla_sum_ready"), sem("gla_squares_ready"), sem("gla_square_sums_ready"),
                                            sem("gla_variance_ready"), sem("gla_std_ready"))
        O4 = area(at_aq, 4 * T)
        SQ4 = area(at_aq + 4 * T, 4 * T)
        with nc.Block() as block:
            @block.vector
            def _(dve):
                dve_o(dve.tensor_tensor(O4, OF[:, 0].rearrange("p h t -> p (h t)"), OF[:, 1].rearrange("p h t -> p (h t)"),
                                        ALU.add))
                dve.sem_inc(s_go2, 1)
                dve.wait_ge(s_gss, 1)
                dve.tensor_scalar(SQ4.rearrange("p (h t) -> p h t", h=4),
                                  ps[:, 0:2048].rearrange("p (h t) -> p h t", h=4)[:, :, 0:T],
                                  1.0 / GV, EPS, ALU.mult, ALU.add).then_inc(s_gv, 1)
                dve.wait_ge(s_gsd, 1)
                dve_o(dve.reciprocal(SQ4, SQ4))
                dve_o(dve.scalar_tensor_tensor(out=SQ4, in0=SQ4, scalar=V[:, V_GNORM:V_GNORM + 1], in1=O4,
                                               op0=ALU.mult, op1=ALU.mult))
                dve_o(dve.tensor_tensor(OT[:, 0:4].rearrange("p h t -> p (h t)"), SQ4, SG.rearrange("p h t -> p (h t)"),
                                        ALU.mult))

            @block.scalar
            def _(act):
                act.wait_ge(s_go2, 1)
                act.activation(SQ4, O4, ACT.Square).then_inc(s_gsq, 1)
                act.wait_ge(s_gv, 1)
                act.activation(SQ4, SQ4, ACT.Sqrt).then_inc(s_gsd, 1)

            @block.tensor
            def _(pe):
                pe.wait_ge(s_gsq, 1)
                for h in range(4):
                    mm = pe.matmul(bank(h), ones, SQ4[:, T * h:T * h + T], start=True, stop=True)
                mm.then_inc(s_gss, 1)

        def out_block(l, at, src, end, name):
            s_o, s_oc = sem(name + "_ready"), sem(name + "_added")
            with nc.Block() as block:
                @block.sync
                def _(sp):
                    stream(sp, end)

                @block.tensor
                def _(pe):
                    linear(pe, at, range(8), src, s_o, s_oc)

                @block.vector
                def _(dve):
                    for m in range(KC):
                        dve.wait_ge(s_o, m + 1)
                        for c, a, b in STREAMS:
                            last = dve.scalar_tensor_tensor(out=XT[:, m, a:b], in0=bank(m)[:, a:b],
                                                            scalar=mod[:, l, 2, m, c:c + 1], in1=XT[:, m, a:b],
                                                            op0=ALU.mult, op1=ALU.add)
                        last.then_inc(s_oc, 1)

        out_block(0, AT_OUT, OT, AT_OUT + N_OUT + RING, "mixer0_out")

        def moe_block(l, at, end):
            tag = f"moe{l}_"
            m0 = 2 * T
            ACC = area(m0, KC * T, k=KC, t=T)
            r0 = m0 + KC * T
            WR = area(r0, KC * 20, k=KC, e=20)
            BR = area(r0 + 160, 20)
            LG = area(r0 + 180, 60, a=3, e=20)
            RW = area(r0 + 240, 3 * 64, a=3, e=64)
            MK = area(r0 + 432, 3 * NE, a=3, e=NE)
            RKM = area(r0 + 480, 3 * (NE + 1), a=3, e=NE + 1)
            CNT = area(r0 + 531, 1)
            CNTI = A[:, r0 + 532:r0 + 533].bitcast(I32)
            RC = area(r0 + 533, CAP + P)
            b0 = r0 + 533 + CAP + P
            IOTA, BEFORE = RC[:, 0:CAP], RC[:, CAP:CAP + P]
            s_rw, s_lg, s_m, s_ex, s_mk, s_rk, s_gu, s_silu, s_hid, s_dn, s_acc, s_ord = (sem(tag + n) for n in (
                "router_weights_in", "logits_ready", "router_max_ready", "router_exps_ready", "assignment_ready",
                "ranks_ready", "gate_up_ready", "silu_ready", "hidden_ready", "products_to_add_ready", "products_added",
                "dve_order"))
            GATES = RW[:, :, 0:16]
            with nc.Block() as block:
                @block.sync
                def _(sp):
                    sp.dma_start(WR, wrt[l]).then_inc(s_rw, 16)
                    sp.dma_start(BR, brt[l].partition_broadcast(P)).then_inc(s_rw, 16)
                    sp.dma_start(RC, rcst).then_inc(s_rw, 16)
                    sp.wait_ge(s_rw, 48)

                @block.tensor
                def _(pe):
                    pe.wait_ge(s_rw, 48)
                    for a in range(3):
                        for k in range(KC):
                            mm = pe.matmul(bank(0, 20, 20 * a), HT[:, k, P * a:P * a + P], WR[:, k, :],
                                           start=k == 0, stop=k == KC - 1)
                    mm.then_inc(s_lg, 1)
                    pe.wait_ge(s_mk, 1)
                    for a in range(3):
                        for b in range(a + 1):
                            pe.matmul(bank(1, NE, NE * a), ones if b < a else BEFORE, MK[:, b], start=b == 0, stop=b == a)
                    for b in range(3):
                        mm = pe.matmul(bank(1, NE, NE * 3), ones, MK[:, b], start=b == 0, stop=b == 2)
                    mm.then_inc(s_rk, 1)

                @block.scalar
                def _(act):
                    act.wait_ge(s_m, 1)
                    for a in range(3):
                        act_o.inc(act.activation(RW[:, a, 44:48], LG[:, a, 0:4], ACT.Exp, bias=RW[:, a, 40:41],
                                                 accum_out=RW[:, a, 48:49]))
                        act_o.inc(act.activation(RW[:, a, 49:50], RW[:, a, 38:39], ACT.Exp, bias=RW[:, a, 39:40]))
                    act_o.wait()
                    act.sem_inc(s_ex, 1)

                @block.vector
                def _(dve):
                    dve_o.inc(dve.memset(ACC, 0.0))
                    dve_o.inc(dve.memset(RKM, 2.0 * T))
                    dve.wait_ge(s_rw, 48)
                    dve.wait_ge(s_lg, 1)
                    dve_o(dve.tensor_tensor(LG, bank(0, 60).rearrange("p (a e) -> p a e", a=3),
                                            BR.unsqueeze(1).broadcast_to([P, 3, 20]), ALU.add))

                    def first_max(x, one, mx, t):
                        dve_o(dve.tensor_reduce(mx, x, AX, ALU.max))
                        dve_o(dve.tensor_tensor(one, x, mx.broadcast_to([P, 3, 4]), ALU.is_equal))
                        dve_o(dve.tensor_scalar(t, one[:, :, 0:1], -1.0, 1.0, ALU.mult, ALU.add))
                        for j in range(1, 4):
                            dve_o(dve.tensor_tensor(one[:, :, j:j + 1], one[:, :, j:j + 1], t, ALU.mult))
                            if j < 3:
                                dve_o(dve.tensor_tensor(t, t, one[:, :, j:j + 1], ALU.subtract))

                    G = RW[:, :, 16:20]
                    first_max(LG[:, :, 0:4], G, RW[:, :, 50:51], RW[:, :, 51:52])
                    sel = RW[:, :, 20:24]
                    by_group = GATES.rearrange("p a (g j) -> p a g j", g=NG)
                    gb = G.unsqueeze(3).broadcast_to([P, 3, NG, EPG])
                    dve_o(dve.tensor_tensor(by_group, LG[:, :, 4:20].rearrange("p a (g j) -> p a g j", g=NG), gb, ALU.mult))
                    dve_o(dve.tensor_reduce(sel, GATES.rearrange("p a (g j) -> p a j g", g=NG), AX, ALU.add))
                    F1, F2 = RW[:, :, 24:28], RW[:, :, 28:32]
                    first_max(sel, F1, RW[:, :, 52:53], RW[:, :, 51:52])
                    sel2 = RW[:, :, 32:36]
                    dve_o(dve.tensor_scalar(sel2, F1, -3.0e38, None, ALU.mult))
                    dve_o(dve.tensor_tensor(sel2, sel2, sel, ALU.add))
                    first_max(sel2, F2, RW[:, :, 38:39], RW[:, :, 51:52])
                    dve_o(dve.tensor_scalar(RW[:, :, 39:40], RW[:, :, 52:53], -1.0, None, ALU.mult))
                    dve_o(dve.tensor_scalar(RW[:, :, 40:41], RW[:, :, 50:51], -1.0, None, ALU.mult))
                    dve.sem_inc(s_m, 1)
                    dve_o(dve.tensor_tensor(sel2, F1, F2, ALU.add))
                    mk4 = MK.rearrange("p a (g j) -> p a g j", g=NG)
                    dve_o(dve.tensor_tensor(mk4, gb, sel2.unsqueeze(2).broadcast_to([P, 3, NG, EPG]), ALU.mult))
                    dve.sem_inc(s_mk, 1)
                    dve.wait_ge(s_ex, 1)
                    x1, den = RW[:, :, 49:50], RW[:, :, 53:54]
                    dve_o(dve.tensor_scalar(den, x1, 1.0, None, ALU.add))
                    dve_o(dve.tensor_tensor(den, den, RW[:, :, 48:49], ALU.mult))
                    dve_o(dve.reciprocal(RW[:, :, 54:55], den))
                    dve_o(dve.tensor_tensor(RW[:, :, 55:56], RW[:, :, 54:55], x1, ALU.mult))
                    dve_o(dve.tensor_tensor(F1, F1, RW[:, :, 54:55].broadcast_to([P, 3, 4]), ALU.mult))
                    dve_o(dve.tensor_tensor(F2, F2, RW[:, :, 55:56].broadcast_to([P, 3, 4]), ALU.mult))
                    dve_o(dve.tensor_tensor(F1, F1, F2, ALU.add))
                    dve_o(dve.tensor_tensor(by_group, gb, F1.unsqueeze(2).broadcast_to([P, 3, NG, EPG]), ALU.mult))
                    dve.wait_ge(s_rk, 1)
                    dve_o(dve.tensor_reduce(CNT, bank(1, NE, NE * 3), AX, ALU.max))
                    dve_o(dve.tensor_copy(CNTI, CNT))
                    dve_o(dve.scalar_tensor_tensor(out=RKM[:, :, 0:NE], in0=MK, scalar=-2.0 * T,
                                                   in1=bank(1, 3 * NE).rearrange("p (a e) -> p a e", a=3),
                                                   op0=ALU.mult, op1=ALU.add))
                    dve_o(dve.tensor_scalar(RKM[:, :, 0:NE], RKM[:, :, 0:NE], 2.0 * T, None, ALU.add))

            HR = area(b0, 3 * D, a=3, d=D)
            HG = area(b0 + 3 * D, KC * CAP, k=KC, s=CAP)
            o1 = b0 + 3 * D + KC * CAP
            SEL = area(o1, 3 * CAP, a=3, s=CAP)
            SELG = area(o1 + 3 * CAP, 3 * CAP, a=3, s=CAP)
            SGT = area(o1 + 6 * CAP, T)
            HIDG = area(o1 + 6 * CAP + T, 4 * CAP, f=4, s=CAP)
            SLG = area(o1 + 10 * CAP + T, 2 * CAP, b=2, s=CAP)
            OUTR = area(o1 + 12 * CAP + T, D)
            assert o1 + 12 * CAP + T + D <= 30880
            GB = area(b0, NE * T, e=NE, t=T)
            HID = area(b0 + NE * T, 4 * T, f=4, t=T)
            SL = area(b0 + (NE + 4) * T, 2 * T, b=2, t=T)
            GT = area(b0 + (NE + 6) * T, T)
            s_hr, s_sl, s_ga, s_hg, s_tr, s_sgt, s_ou, s_ous = (sem(tag + n) for n in (
                "token_rows_stored", "slots_ready", "gather_ready", "gather_stored", "gates_turned",
                "turned_gates_stored", "expert_out_ready", "expert_out_stored"))

            with nc.Block() as block:
                @block.sync
                def _(sp):
                    stream(sp, end)

                def gathered_pe(pe):
                    for j in range(6):
                        for i in range(4):
                            k = 4 * (j % 2) + i
                            mm = pe.transpose(bank(j, P, P * i), HT[:, k, P * (j // 2):P * (j // 2) + P], ident)
                        if j % 2:
                            mm.then_inc(s_ga, 1)
                    pe.wait_ge(s_hr, 3)

                    def gather():
                        for k in range(KC):
                            for a in range(3):
                                mm = pe.matmul(bank(3 + k // 4, CAP, CAP * (k % 4)), HR[:, a, P * k:P * k + P], SEL[:, a, :],
                                               start=a == 0, stop=a == 2)
                        mm.then_inc(s_ga, 1)

                    def scatter(e):
                        pe.wait_ge(s_ous, e * 2 + 2)
                        pe.wait_ge(s_sgt, e + 1)
                        for m in range(KC):
                            pe.wait_ge(s_acc, e * 8 + (m + 1))
                            pe.matmul(bank(4 + m % 4), OUTR[0:CAP, P * m:P * m + P], SGT[0:CAP, :],
                                      start=True, stop=True).then_inc(s_dn, 1)

                    pe.wait_ge(s_sl, 1)
                    gather()
                    with pe.Fori(0, NE) as e:
                        pe.wait_ge(s_hg, e + 1)
                        for f in range(4):
                            pe.wait_ge(s_hid, e * 4 + (f + 1))
                            for w in range(2):
                                n = at + 2 * (f // 2) + w
                                if f % 2 == 0:
                                    tile_in(pe, n, e)
                                wt = tile(n, k=KC, c=256)
                                for k in range(KC):
                                    mm = pe.matmul(bank(f % 2, CAP, CAP * w), wt[:, k, f % 2 * P:f % 2 * P + P],
                                                   HG[:, k, :], start=k == 0, stop=k == KC - 1)
                            mm.then_inc(s_gu, 1)
                            if f % 2 == 1:
                                pe.wait_ge(s_gu, e * 4 + (f + 1))
                                pe.sem_inc(w_used, 2)
                        scatter(e)
                        pe.wait_ge(s_sl, e + 2)
                        for a in range(3):
                            mm = pe.transpose(bank(2, P, P * a)[0:CAP], SELG[:, a, :], ident)
                        mm.then_inc(s_tr, 1)
                        pe.wait_ge(s_acc, e * 8 + 9)
                        gather()
                        pe.wait_ge(s_hid, e * 4 + 6)
                        pe.wait_ge(s_acc, e * 8 + 12)
                        for j in range(2):
                            n = at + 4 + j
                            tile_in(pe, n, e)
                            wt = tile(n, f=4, c=512)
                            for f in range(4):
                                mm = pe.matmul(bank(6 + j, 512)[0:CAP], HIDG[:, f, :], wt[:, f, :], start=f == 0, stop=f == 3)
                            mm.then_inc(s_ou, 1)
                            pe.wait_ge(s_ou, e * 2 + (j + 1))
                            pe.sem_inc(w_used, 1)
                    scatter(NE)

                def gathered_act(act):
                    for a in range(3):
                        act.wait_ge(s_ga, a + 1)
                        act.activation(HR[:, a, :], ps[:, 1024 * a:1024 * a + 1024], ACT.Copy).then_inc(s_hr, 1)

                    def store_gathered(ready):
                        act.wait_ge(s_ga, ready)
                        act.activation(HG[:, 0:4], bank(3, 4 * CAP).rearrange("p (k s) -> p k s", k=4), ACT.Copy)
                        act.activation(HG[:, 4:8], bank(4, 4 * CAP).rearrange("p (k s) -> p k s", k=4),
                                       ACT.Copy).then_inc(s_hg, 1)

                    store_gathered(4)
                    with act.Fori(0, NE) as e:
                        for f in range(4):
                            act.wait_ge(s_gu, e * 4 + (f + 1))
                            act.wait_ge(s_hid, e * 4 + (f + 1))
                            act.activation(SLG[:, f % 2, :], bank(f % 2, CAP), ACT.Silu).then_inc(s_silu, 1)
                        act.wait_ge(s_tr, e + 1)
                        act.activation(SGT[0:CAP, :], bank(2)[0:CAP], ACT.Copy).then_inc(s_sgt, 1)
                        store_gathered(e + 5)
                        for j in range(2):
                            act.wait_ge(s_ou, e * 2 + (j + 1))
                            act.activation(OUTR[0:CAP, 512 * j:512 * j + 512], bank(6 + j, 512)[0:CAP],
                                           ACT.Copy).then_inc(s_ous, 1)

                def gathered_dve(dve):
                    order = Order(dve, s_ord)
                    order.inc(dve.memset(OUTR, 0.0))
                    order.inc(dve.memset(SGT, 0.0))
                    for a in range(3):
                        order.inc(dve.tensor_scalar(SEL[:, a, :], IOTA, RKM[:, a, 0:1], None, ALU.is_equal))
                    order.wait()
                    dve.sem_inc(s_sl, 1)
                    dve.sem_inc(s_ous, 2)
                    dve.sem_inc(s_sgt, 1)
                    dve.sem_inc(s_hid, 2)
                    dve.sem_inc(s_acc, 4)

                    def add(e):
                        for m in range(KC):
                            dve.wait_ge(s_dn, e * 8 + (m + 1))
                            dve.wait_ge(s_acc, e * 8 + (m + 1))
                            dve.tensor_tensor(ACC[:, m, :], ACC[:, m, :], bank(4 + m % 4), ALU.add).then_inc(s_acc, 1)

                    with dve.Fori(0, NE) as e:
                        order.enter(e, 6)
                        dve.wait_ge(s_ga, e + 4)
                        for a in range(3):
                            order.inc(dve.tensor_scalar(SEL[:, a, :], IOTA, RKM[:, a, bass.ds(e + 1, 1)], None, ALU.is_equal))
                            order.inc(dve.tensor_scalar(SELG[:, a, :], IOTA, RKM[:, a, bass.ds(e, 1)],
                                                        GATES[:, a, bass.ds(e, 1)], ALU.is_equal, ALU.mult))
                        order.wait()
                        dve.sem_inc(s_sl, 1)
                        for f in range(4):
                            dve.wait_ge(s_silu, e * 4 + (f + 1))
                            dve.tensor_tensor(HIDG[:, f, :], SLG[:, f % 2, :], bank(f % 2, CAP, CAP),
                                              ALU.mult).then_inc(s_hid, 1)
                        add(e)
                        order.leave(NE)
                    add(NE)
                    dve.wait_ge(s_acc, 4 + 8 * (NE + 1))

                def general_pe(pe):
                    for a in range(3):
                        mm = pe.transpose(bank(1, P, P * a)[0:NE], GATES[:, a, :], ident)
                    mm.then_inc(s_tr, 1)
                    pe.wait_ge(s_sgt, 1)
                    for e in range(NE):
                        if e >= 4:
                            pe.wait_ge(s_hg, e - 3)
                        pe.matmul(bank(4 + e % 4), ident[0:NE, e:e + 1].broadcast_to([NE, P]), GT[0:NE, :],
                                  start=True, stop=True).then_inc(s_ga, 1)
                    pe.wait_ge(s_hg, NE)
                    with pe.Fori(0, NE) as e:
                        for f in range(4):
                            pe.wait_ge(s_hid, e * 4 + (f + 1))
                            for w in range(2):
                                n = at + 2 * (f // 2) + w
                                if f % 2 == 0:
                                    tile_in(pe, n, e)
                                wt = tile(n, k=KC, c=256)
                                for k in range(KC):
                                    mm = pe.matmul(bank(2 * (f % 2) + w), wt[:, k, f % 2 * P:f % 2 * P + P], HT[:, k, :],
                                                   start=k == 0, stop=k == KC - 1)
                            mm.then_inc(s_gu, 1)
                            if f % 2 == 1:
                                pe.wait_ge(s_gu, e * 4 + (f + 1))
                                pe.sem_inc(w_used, 2)
                        pe.wait_ge(s_hid, e * 4 + 6)
                        for m in range(8):
                            n = at + 4 + m // 4
                            if m % 4 == 0:
                                tile_in(pe, n, e)
                            pe.wait_ge(s_acc, e * 8 + (m + 1))
                            wt = tile(n, f=4, c=512)
                            for f in range(4):
                                mm = pe.matmul(bank(4 + m % 4), wt[:, f, m % 4 * P:m % 4 * P + P], HID[:, f, :],
                                               start=f == 0, stop=f == 3)
                            mm.then_inc(s_dn, 1)
                            if m % 4 == 3:
                                pe.wait_ge(s_dn, e * 8 + (m + 1))
                                pe.sem_inc(w_used, 1)

                def general_act(act):
                    act.wait_ge(s_tr, 1)
                    act.activation(GT[0:NE, :], bank(1)[0:NE], ACT.Copy).then_inc(s_sgt, 1)
                    for e in range(NE):
                        act.wait_ge(s_ga, e + 1)
                        act.activation(GB[:, e, :], bank(4 + e % 4), ACT.Copy).then_inc(s_hg, 1)
                    with act.Fori(0, NE) as e:
                        for f in range(4):
                            act.wait_ge(s_gu, e * 4 + (f + 1))
                            act.wait_ge(s_hid, e * 4 + (f + 1))
                            act.activation(SL[:, f % 2, :], bank(2 * (f % 2)), ACT.Silu).then_inc(s_silu, 1)

                def general_dve(dve):
                    order = Order(dve, s_ord)
                    dve.sem_inc(s_hid, 2)
                    dve.sem_inc(s_acc, 4)
                    dve.wait_ge(s_hg, NE)
                    with dve.Fori(0, NE) as e:
                        order.enter(e, 4)
                        for f in range(4):
                            dve.wait_ge(s_silu, e * 4 + (f + 1))
                            order(dve.tensor_tensor(SL[:, f % 2, :], SL[:, f % 2, :], bank(2 * (f % 2) + 1), ALU.mult))
                            dve.tensor_tensor(HID[:, f, :], SL[:, f % 2, :],
                                              GB[:, bass.ds(e, 1), :].rearrange("p a t -> p (a t)"),
                                              ALU.mult).then_inc(s_hid, 1)
                        order.leave(NE)
                        for m in range(8):
                            dve.wait_ge(s_dn, e * 8 + (m + 1))
                            dve.wait_ge(s_acc, e * 8 + (m + 1))
                            dve.tensor_tensor(ACC[:, m, :], ACC[:, m, :], bank(4 + m % 4), ALU.add).then_inc(s_acc, 1)
                    dve.wait_ge(s_acc, 4 + 8 * NE)

                def by_load(eng, gathered, general):
                    most = eng.value_load(CNTI[0:1, 0:1])
                    with eng.If(most < CAP + 1):
                        gathered(eng)
                    with eng.Else():
                        general(eng)

                @block.tensor
                def _(pe):
                    by_load(pe, gathered_pe, general_pe)

                @block.scalar
                def _(act):
                    by_load(act, gathered_act, general_act)

                @block.vector
                def _(dve):
                    by_load(dve, gathered_dve, general_dve)
                    for m in range(KC):
                        for c, a, b in STREAMS:
                            dve_o.inc(dve.scalar_tensor_tensor(out=XT[:, m, a:b], in0=ACC[:, m, a:b],
                                                               scalar=mod[:, l, 5, m, c:c + 1], in1=XT[:, m, a:b],
                                                               op0=ALU.mult, op1=ALU.add))
                    dve_o.wait()


        norm_block(0, 1, AT_MOE0 + RING)
        moe_block(0, AT_MOE0, AT_RKV + RING)

        norm_block(1, 0, AT_RKV + RING)
        a_[0] = 0
        XX = area(take(KC * T), KC * T, k=KC, t=T)
        XM = [area(take(KC * T), KC * T, k=KC, t=T) for _ in range(2)]
        at_scan_low = 0
        RT, KT, VT, GG = (area(take(KC * T), KC * T, k=KC, t=T) for _ in range(4))
        LH = area(take(2 * T), 2 * T, d=2, t=T)
        WA2 = area(take(2 * D), 2 * D, d=2, k=KC, c=P)
        GHID = area(take(T), T)
        at_top = a_[0]
        assert at_top <= 30880
        s_xx, s_xm, s_pj, s_pjc, s_wa = (sem("shift_ready"), sem("mixed_input_ready"), sem("rwkv_product_ready"),
                                         sem("rwkv_product_stored"), sem("second_factors_in"))
        with nc.Block() as block:
            MIX = (0, 2, 3, 1, 4, 5)

            @block.sync
            def _(sp):
                sp.dma_start(WA2, wa2).then_inc(s_wa, 16)
                stream(sp, AT_WO + 4)
                sp.wait_ge(s_wa, 16)

            @block.vector
            def _(dve):
                for _, a, b in STREAMS:
                    dve_o.inc(dve.tensor_tensor(XX[:, :, a + 1:b - 1], HT[:, :, a:b - 2], HT[:, :, a + 2:b], ALU.add))
                    dve_o.inc(dve.tensor_copy(XX[:, :, a:a + 1], HT[:, :, a + 1:a + 2]))
                    dve_o.inc(dve.tensor_copy(XX[:, :, b - 1:b], HT[:, :, b - 2:b - 1]))
                dve_o.wait()
                dve_o(dve.scalar_tensor_tensor(out=XX.rearrange("p k t -> p (k t)"), in0=XX.rearrange("p k t -> p (k t)"),
                                               scalar=0.5, in1=HT_[:, :], op0=ALU.mult, op1=ALU.subtract))
                done = (0, 0, 8, 16, 24, 26)
                for x, mu in enumerate(MIX):
                    if x >= 2:
                        dve.wait_ge(s_pj, done[x])
                    for k in range(KC):
                        last = dve.scalar_tensor_tensor(out=XM[x % 2][:, k, :], in0=XX[:, k, :],
                                                        scalar=V[:, V_MU + KC * mu + k:V_MU + KC * mu + k + 1],
                                                        in1=HT[:, k, :], op0=ALU.mult, op1=ALU.add)
                        dve_o.inc(last)
                    dve_o.wait()
                    dve.sem_inc(s_xm, 1)

            @block.tensor
            def _(pe):
                for x in range(3):
                    pe.wait_ge(s_xm, x + 1)
                    linear(pe, AT_RKV, range(8 * x, 8 * x + 8), XM[x % 2], s_pj, s_pjc)
                tile_in(pe, AT_LORA)
                w = tile(AT_LORA, k=KC, c=256)
                for x in range(3, 5):
                    pe.wait_ge(s_xm, x + 1)
                    for d in range(2):
                        u = 2 * (x - 3) + d
                        pe.wait_ge(s_pjc, 24 + u - 7)
                        o = bank(u)[HD * (x - 3):HD * (x - 3) + HD]
                        for k in range(KC):
                            mm = pe.matmul(o, w[:, k, HD * u:HD * u + HD], XM[x % 2][:, k, :], start=k == 0, stop=k == KC - 1)
                        mm.then_inc(s_pj, 1)
                pe.wait_ge(s_pj, 28)
                pe.sem_inc(w_used, 1)
                tile_in(pe, AT_GATE)
                pe.wait_ge(s_xm, 6)
                g1 = ring[:, AT_GATE % RING * TILE:AT_GATE % RING * TILE + D].rearrange("p (k c) -> p k c", k=KC)
                g2 = ring[:, AT_GATE % RING * TILE + D:AT_GATE % RING * TILE + 2 * D]
                pe.wait_ge(s_pjc, 21)
                for k in range(KC):
                    mm = pe.matmul(bank(4), g1[:, k, :], XM[1][:, k, :], start=k == 0, stop=k == KC - 1)
                mm.then_inc(s_pj, 1)
                pe.wait_ge(s_pjc, 29)
                for m in range(KC):
                    pe.matmul(bank(m), g2[:, P * m:P * m + P], GHID, start=True, stop=True).then_inc(s_pj, 1)
                pe.wait_ge(s_pj, 37)
                pe.sem_inc(w_used, 1)

            @block.scalar
            def _(act):
                for m in range(37):
                    act.wait_ge(s_pj, m + 1)
                    if m < 24:
                        last = act.activation((RT, KT, VT)[m // 8][:, m % 8, :], bank(m % 8), ACT.Copy)
                    elif m < 26:
                        last = act.activation(LH[0:HD, m - 24, :], bank(m - 24)[0:HD], ACT.Tanh)
                    elif m < 28:
                        last = act.activation(LH[HD:P, m - 26, :], bank(m - 24)[HD:P], ACT.Copy)
                    elif m == 28:
                        last = act.activation(GHID, bank(4), ACT.Sigmoid)
                    else:
                        last = act.activation(GG[:, m - 29, :], bank(m - 29), ACT.Copy)
                    last.then_inc(s_pjc, 1)

        U2 = 2 * T
        a_[0] = at_scan_low

        def two():
            return take(U2)

        def dt(at):
            return area(at, U2, d=2, t=T)

        def dn(at):
            return area(at, U2, d=2, n=NCH, i=CH)

        low = 3 * KC * T
        at_ld, at_b, at_al, at_rho, at_be, at_ka, at_bc, at_kc, at_kka, at_kd, at_at, at_bt = (two() for _ in range(12))
        assert a_[0] <= low
        a_[0] = at_top
        at_m1, at_m2, at_bcr, at_kcr = (two() for _ in range(4))
        VRW = area(take(T), T, n=NCH, v=HD)
        RKV = area(take(3 * T), 3 * T, x=3, t=T)
        PV = area(take(PAIR_VECS), PAIR_VECS)
        W2C = area(take(2 * P), 2 * P, d=2, c=P)
        KK = area(take(T), T)
        TW = area(take(2 * NCH), 2 * NCH, d=2, n=NCH)
        EW = area(take(2 * NCH), 2 * NCH, d=2, n=NCH)
        ZW = area(take(4 * HD), 4 * HD, a=4, v=HD)
        RH = area(take(4 * HD), 4 * HD, a=4, v=HD)
        UU = area(take(4 * HD), 4 * HD, a=4, v=HD)
        BON = GHID
        assert a_[0] <= 30880, a_[0]
        OD = dt(at_ld)
        at_D, at_DT, at_P = at_b, at_kka, at_kd
        KK2 = area(at_kd, T)
        NLEV = len(LEVELS) - 1
        ACT_PER, DVE_PER = 26, 57
        (s_ic, s_si, s_lo, s_sg, s_ksq, s_kss, s_kv, s_kr, s_cu, s_ex2, s_op, s_ma, s_ms, s_rst, s_inv, s_ll, s_ls, s_lr,
         s_rh, s_rhs, s_so, s_sos, s_st, s_os, s_zu, s_osum, s_mean, s_osq, s_var2, s_vs, s_or, s_pd, s_po) = (
            sem("rw_" + name) for name in (
                "pair_inputs_copied", "pair_state_in", "lora_products_ready", "lora_sigmoids_ready", "kk_squares_ready",
                "kk_square_sums_ready", "kk_variance_ready", "kk_root_ready", "cumulated_ready", "decay_exps_ready",
                "operands_ready", "matrices_ready", "matrices_stored", "rows_stored", "inverse_level_ready",
                "level_left_ready", "level_left_stored", "level_right_ready", "rhs_ready", "rhs_stored", "solved_ready",
                "solved_stored", "step_products_ready", "step_out_stored", "state_updated", "out_sum_ready",
                "out_mean_ready", "out_squares_ready", "out_square_sums_ready", "out_variance_ready", "out_root_ready",
                "pair_done", "pair_state_out"))

        s_past = sem("rw_products_past_a_wait")

        def full(at):
            return area(at, U2)

        def psn(b):
            return ps[:, 512 * b:512 * b + U2].rearrange("p (d n i) -> p d n i", d=2, n=NCH)

        def msk(at):
            return C[:, at:at + 2 * CH].rearrange("p (d i) -> p d i", d=2).unsqueeze(2).broadcast_to([P, 2, NCH, CH])

        with nc.Block() as block:
            @block.sync
            def _(sp):
                sp.sem_inc(s_po, 16)
                with sp.Fori(0, KC) as c:
                    sp.wait_ge(s_pd, c + 1)
                    sp.dma_start(ZW[:, 0:2], zrwkv[bass.ds(c, 1)].rearrange("r p d v -> (r p) d v")).then_inc(s_si, 16)
                    sp.wait_ge(s_zu, c * 4 + 2)
                    sp.dma_start(rwkv_out[bass.ds(c, 1)].rearrange("r p d v -> (r p) d v"), ZW[:, 2:4]).then_inc(s_po, 16)
                sp.wait_ge(s_po, 16 * KC + 16)

            @block.scalar
            def _(act):
                with act.Fori(0, KC) as c:
                    act_o.enter(c, ACT_PER)
                    act.wait_ge(s_pd, c + 1)
                    for x, src in enumerate((RT, KT, VT)):
                        act_o.inc(act.activation(RKV[:, x, :], src[:, bass.ds(c, 1), :].rearrange("p a t -> p (a t)"),
                                                 ACT.Copy))
                    act_o.inc(act.activation(W2C, WA2[:, :, bass.ds(c, 1), :].rearrange("p d a c -> p d (a c)"), ACT.Copy))
                    act_o.inc(act.activation(PV, V[:, bass.ds(c * PAIR_VECS + V_PAIR, PAIR_VECS)], ACT.Copy))
                    act_o.wait()
                    act.sem_inc(s_ic, 1)
                    act.wait_ge(s_lo, c + 1)
                    for d in range(2):
                        act_o.inc(act.activation(dt(at_ld)[:, d], bank(d), ACT.Sigmoid, bias=PV[:, d:d + 1]))
                        act_o.inc(act.activation(dt(at_kka)[:, d], bank(2 + d), ACT.Sigmoid, bias=PV[:, 2 + d:3 + d]))
                    act_o.wait()
                    act.sem_inc(s_sg, 1)
                    act.wait_ge(s_kv, c + 1)
                    act.activation(KK2, KK2, ACT.Sqrt).then_inc(s_kr, 1)
                    act.wait_ge(s_cu, c + 1)
                    act_o.inc(act.activation(EW, TW, ACT.Exp))
                    act_o.inc(act.activation(full(at_al), full(at_al), ACT.Exp))
                    act_o.inc(act.activation(full(at_rho), full(at_b), ACT.Exp))
                    act_o.inc(act.activation(full(at_be), full(at_b), ACT.Exp, scale=-1.0))
                    act_o.inc(act.activation(full(at_bc), full(at_bc), ACT.Exp))
                    act_o.wait()
                    act.sem_inc(s_ex2, 1)
                    for n, (dst, b) in enumerate(((full(at_bcr), 2), (full(at_kcr), 4), (VRW.rearrange("p n v -> p (n v)"), 6))):
                        act.wait_ge(s_ma, c * 8 + (6 + n))
                        w = U2 if n < 2 else T
                        act.activation(dst, ps[:, 512 * b:512 * b + w], ACT.Copy).then_inc(s_rst, 1)
                    for s in range(4):
                        act.wait_ge(s_st, c * 4 + (s + 1))
                        for a, d, n in lanes_at(s):
                            act_o.inc(act.activation(OD[:, d, CH * n:CH * n + CH], bank(2, CH, CH * a), ACT.Copy))
                        act_o.wait()
                        act.sem_inc(s_os, 1)
                    act.wait_ge(s_vs, c + 1)
                    act.activation(OD[:, 1], OD[:, 1], ACT.Sqrt).then_inc(s_or, 1)
                    act_o.leave(KC)

            @block.vector
            def _(dve):
                r_, k_, v_ = RKV[:, 0, :], RKV[:, 1, :], RKV[:, 2, :]
                ld, b = dt(at_ld), dt(at_b)
                dve.sem_inc(s_pd, 1)
                kb, kkb, rb = (v.unsqueeze(1).broadcast_to([P, 2, T]) for v in (k_, KK, r_))
                with dve.Fori(0, KC) as c:
                    dve_o.enter(c, DVE_PER)
                    dve.wait_ge(s_ic, c + 1)
                    dve_o(dve.tensor_scalar(KK, k_, PV[:, 4:5], None, ALU.mult))
                    dve_o(dve.tensor_tensor(KK2, KK, KK, ALU.mult))
                    dve.sem_inc(s_ksq, 1)
                    dve.wait_ge(s_po, c * 16 + 16)
                    dve_o.inc(dve.memset(ZW[:, 2:4], 0.0))
                    dve.wait_ge(s_sg, c + 1)
                    dve_o(dve.tensor_scalar(full(at_ld), full(at_ld), -HALF_DECAY, None, ALU.mult))
                    for d in range(2):
                        dve_o.inc(dve.tensor_tensor_scan(b[:, d], C[:, C_KEEP:C_KEEP + T], ld[:, d], 0.0, ALU.mult, ALU.add))
                    dve_o.wait()
                    dve_o(dve.tensor_copy(TW, dn(at_b)[:, :, :, CH - 1]))
                    dve_o(dve.scalar_tensor_tensor(out=b[:, 1], in0=b[:, 1], scalar=-1.0, in1=ld[:, 1],
                                                   op0=ALU.mult, op1=ALU.add))
                    dve_o(dve.tensor_tensor(dn(at_b)[:, 1], dn(at_b)[:, 1],
                                            TW[:, 1].unsqueeze(2).broadcast_to([P, NCH, CH]), ALU.add))
                    dve_o.inc(dve.tensor_tensor(full(at_al), full(at_b), full(at_ld), ALU.subtract))
                    dve_o.inc(dve.scalar_tensor_tensor(
                        out=full(at_bc).rearrange("p (n i) -> p n i", i=CH),
                        in0=full(at_b).rearrange("p (n i) -> p n i", i=CH), scalar=-1.0,
                        in1=TW.rearrange("p d n -> p (d n)").unsqueeze(2).broadcast_to([P, 2 * NCH, CH]),
                        op0=ALU.mult, op1=ALU.add))
                    dve_o.wait()
                    dve.sem_inc(s_cu, 1)
                    dve.wait_ge(s_kss, c + 1)
                    dve.tensor_scalar(KK2, bank(4), 1e-12, None, ALU.add).then_inc(s_kv, 1)
                    dve.wait_ge(s_kr, c + 1)
                    dve_o(dve.reciprocal(KK2, KK2))
                    dve_o(dve.tensor_tensor(KK, KK, KK2, ALU.mult))
                    dve_o(dve.tensor_scalar(full(at_kd), full(at_kka), -1.0, PV[:, 5:6], ALU.add, ALU.mult))
                    dve_o(dve.scalar_tensor_tensor(out=dt(at_kd), in0=dt(at_kd), scalar=1.0, in1=kb,
                                                   op0=ALU.add, op1=ALU.mult))
                    dve_o.inc(dve.tensor_tensor(dt(at_kka), dt(at_kka), kkb, ALU.mult))
                    dve_o.wait()
                    dve.wait_ge(s_ex2, c + 1)
                    dve_o.inc(dve.tensor_tensor(dt(at_al), dt(at_al), kkb, ALU.mult))
                    dve_o.inc(dve.tensor_tensor(dt(at_rho), dt(at_rho), rb, ALU.mult))
                    dve_o.inc(dve.tensor_tensor(full(at_ka), full(at_kd), full(at_be), ALU.mult))
                    dve_o.inc(dve.tensor_tensor(full(at_kc), full(at_kd), full(at_bc), ALU.mult))
                    dve_o.wait()
                    dve_o.inc(dve.tensor_tensor(full(at_be), full(at_kka), full(at_be), ALU.mult))
                    dve_o.inc(dve.tensor_tensor(full(at_bc), full(at_kka), full(at_bc), ALU.mult))
                    dve_o(dve.tensor_tensor(BON, dt(at_kd)[:, 0], dt(at_kd)[:, 1], ALU.add))
                    dve_o(dve.scalar_tensor_tensor(out=BON, in0=BON, scalar=0.5, in1=r_, op0=ALU.mult, op1=ALU.mult))
                    dve_o(dve.tensor_scalar(BON, BON, PV[:, 6:7], None, ALU.mult))
                    dve.sem_inc(s_op, 1)
                    dve.wait_ge(s_ma, c * 8 + 1)
                    dve_o.inc(dve.tensor_tensor(dn(at_at), psn(0), msk(C_STRICT), ALU.mult))
                    dve_o.inc(dve.tensor_tensor(dn(at_DT), psn(0), msk(C_LEV1T), ALU.mult))
                    dve_o.wait()
                    dve.sem_inc(s_ms, 1)
                    dve.wait_ge(s_ma, c * 8 + 2)
                    dve_o.inc(dve.tensor_tensor(dn(at_D), psn(2), msk(C_LEV), ALU.mult))
                    dve_o.wait()
                    dve.sem_inc(s_ms, 1)
                    i64 = C[:, C_I64:C_I64 + CH].unsqueeze(1).broadcast_to([P, 2 * NCH, CH])
                    for at in (at_D, at_DT):
                        v = full(at).rearrange("p (n i) -> p n i", i=CH)
                        dve_o.inc(dve.scalar_tensor_tensor(out=v, in0=v, scalar=-1.0, in1=i64, op0=ALU.mult, op1=ALU.add))
                    dve_o.wait()
                    dve.sem_inc(s_inv, 1)
                    for n, (at, bk, cm) in enumerate(((at_bt, 4, C_STRICT), (at_m1, 6, C_INCL), (at_m2, 0, C_INCL))):
                        dve.wait_ge(s_ma, c * 8 + (3 + n))
                        dve.tensor_tensor(dn(at), psn(bk), msk(cm), ALU.mult).then_inc(s_ms, 1)
                    dve.wait_ge(s_ma, c * 8 + 8)
                    dve_o(dve.tensor_tensor(BON, bank(7), v_, ALU.mult))
                    for n in range(1, NLEV + 1):
                        dve.wait_ge(s_ll, c * NLEV + n)
                        dve.tensor_tensor(dn(at_P), psn(0), msk(C_LEV + 2 * n * CH), ALU.mult).then_inc(s_ls, 1)
                        dve.wait_ge(s_lr, c * NLEV + n)
                        if n < NLEV:
                            dve_o.inc(dve.tensor_tensor(full(at_D), full(at_D), ps[:, 1024:1024 + U2], ALU.subtract))
                        dve_o.inc(dve.tensor_tensor(full(at_DT), full(at_DT), ps[:, 2048:2048 + U2], ALU.subtract))
                        dve_o.wait()
                        dve.sem_inc(s_inv, 1)
                    for s in range(4):
                        ln = lanes_at(s)
                        w = len(ln) * HD
                        dve.wait_ge(s_rh, c * 4 + (s + 1))
                        dve.tensor_copy(RH.rearrange("p a v -> p (a v)")[:, 0:w], bank(0, w)).then_inc(s_rhs, 1)
                        dve.wait_ge(s_so, c * 4 + (s + 1))
                        dve.tensor_scalar(UU.rearrange("p a v -> p (a v)")[:, 0:w], bank(1, w), -1.0, None,
                                          ALU.mult).then_inc(s_sos, 1)
                        dve.wait_ge(s_st, c * 4 + (s + 1))
                        for a, d, n in ln:
                            dve_o.inc(dve.scalar_tensor_tensor(out=ZW[:, a], in0=ZW[:, a], scalar=EW[:, d, n:n + 1],
                                                               in1=bank(3, HD, HD * a), op0=ALU.mult, op1=ALU.add))
                        dve_o.wait()
                        dve.sem_inc(s_zu, 1)
                    dve.wait_ge(s_os, c * 4 + 4)
                    dve.tensor_tensor(OD[:, 0], OD[:, 0], OD[:, 1], ALU.add).then_inc(s_osum, 1)
                    dve.wait_ge(s_mean, c + 1)
                    dve_o(dve.scalar_tensor_tensor(out=OD[:, 0], in0=bank(0), scalar=-1.0 / HD, in1=OD[:, 0],
                                                   op0=ALU.mult, op1=ALU.add))
                    dve.tensor_tensor(OD[:, 1], OD[:, 0], OD[:, 0], ALU.mult).then_inc(s_osq, 1)
                    dve.wait_ge(s_var2, c + 1)
                    dve.tensor_scalar(OD[:, 1], bank(1), 1.0 / HD, LN_EPS, ALU.mult, ALU.add).then_inc(s_vs, 1)
                    dve.wait_ge(s_or, c + 1)
                    dve_o(dve.reciprocal(OD[:, 1], OD[:, 1]))
                    dve_o(dve.tensor_tensor(OD[:, 0], OD[:, 0], OD[:, 1], ALU.mult))
                    dve_o(dve.tensor_scalar(OD[:, 0], OD[:, 0], PV[:, 7:8], PV[:, 8:9], ALU.mult, ALU.add))
                    dve_o(dve.tensor_tensor(OD[:, 0], OD[:, 0], BON, ALU.add))
                    dve.tensor_tensor(OT[:, bass.ds(c, 1), :].rearrange("p a t -> p (a t)"), OD[:, 0],
                                      GG[:, bass.ds(c, 1), :].rearrange("p a t -> p (a t)"), ALU.mult).then_inc(s_pd, 1)
                    dve_o.leave(KC)

            @block.tensor
            def _(pe):
                halves = (slice(0, HD), slice(HD, P))
                chunks = [(d, n) for d in range(2) for n in range(NCH)]
                al, rho, be, ka, bc, kc = (dt(a) for a in (at_al, at_rho, at_be, at_ka, at_bc, at_kc))

                def each(bk, left, right):
                    for d, n in chunks:
                        for h in halves:
                            mm = pe.matmul(ps[h, 512 * bk + T * d + CH * n:512 * bk + T * d + CH * n + CH],
                                           left(h, d, n), right(h, d, n), start=True, stop=True)
                    return mm

                def seg(v):
                    return lambda h, d, n: v[h, d, CH * n:CH * n + CH]

                def mat(at):
                    v = dn(at)
                    return lambda h, d, n: v[h, d, n]

                def unit(h, d, n):
                    return C[h, C_I64:C_I64 + CH]

                def wait(s, value):
                    pe.wait_ge(s, value)
                    pe.sem_inc(s_past, 1)

                with pe.Fori(0, KC) as c:
                    wait(s_ic, c + 1)
                    for d in range(2):
                        for g in range(2):
                            mm = pe.matmul(bank(2 * g + d), W2C[halves[g], d], LH[halves[g], d], start=True, stop=True)
                    mm.then_inc(s_lo, 1)
                    wait(s_ksq, c + 1)
                    pe.matmul(bank(4), heads, KK2, start=True, stop=True).then_inc(s_kss, 1)
                    wait(s_op, c + 1)
                    each(0, seg(be), seg(al)).then_inc(s_ma, 1)
                    each(2, seg(al), seg(be)).then_inc(s_ma, 1)
                    each(4, seg(ka), seg(al)).then_inc(s_ma, 1)
                    each(6, seg(be), seg(rho)).then_inc(s_ma, 1)
                    wait(s_ms, c * 5 + 1)
                    each(0, seg(ka), seg(rho)).then_inc(s_ma, 1)
                    wait(s_ms, c * 5 + 2)
                    each(2, seg(bc), unit).then_inc(s_ma, 1)
                    wait(s_ms, c * 5 + 3)
                    each(4, seg(kc), unit).then_inc(s_ma, 1)
                    wait(s_ms, c * 5 + 4)
                    for n in range(NCH):
                        for h in halves:
                            pe.matmul(ps[h, 3072 + CH * n:3072 + CH * n + CH], RKV[h, 2, CH * n:CH * n + CH],
                                      C[h, C_I64:C_I64 + CH], start=True, stop=True)
                    pe.matmul(bank(7), heads, BON, start=True, stop=True).then_inc(s_ma, 1)
                    wait(s_ms, c * 5 + 5)
                    for n in range(1, NLEV + 1):
                        wait(s_inv, c * (NLEV + 1) + n)
                        each(0, mat(at_at), mat(at_D)).then_inc(s_ll, 1)
                        if n == 1:
                            wait(s_rst, c * 3 + 3)
                        wait(s_ls, c * NLEV + n)
                        if n < NLEV:
                            each(2, mat(at_DT), mat(at_P))
                        each(4, mat(at_P), mat(at_DT)).then_inc(s_lr, 1)
                    wait(s_inv, c * (NLEV + 1) + (NLEV + 1))
                    wait(s_si, c * 16 + 16)
                    bt, dT, m1, m2, bcr, kcr = (dn(a) for a in (at_bt, at_DT, at_m1, at_m2, at_bcr, at_kcr))
                    for s in range(4):
                        ln = lanes_at(s)
                        if s:
                            wait(s_zu, c * 4 + s)
                        for h in halves:
                            for a, d, n in ln:
                                o = bank(0, HD, HD * a)[h]
                                pe.matmul(o, al[h, d, CH * n:CH * n + CH], ZW[h, a], start=True, stop=False)
                                mm = pe.matmul(o, bt[h, d, n], VRW[h, n], start=False, stop=True)
                        mm.then_inc(s_rh, 1)
                        wait(s_rhs, c * 4 + (s + 1))
                        for h in halves:
                            for a, d, n in ln:
                                mm = pe.matmul(bank(1, HD, HD * a)[h], dT[h, d, n], RH[h, a], start=True, stop=True)
                        mm.then_inc(s_so, 1)
                        wait(s_sos, c * 4 + (s + 1))
                        if s:
                            wait(s_os, c * 4 + s)
                        for h in halves:
                            for a, d, n in ln:
                                o = bank(2, CH, CH * a)[h]
                                pe.matmul(o, ZW[h, a], rho[h, d, CH * n:CH * n + CH], start=True, stop=False)
                                pe.matmul(o, UU[h, a], m1[h, d, n], start=False, stop=False)
                                pe.matmul(o, VRW[h, n], m2[h, d, n], start=False, stop=True)
                                z = bank(3, HD, HD * a)[h]
                                pe.matmul(z, bcr[h, d, n], UU[h, a], start=True, stop=False)
                                mm = pe.matmul(z, kcr[h, d, n], VRW[h, n], start=False, stop=True)
                        mm.then_inc(s_st, 1)
                    wait(s_osum, c + 1)
                    pe.matmul(bank(0), heads, OD[:, 0], start=True, stop=True).then_inc(s_mean, 1)
                    wait(s_osq, c + 1)
                    pe.matmul(bank(1), heads, OD[:, 1], start=True, stop=True).then_inc(s_var2, 1)

        out_block(1, AT_WO, OT, AT_MOE1 + RING, "mixer1_out")
        norm_block(1, 1, AT_MOE1 + RING)
        moe_block(1, AT_MOE1, N_TILES)
        norm_block(None, 0, N_TILES)


_INS = ["xT", "cst", "rcst", "vec", "sinkr", "ckT", "cv", "zgla", "zrwkv", "wrt", "brt", "dec2", "wa2", "wstream"]
_OUTS = [("yT", (P, KC * T)), ("kT_out", (HD, 2, CTX)), ("vT_out", (P, CTX)), ("gla_out", (2, P, 2, GV)),
         ("rwkv_out", (KC, P, 2, HD))]


def cols(v):
    return np.asarray(v, np.float32).reshape(-1, P).T


def tiles_of(w, width=256):
    k, n = w.shape
    return w.reshape(k // P, P, n // width, width).transpose(2, 1, 0, 3).reshape(n // width, P, -1)


def lay_out(i):
    f = {k: np.asarray(v) for k, v in i.items()}
    h = {}
    x = np.concatenate([f["x_prompt"][0], f["x_sample"][0]], 0)
    h["xT"] = np.ascontiguousarray(x.T.reshape(KC, P, T).transpose(1, 0, 2).reshape(P, KC * T))
    h["cst"] = constants()
    h["rcst"] = router_constants()
    v = np.zeros((P, V_N), np.float32)
    v[:, V_COND:V_COND + 2 * KC] = np.stack([cols(f["c_ctx"]), cols(f["c"][0])], 2).reshape(P, -1)
    v[:, V_ADA_B:V_NMIX] = cols(f["ada_b"].ravel())
    v[:, V_NMIX:V_NFFN] = cols(f["norm_mix"].ravel())
    v[:, V_NFFN:V_NOUT] = cols(f["norm_ffn"].ravel())
    v[:, V_NOUT:V_MU] = cols(f["norm_out"])
    v[:, V_MU:V_PAIR] = cols(f["rw_mu"][0].ravel())
    pair = [f["rw_w0"][0, 0], f["rw_w0"][0, 1], f["rw_a0"][0, 0], f["rw_a0"][0, 1], f["rw_kk"][0], f["rw_ka"][0],
            f["rw_rk"][0].ravel(), f["rw_lnx_w"][0], f["rw_lnx_b"][0]]
    v[:, V_PAIR:V_GNORM] = np.stack([cols(a) for a in pair], 2).reshape(P, -1)
    v[:, V_GNORM] = f["gla_norm"][0]
    v[:, V_DECB:V_DECB + 4] = f["gla_dec_b"][0].reshape(2, 2, P).transpose(2, 1, 0).reshape(P, 4)
    h["vec"] = v
    h["sinkr"] = f["att_sink"][0].copy()
    h["ckT"] = np.ascontiguousarray(f["cache_attn_k"][0, 0].transpose(2, 1, 0))
    h["cv"] = np.ascontiguousarray(f["cache_attn_v"][0, 0])
    h["zgla"] = np.ascontiguousarray(f["state_gla"][0, 0].reshape(2, 2, P, GV).transpose(1, 2, 0, 3))
    h["zrwkv"] = np.ascontiguousarray(
        f["state_rwkv"][0, 0].reshape(2, KC, 2, HD, HD).transpose(1, 2, 4, 0, 3).reshape(KC, P, 2, HD))
    wr = np.concatenate([f["moe_w_grp"], f["moe_w_exp"]], 2)
    h["wrt"] = np.ascontiguousarray(wr.reshape(2, KC, P, 20).transpose(0, 2, 1, 3))
    h["brt"] = np.concatenate([f["moe_b_grp"], f["moe_b_exp"]], 1)
    dec = np.zeros((2 * LR, 4 * P), np.float32)
    dec[:LR, :256] = f["gla_dec_w"][0, 0]
    dec[LR:, 256:] = f["gla_dec_w"][0, 1]
    h["dec2"] = dec
    h["wa2"] = np.concatenate([f["rw_w2"][0].transpose(1, 0, 2), f["rw_a2"][0].transpose(1, 0, 2)], 0
                              ).reshape(P, 2, KC, P)
    w = np.zeros((N_TILES, P, TILE), np.float32)
    for l in range(2):
        w[AT_ADA + l * MC // 2:AT_ADA + (l + 1) * MC // 2] = tiles_of(f["ada_w"][l])
    w_in = np.zeros((D, 2560), np.float32)
    w_in[:, :IN_W] = f["ev_w_in"][0]
    w[AT_IN:AT_OUT] = tiles_of(w_in)
    w[AT_OUT:AT_MOE0] = tiles_of(f["ev_w_out"][0])
    for l, at in ((0, AT_MOE0), (1, AT_MOE1)):
        for e in range(NE):
            t = at + 6 * e
            w[t:t + 4:2] = tiles_of(f["moe_w_gate"][l, e])
            w[t + 1:t + 4:2] = tiles_of(f["moe_w_up"][l, e])
            w[t + 4:t + 6] = tiles_of(f["moe_w_down"][l, e], 512)
    for n, name in enumerate(("rw_wr", "rw_wk", "rw_wv")):
        w[AT_RKV + 4 * n:AT_RKV + 4 * n + 4] = tiles_of(f[name][0])
    lora = np.concatenate([f["rw_w1"][0, 0], f["rw_w1"][0, 1], f["rw_a1"][0, 0], f["rw_a1"][0, 1]], 1)
    w[AT_LORA] = tiles_of(lora)[0]
    w[AT_GATE, :, :D] = tiles_of(f["rw_g1"][0], P)[0]
    w[AT_GATE, :, D:] = f["rw_g2"][0]
    w[AT_WO:AT_MOE1] = tiles_of(f["rw_wo"][0])
    h["wstream"] = w
    return h


def kernel(**inputs):
    import concourse.bacc as bacc
    from concourse.bass_utils import run_bass_kernel_spmd

    nc = bacc.Bacc("TRN2", target_bir_lowering=False, num_devices=1)
    arrays = lay_out(inputs)
    args = [nc.dram_tensor(n, arrays[n].shape, F32, kind="ExternalInput").ap() for n in _INS]
    args += [nc.dram_tensor(n, shape, F32, kind="ExternalOutput").ap() for n, shape in _OUTS]
    build(nc, *args)
    r = run_bass_kernel_spmd(nc, [arrays], core_ids=[0]).results[0]
    y = r["yT"].reshape(P, KC, T).transpose(2, 1, 0).reshape(1, T, D)
    k = r["kT_out"].transpose(2, 1, 0).reshape(1, 1, CTX, AKV, HD)
    v = r["vT_out"].T.reshape(1, 1, CTX, AKV, HD)
    g = r["gla_out"].reshape(2, 2, HD, 2, GV).transpose(3, 0, 1, 2, 4).reshape(1, 1, 2, GH, HD, GV)
    s = r["rwkv_out"].reshape(KC, 2, HD, 2, HD).transpose(3, 0, 1, 4, 2).reshape(1, 1, 2, 2 * KC, HD, HD)
    c = np.ascontiguousarray
    return c(y[:, :CTX]), c(y[:, CTX:]), c(k), c(v), c(g), c(s)
```

```python
from contextlib import ExitStack

import numpy as np

import concourse.bass as bass
from concourse import mybir

F32 = mybir.dt.float32
I32 = mybir.dt.int32
ALU = mybir.AluOpType
ACT = mybir.ActivationFunctionType
AX = mybir.AxisListType.X

P = 128
D = 1024
KC = D // P
CTX, LAT = 128, 256
T = CTX + LAT
STREAMS = ((0, 0, CTX), (1, CTX, T))
TILE = 2048
RING = 6
MC = 6 * KC
HD = 64
CH = 64
NCH = T // CH
GH, GV = 4, 128
AH, AKV = 8, 2
LR = 16
IN_W = 2336
NE, NG, EPG, FE = 16, 4, 4, 512
CAP = 96
EPS = 1e-6
LN_EPS = 64e-5
HALF_DECAY = float(np.exp(-0.5))

N_ADA = 2 * MC // 2
N_IN = 10
N_OUT = 4
N_MOE = NE * 6
AT_ADA = 0
AT_IN = AT_ADA + N_ADA
AT_OUT = AT_IN + N_IN
AT_MOE0 = AT_OUT + N_OUT
AT_RKV = AT_MOE0 + N_MOE
AT_LORA = AT_RKV + 12
AT_GATE = AT_LORA + 1
AT_WO = AT_GATE + 1
AT_MOE1 = AT_WO + 4
N_TILES = AT_MOE1 + N_MOE

V_COND = 0
V_ADA_B = V_COND + 2 * KC
V_NMIX = V_ADA_B + 2 * MC
V_NFFN = V_NMIX + 2 * KC
V_NOUT = V_NFFN + 2 * KC
V_MU = V_NOUT + KC
V_PAIR = V_MU + 6 * KC
PAIR_VECS = 9
V_GNORM = V_PAIR + PAIR_VECS * KC
V_DECB = V_GNORM + 1
V_N = V_DECB + 4

LEVELS = (1, 2, 4, 8, 16, 32)
C_ID = 0
C_ONES = C_ID + P
C_HEADS = C_ONES + P
C_INCL = C_HEADS + P
C_STRICT = C_INCL + 2 * CH
C_LEV = C_STRICT + 2 * CH
C_LEV1T = C_LEV + (len(LEVELS) - 1) * 2 * CH
C_BLOCK = C_LEV1T + 2 * CH
C_I32 = C_BLOCK + CH
C_I64 = C_I32 + 32
C_KEEP = C_I64 + CH
C_MASK = C_KEEP + T
C_COS = C_MASK + 2 * T
C_SIN = C_COS + LAT
C_PERM = C_SIN + LAT
C_TINY = C_PERM + HD
C_N = C_TINY + 1


def constants():
    c = np.zeros((P, C_N), np.float32)
    c[:, C_ID:C_ID + P] = np.eye(P)
    c[:, C_ONES:C_ONES + P] = 1.0
    c[:64, C_HEADS:C_HEADS + 64] = 1.0
    c[64:, C_HEADS + 64:C_HEADS + 128] = 1.0
    p = np.arange(CH)[:, None]
    f = np.arange(CH)[None, :]

    def put(at, m):
        c[:64, at:at + CH] = m
        c[64:, at:at + CH] = m

    put(C_INCL, p <= f)
    put(C_INCL + CH, p >= f)
    put(C_STRICT, p < f)
    put(C_STRICT + CH, p > f)
    for n, s in enumerate(LEVELS):
        lower = (p // (2 * s) == f // (2 * s)) & (p % (2 * s) >= s) & (f % (2 * s) < s)
        if s == 1:
            put(C_LEV1T, lower.T)
            put(C_LEV1T + CH, lower)
        else:
            put(C_LEV + 2 * (n - 1) * CH, lower)
            put(C_LEV + (2 * n - 1) * CH, lower.T)
    put(C_BLOCK, p // 32 == f // 32)
    put(C_I64, p == f)
    c[:, C_I32:C_I32 + 32] = np.arange(P)[:, None] % 32 == np.arange(32)[None, :]
    c[:, C_KEEP:C_KEEP + T] = np.arange(T) % CH != 0
    for b in range(2):
        q = b * P + np.arange(P)[:, None]
        k = np.arange(LAT)[None, :]
        c[:, C_MASK + b * T + CTX:C_MASK + (b + 1) * T] = np.where(np.abs(q - k) <= 128, 0.0, -1e30)
    freqs = (np.float32(10000.0) ** (-np.arange(0, 32, 2, dtype=np.float32) / np.float32(32))).astype(np.float32)
    t = np.arange(LAT)
    row = (t // 64).astype(np.float32)[None, :] * freqs[:, None]
    col = (t % 64).astype(np.float32)[None, :] * freqs[:, None]
    ang = np.concatenate([row, row, col, col], 0)
    put_at = slice(0, HD)
    c[put_at, C_COS:C_COS + LAT] = np.cos(ang)
    c[put_at, C_SIN:C_SIN + LAT] = np.sin(ang)
    perm = np.zeros((HD, HD), np.float32)
    for half in (0, 32):
        for i in range(16):
            perm[half + 16 + i, half + i] = -1.0
            perm[half + i, half + 16 + i] = 1.0
    c[:HD, C_PERM:C_PERM + HD] = perm
    c[:, C_TINY] = 1e-12
    return c


def router_constants():
    c = np.zeros((P, CAP + P), np.float32)
    c[:, :CAP] = np.arange(CAP)
    c[:, CAP:] = np.arange(P)[:, None] < np.arange(P)[None, :]
    return c


class Order:

    def __init__(self, eng, sem, past=None):
        self.eng, self.sem, self.past, self.n, self.at = eng, sem, past, 0, 0

    def __call__(self, ins):
        self.inc(ins)
        self.wait()

    def inc(self, ins):
        ins.then_inc(self.sem, 1)
        self.n += 1

    def wait(self):
        self.eng.wait_ge(self.sem, self.at + self.n)
        if self.past is not None:
            self.eng.sem_inc(self.past, 1)

    def enter(self, i, per):
        self.start, self.per = self.n, per
        self.at = i * per

    def leave(self, turns):
        assert self.n - self.start == self.per, self.n - self.start
        self.n = self.start + self.per * turns
        self.at = 0


def build(nc, xT, cst, rcst, vec, sinkr, ckT, cv, zgla, zrwkv, wrt, brt, dec2, wa2, wstream,
          yT, kT_out, vT_out, gla_out, rwkv_out):
    ctx = ExitStack()

    def sb(name, words):
        return ctx.enter_context(nc.sbuf_tensor(name, [P, words], F32))

    def sem(name):
        return ctx.enter_context(nc.semaphore(name))

    with ctx:
        ring = sb("ring", RING * TILE)
        XT_ = sb("XT", KC * T)
        HT_ = sb("HT", KC * T)
        C = sb("consts", C_N)
        V = sb("vecs", V_N)
        MOD = sb("mod", 2 * MC * 2)
        GAIN = sb("gain", 2 * 2 * KC * 2)
        SINK = sb("sink", AH)
        A = sb("arena", 30880)
        ps = ctx.enter_context(nc.psum_tensor("ps", [P, 8 * 512], F32))

        XT = XT_[:, :].rearrange("p (k t) -> p k t", k=KC)
        HT = HT_[:, :].rearrange("p (k t) -> p k t", k=KC)
        mod = MOD[:, :].rearrange("p (l a k c) -> p l a k c", l=2, a=6, k=KC)
        gain = GAIN[:, :].rearrange("p (l w k c) -> p l w k c", l=2, w=2, k=KC)
        ident = C[:, C_ID:C_ID + P]
        ones = C[:, C_ONES:C_ONES + P]
        heads = C[:, C_HEADS:C_HEADS + P]

        def bank(b, cols=T, at=0):
            return ps[:, b * 512 + at:b * 512 + at + cols]

        def area(at, words, **dims):
            v = A[:, at:at + words]
            if not dims:
                return v
            names = " ".join(dims)
            return v.rearrange(f"p ({names}) -> p {names}", **dims)

        w_in = [sem(f"weight_tile_in_slot{i}") for i in range(RING)]
        w_used = sem("weight_tiles_used")
        out_sem = sem("outputs_written")
        n_out = [0]

        issued = [0]

        def stream(sp, end):
            n = issued[0]
            while n < end:
                if n >= RING and n + RING <= end:
                    turns = (end - n) // RING
                    with sp.Fori(0, turns) as i:
                        for j in range(RING):
                            m = n + j
                            sp.wait_ge(w_used, i * RING + (m - RING + 1))
                            sp.dma_start(ring[:, m % RING * TILE:(m % RING + 1) * TILE],
                                         wstream[bass.ds(i * RING + m, 1)].rearrange("a p n -> (a p) n")
                                         ).then_inc(w_in[m % RING], 16)
                    n += turns * RING
                    continue
                if n >= RING:
                    sp.wait_ge(w_used, n - RING + 1)
                sp.dma_start(ring[:, n % RING * TILE:(n % RING + 1) * TILE], wstream[n]).then_inc(w_in[n % RING], 16)
                n += 1
            issued[0] = n

        def tile_in(pe, n, i=0):
            pe.wait_ge(w_in[n % RING], i * 16 + 16 * (n // RING + 1))

        def tile(n, **dims):
            names = " ".join(dims)
            return ring[:, n % RING * TILE:(n % RING + 1) * TILE].rearrange(f"p ({names}) -> p {names}", **dims)

        def linear(pe, at, chunks, rhs, ready, freed, rhs_wait=None, last_of=2, first=0):
            if rhs_wait is not None:
                pe.wait_ge(*rhs_wait)
            for m in chunks:
                n = at + m // 2
                if m % 2 == 0:
                    tile_in(pe, n)
                if m - first >= 8:
                    pe.wait_ge(freed, m - 7)
                w = tile(n, k=KC, c=256)
                for k in range(KC):
                    mm = pe.matmul(bank(m % 8), w[:, k, m % 2 * P:m % 2 * P + P], rhs[:, k, :],
                                   start=k == 0, stop=k == KC - 1)
                mm.then_inc(ready, 1)
                if m % 2 == 1:
                    pe.wait_ge(ready, m + 1)
                    pe.sem_inc(w_used, 1)

        s_small, s_state = sem("small_inputs_in"), sem("x_in")
        s_cond, s_ada, s_ada_ev = sem("cond_silu_ready"), sem("ada_products_ready"), sem("ada_chunks_stored")
        s_dve, s_act, s_pool = sem("dve_order"), sem("act_order"), sem("pool_order")
        dve_o, act_o = Order(nc.vector, s_dve), Order(nc.scalar, s_act)
        SC = area(0, 2 * KC, k=KC, c=2)
        ROWS = area(2 * KC, N_ADA * 256)
        with nc.Block() as block:
            @block.sync
            def _(sp):
                stream(sp, AT_IN + RING)

            @block.scalar
            def _(act):
                act.dma_start(V[:, :], vec).then_inc(s_small, 16)
                act.dma_start(C[:, :], cst).then_inc(s_small, 16)
                act.dma_start(SINK[:, :], sinkr.partition_broadcast(P)).then_inc(s_small, 16)
                act.dma_start(XT_[:, :], xT).then_inc(s_state, 16)
                act.wait_ge(s_small, 48)
                act.activation(SC, V[:, V_COND:V_COND + 2 * KC].rearrange("p (k c) -> p k c", c=2),
                               ACT.Silu).then_inc(s_cond, 1)
                act.wait_ge(s_state, 16)

                with act.Fori(0, N_ADA // RING) as i:
                    for b in range(RING // 2):
                        act.wait_ge(w_used, i * RING + (2 * b + 2))
                        act.activation(ROWS[0:2, bass.ds(i * (RING * 256) + b * 512, 512)], bank(b, 512)[0:2],
                                       ACT.Copy).then_inc(s_ada_ev, 1)

            @block.tensor
            def _(pe):
                pe.wait_ge(s_cond, 1)
                with pe.Fori(0, N_ADA // RING) as i:
                    for j in range(RING):
                        if j % 2 == 0:
                            pe.wait_ge(s_ada_ev, i * (RING // 2) + (j // 2 + 1))
                        tile_in(pe, j, i)
                        w = tile(j, k=KC, c=256)
                        for k in range(KC):
                            mm = pe.matmul(bank(j // 2, 256, j % 2 * 256)[0:2], SC[:, k, :], w[:, k, :],
                                           start=k == 0, stop=k == KC - 1)
                        mm.then_inc(w_used, 1)
                pe.wait_ge(s_ada_ev, N_ADA // 2 + RING // 2)
                for m in range(2 * MC):
                    mm = pe.transpose(bank(4, 2, 2 * m), ROWS[0:2, P * m:P * m + P], ident[0:2, 0:2])
                mm.then_inc(s_ada, 1)

            @block.vector
            def _(dve):
                dve.wait_ge(s_small, 48)
                dve.sem_inc(s_ada_ev, RING // 2)
                dve.wait_ge(s_ada, 1)
                b = V[:, V_ADA_B:V_ADA_B + 2 * MC].unsqueeze(2).broadcast_to([P, 2 * MC, 2])
                dve_o(dve.tensor_tensor(MOD[:, :].rearrange("p (m c) -> p m c", c=2),
                                        bank(4, 4 * MC).rearrange("p (m c) -> p m c", c=2), b, ALU.add))
                for l in range(2):
                    for w, vn in ((0, V_NMIX), (1, V_NFFN)):
                        nw = V[:, vn + l * KC:vn + (l + 1) * KC].unsqueeze(2).broadcast_to([P, KC, 2])
                        last = dve.scalar_tensor_tensor(out=gain[:, l, w], in0=mod[:, l, 3 * w + 1], scalar=1.0,
                                                        in1=nw, op0=ALU.add, op1=ALU.mult)
                        dve_o(last)

        s_sq, s_ss, s_var, s_sd, s_rs, s_xn = (sem("squares_ready"), sem("square_sums_ready"), sem("variance_ready"),
                                               sem("std_ready"), sem("rstd_ready"), sem("normalised_ready"))
        norms = [0]

        def norm_block(l, w, end, save=None):
            n = norms[0]
            norms[0] += 1
            RS, VAR = area(0, T), area(T, T)
            with nc.Block() as block:
                @block.sync
                def _(sp):
                    stream(sp, end)

                @block.scalar
                def _(act):
                    act.activation(HT_[:, :], XT_[:, :], ACT.Square).then_inc(s_sq, 1)
                    act.wait_ge(s_var, n + 1)
                    act.activation(VAR, VAR, ACT.Sqrt).then_inc(s_sd, 1)
                    for k in range(KC):
                        act.wait_ge(s_xn, n * KC + k + 1)
                        if l is None:
                            act_o(act.activation(HT[:, k, :], HT[:, k, :], ACT.Copy,
                                                 scale=V[:, V_NOUT + k:V_NOUT + k + 1]))
                            continue
                        for c, a, b in STREAMS:
                            act_o.inc(act.activation(HT[:, k, a:b], HT[:, k, a:b], ACT.Identity,
                                                     bias=mod[:, l, 3 * w, k, c:c + 1],
                                                     scale=gain[:, l, w, k, c:c + 1]))
                    act_o.wait()
                    if l is None:
                        act.dma_start(yT, HT_[:, :]).then_inc(out_sem, 16)
                        n_out[0] += 16
                        act.wait_ge(out_sem, n_out[0])

                @block.tensor
                def _(pe):
                    pe.wait_ge(s_sq, n + 1)
                    for k in range(KC):
                        mm = pe.matmul(bank(0), ones, HT[:, k, :], start=k == 0, stop=k == KC - 1)
                    mm.then_inc(s_ss, 1)

                @block.vector
                def _(dve):
                    dve.wait_ge(s_ss, n + 1)
                    dve.tensor_scalar(VAR, bank(0), 1.0 / D, EPS, ALU.mult, ALU.add).then_inc(s_var, 1)
                    dve.wait_ge(s_sd, n + 1)
                    dve_o(dve.reciprocal(RS, VAR))
                    for k in range(KC):
                        dve.tensor_tensor(HT[:, k, :], XT[:, k, :], RS, ALU.mult).then_inc(s_xn, 1)

        norm_block(0, 0, AT_IN + RING)

        a_ = [0]

        def take(words):
            a_[0] += words
            return a_[0] - words

        QG = area(take(2 * T), 2 * T, c=2, t=T)
        KG = area(take(2 * T), 2 * T, c=2, t=T)
        GVT = area(take(4 * T), 4 * T, h=4, t=T)
        SG = area(take(4 * T), 4 * T, h=4, t=T)
        at_aq = take(8 * T)
        AQK = area(at_aq, 8 * T, h=8, t=T)
        AK = area(take(2 * T), 2 * T, h=2, t=T)
        AVT = area(take(T), T)
        LRT = area(take(T), T)
        VR = area(take(T), T, a=3, d=P)
        GVR = area(take(2 * NCH * GV), 2 * NCH * GV, r=2, n=NCH, v=GV)
        LD = area(take(4 * T), 4 * T, r=2, d=2, t=T)
        CK = area(take(2 * P), 2 * P, h=2, t=P)
        CV = area(take(P), P, h=2, e=HD)
        DEC = area(take(4 * P), 4 * P)
        at_tmp = a_[0]
        OT = HT
        s_in, s_in_ev, s_side = sem("projection_ready"), sem("projection_stored"), sem("side_inputs_in")
        with nc.Block() as block:
            @block.sync
            def _(sp):
                sp.dma_start(CK[0:HD], ckT).then_inc(s_side, 16)
                sp.dma_start(CV, cv).then_inc(s_side, 16)
                sp.dma_start(DEC[0:2 * LR, :], dec2).then_inc(s_side, 16)
                stream(sp, AT_OUT + N_OUT)
                sp.wait_ge(s_side, 48)

            @block.tensor
            def _(pe):
                linear(pe, AT_IN, range(18), HT, s_in, s_in_ev)
                tile_in(pe, AT_IN + 9)
                pe.wait_ge(s_in_ev, 11)
                w = tile(AT_IN + 9, k=KC, c=256)
                for k in range(KC):
                    mm = pe.matmul(bank(2)[0:2 * LR, :], w[:, k, 0:2 * LR], HT[:, k, :], start=k == 0, stop=k == KC - 1)
                mm.then_inc(s_in, 1)
                pe.wait_ge(s_in, 19)
                pe.sem_inc(w_used, 1)

            @block.scalar
            def _(act):
                for m in range(19):
                    act.wait_ge(s_in, m + 1)
                    o = bank(m % 8)
                    if m < 2:
                        last = act.activation(QG[:, m, :], o, ACT.Copy, scale=HD ** -0.5)
                    elif m < 4:
                        last = act.activation(KG[:, m - 2, :], o, ACT.Copy)
                    elif m < 8:
                        last = act.activation(GVT[:, m - 4, :], o, ACT.Copy)
                    elif m < 12:
                        last = act.activation(SG[:, m - 8, :], o, ACT.Silu)
                    elif m < 16:
                        h = 2 * (m - 12)
                        act.activation(AQK[0:HD, h, :], o[0:HD], ACT.Copy, scale=HD ** -0.5)
                        last = act.activation(AQK[0:HD, h + 1, :], o[HD:P], ACT.Copy, scale=HD ** -0.5)
                    elif m == 16:
                        act.activation(AK[0:HD, 0, :], o[0:HD], ACT.Copy)
                        last = act.activation(AK[0:HD, 1, :], o[HD:P], ACT.Copy)
                    elif m == 17:
                        last = act.activation(AVT, o, ACT.Copy)
                    else:
                        last = act.activation(LRT[0:2 * LR, :], o[0:2 * LR], ACT.Copy)
                    last.then_inc(s_in_ev, 1)

        ROT = area(at_tmp, 10 * LAT, h=10, t=LAT)
        Z_ = area(at_tmp + 10 * LAT, 4 * T, r=2, d=2, t=T)
        E_ = area(at_tmp + 10 * LAT + 4 * T, 4 * T, r=2, d=2, t=T)
        assert at_tmp + 10 * LAT + 8 * T <= 30880
        s_rows, s_ldp, s_rope, s_free = sem("value_rows_ready"), sem("decay_products_ready"), sem("rotated_ready"), sem("rope_banks_read")
        s_z, s_l = sem("decay_argument_ready"), sem("decay_log_ready")
        with nc.Block() as block:
            @block.scalar
            def _(act):
                act.dma_start(kT_out, AK[0:HD, :, 0:CTX]).then_inc(out_sem, 16)
                act.dma_start(vT_out, AVT[:, 0:CTX]).then_inc(out_sem, 16)
                n_out[0] += 32
                for r in range(2):
                    act.wait_ge(s_rows, r + 1)
                    act_o.inc(act.activation(GVR[:, r], ps[:, 1024 * r:1024 * r + NCH * GV].rearrange(
                        "p (n v) -> p n v", v=GV), ACT.Copy))
                act.wait_ge(s_rows, 3)
                act_o(act.activation(VR, bank(4).rearrange("p (a d) -> p a d", d=P), ACT.Copy))
                act.sem_inc(s_free, 1)
                for r in range(2):
                    for d in range(2):
                        u = 2 * r + d
                        act.wait_ge(s_ldp, u + 1)
                        o = bank(5 + u) if u < 3 else bank(4)
                        act_o.inc(act.activation(Z_[:, r, d, :], o, ACT.Identity,
                                                 bias=V[:, V_DECB + u:V_DECB + u + 1]))
                        if u == 0:
                            act_o.wait()
                            act.sem_inc(s_free, 1)
                act_o.wait()
                act.sem_inc(s_z, 1)
                zf, ef = Z_.rearrange("p r d t -> p (r d t)"), E_.rearrange("p r d t -> p (r d t)")
                act_o(act.activation(ef, zf, ACT.Abs))
                act_o(act.activation(ef, ef, ACT.Exp, scale=-1.0))
                act.activation(ef, ef, ACT.Ln, bias=1.0).then_inc(s_l, 1)

            @block.tensor
            def _(pe):
                for r in range(2):
                    for n in range(NCH):
                        for hp in range(2):
                            mm = pe.matmul(ps[HD * hp:HD * hp + HD, 1024 * r + GV * n:1024 * r + GV * (n + 1)],
                                           GVT[:, 2 * r + hp, CH * n:CH * (n + 1)], ident, start=True, stop=True)
                    mm.then_inc(s_rows, 1)
                for a in range(3):
                    mm = pe.matmul(bank(4, P, P * a), AVT[:, P * a:P * a + P], ident, start=True, stop=True)
                mm.then_inc(s_rows, 1)
                for u in range(4):
                    if u == 3:
                        pe.wait_ge(s_free, 1)
                    r, d = divmod(u, 2)
                    pe.matmul(bank(5 + u) if u < 3 else bank(4), DEC[0:2 * LR, 256 * d + P * r:256 * d + P * r + P],
                              LRT[0:2 * LR, :], start=True, stop=True).then_inc(s_ldp, 1)
                for h in range(10):
                    if h == 8:
                        pe.wait_ge(s_free, 2)
                    src = AQK[0:HD, h, CTX:T] if h < 8 else AK[0:HD, h - 8, CTX:T]
                    b = h // 2 if h < 8 else 5
                    mm = pe.matmul(bank(b, LAT, LAT * (h % 2))[0:HD], C[0:HD, C_PERM:C_PERM + HD], src,
                                   start=True, stop=True)
                    mm.then_inc(s_rope, 1)

            @block.gpsimd
            def _(pool):
                pass

            @block.vector
            def _(dve):
                cos = C[0:HD, C_COS:C_COS + LAT]
                sin = C[0:HD, C_SIN:C_SIN + LAT]
                for h in range(10):
                    dve.wait_ge(s_rope, h // 2 * 2 + 2)
                    b = h // 2 if h < 8 else 5
                    x = AQK[0:HD, h, CTX:T] if h < 8 else AK[0:HD, h - 8, CTX:T]
                    dve.tensor_tensor(ROT[0:HD, h, :], bank(b, LAT, LAT * (h % 2))[0:HD], sin, ALU.mult)
                    dve_o(dve.tensor_tensor(x, x, cos, ALU.mult))
                    dve_o.inc(dve.tensor_tensor(x, x, ROT[0:HD, h, :], ALU.add))
                dve_o.wait()
                dve.wait_ge(s_l, 1)
                zf, ef, lf = (v.rearrange("p r d t -> p (r d t)") for v in (Z_, E_, LD))
                dve_o(dve.tensor_scalar(zf, zf, 0.0, 1.0 / 16.0, ALU.min, ALU.mult))
                dve_o(dve.scalar_tensor_tensor(out=lf, in0=ef, scalar=-1.0 / 16.0, in1=zf,
                                               op0=ALU.mult, op1=ALU.add))

        units = [(h, -1) for h in range(AH)] + [(h, b) for h in range(AH) for b in range(2)]
        NU = len(units)
        S = area(at_tmp, 3 * T, b=3, t=T)
        PR = area(at_tmp + 3 * T, 2 * T, b=2, t=T)
        PTR = area(at_tmp + 5 * T, 2 * T, b=2, t=T)
        ST = area(at_tmp + 7 * T, 8 * NU, u=NU, v=8)
        s_sc, s_scr, s_nm, s_p, s_pn = (sem("scores_ready"), sem("scores_read"), sem("row_max_ready"), sem("probs_ready"),
                                        sem("probs_normalised"))
        s_pt, s_ptc, s_ao, s_aoc = sem("probs_turned"), sem("turned_probs_stored"), sem("attention_ready"), sem("attention_stored")
        with nc.Block() as block:
            def keys(b):
                return CTX if b < 0 else T

            @block.tensor
            def _(pe):
                def scores(u):
                    h, b = units[u]
                    kv = h // (AH // AKV)
                    if u >= 3:
                        pe.wait_ge(s_scr, u - 2)
                    if b < 0:
                        mm = pe.matmul(bank(u % 3, CTX), AQK[0:HD, h, 0:CTX], AK[0:HD, kv, 0:CTX], start=True, stop=True)
                    else:
                        q = AQK[0:HD, h, CTX + P * b:CTX + P * b + P]
                        pe.matmul(bank(u % 3, P), q, CK[0:HD, kv, :], start=True, stop=True)
                        mm = pe.matmul(bank(u % 3, LAT, P), q, AK[0:HD, kv, CTX:T], start=True, stop=True)
                    mm.then_inc(s_sc, 1)

                def turn(u):
                    pe.wait_ge(s_pn, u + 1)
                    if u >= 2:
                        pe.wait_ge(s_ptc, u - 1)
                    for a in range(keys(units[u][1]) // P):
                        mm = pe.transpose(bank(3 + u % 2, P, P * a), PR[:, u % 2, P * a:P * a + P], ident)
                    mm.then_inc(s_pt, 1)

                def mix(u):
                    h, b = units[u]
                    kv = h // (AH // AKV)
                    pe.wait_ge(s_ptc, u + 1)
                    if u >= 2:
                        pe.wait_ge(s_aoc, u - 1)
                    vs = [VR[:, 0, HD * kv:HD * kv + HD]] if b < 0 else \
                        [CV[:, kv, :], VR[:, 1, HD * kv:HD * kv + HD], VR[:, 2, HD * kv:HD * kv + HD]]
                    o = bank(5 + u % 2, P)[HD * (h % 2):HD * (h % 2) + HD]
                    for a, v in enumerate(vs):
                        mm = pe.matmul(o, v, PTR[:, u % 2, P * a:P * a + P], start=a == 0, stop=a == len(vs) - 1)
                    mm.then_inc(s_ao, 1)

                scores(0)
                for u in range(NU):
                    if u + 1 < NU:
                        scores(u + 1)
                    turn(u)
                    if u >= 1:
                        mix(u - 1)
                mix(NU - 1)

            @block.scalar
            def _(act):
                def exps(u):
                    h, b = units[u]
                    n = keys(b)
                    act.wait_ge(s_nm, u + 1)
                    if u >= 2:
                        act.wait_ge(s_pt, u - 1)
                    act.activation(ST[:, u, 3:4], SINK[:, h:h + 1], ACT.Exp, bias=ST[:, u, 1:2])
                    act.activation(PR[:, u % 2, 0:n], S[:, u % 3, 0:n], ACT.Exp, bias=ST[:, u, 1:2],
                                   accum_out=ST[:, u, 2:3]).then_inc(s_p, 1)

                def store_turned(u):
                    n = keys(units[u][1])
                    act.wait_ge(s_pt, u + 1)
                    if u >= 2:
                        act.wait_ge(s_ao, u - 1)
                    act.activation(PTR[:, u % 2, 0:n], bank(3 + u % 2, n), ACT.Copy).then_inc(s_ptc, 1)

                def store_out(u):
                    h, b = units[u]
                    act.wait_ge(s_ao, u + 1)
                    p0, t0 = HD * (h % 2), 0 if b < 0 else CTX + P * b
                    act.activation(OT[p0:p0 + HD, 4 + h // 2, t0:t0 + P], bank(5 + u % 2, P)[p0:p0 + HD],
                                   ACT.Copy).then_inc(s_aoc, 1)

                for u in range(NU + 2):
                    if u < NU:
                        exps(u)
                    if 1 <= u <= NU:
                        store_turned(u - 1)
                    if u >= 2:
                        store_out(u - 2)

            @block.vector
            def _(dve):
                def front(u):
                    h, b = units[u]
                    n = keys(b)
                    dve.wait_ge(s_sc, u + 1)
                    if u >= 3:
                        dve.wait_ge(s_p, u - 2)
                    if b < 0:
                        dve.tensor_copy(S[:, u % 3, 0:n], bank(u % 3, n)).then_inc(s_scr, 1)
                    else:
                        dve.tensor_tensor(S[:, u % 3, :], bank(u % 3), C[:, C_MASK + T * b:C_MASK + T * (b + 1)],
                                          ALU.add).then_inc(s_scr, 1)
                    dve.wait_ge(s_scr, u + 1)
                    dve_o(dve.reduce_max(ST[:, u, 0:1], S[:, u % 3, 0:n], AX))
                    dve.tensor_scalar(ST[:, u, 1:2], ST[:, u, 0:1], SINK[:, h:h + 1], -1.0,
                                      ALU.max, ALU.mult).then_inc(s_nm, 1)

                def back(u):
                    n = keys(units[u][1])
                    dve.wait_ge(s_p, u + 1)
                    dve_o(dve.tensor_tensor(ST[:, u, 4:5], ST[:, u, 2:3], ST[:, u, 3:4], ALU.add))
                    dve_o(dve.reciprocal(ST[:, u, 5:6], ST[:, u, 4:5]))
                    dve.tensor_scalar(PR[:, u % 2, 0:n], PR[:, u % 2, 0:n], ST[:, u, 5:6], None,
                                      ALU.mult).then_inc(s_pn, 1)

                front(0)
                for u in range(NU):
                    if u + 1 < NU:
                        front(u + 1)
                    back(u)

        a_[0] = at_aq
        B = area(take(4 * T), 4 * T, r=2, d=2, t=T)
        QE = area(take(4 * T), 4 * T, r=2, d=2, t=T)
        assert a_[0] <= at_aq + 8 * T
        a_[0] = at_tmp
        KN = area(take(4 * T), 4 * T, r=2, d=2, t=T)
        KD = area(take(4 * T), 4 * T, r=2, d=2, t=T)
        KDR = area(take(4 * T), 4 * T, r=2, d=2, n=NCH, k=HD)
        AT = area(take(4 * T), 4 * T, r=2, d=2, n=NCH, k=CH)
        TOT = area(take(4 * NCH), 4 * NCH, r=2, d=2, n=NCH)
        EBT = area(take(4 * NCH), 4 * NCH, r=2, d=2, n=NCH)
        ZG = area(take(8 * GV), 8 * GV, r=2, a=4, v=GV)
        OF = area(take(8 * T), 8 * T, d=2, h=4, t=T)
        assert a_[0] <= 30880
        LANES = ((0, (2, 3, 4, 5)), (1, (5, 4, 3, 2)), (0, (0, 1)), (1, (1, 0)))

        def lanes_at(s):
            return [(a, d, n[s]) for a, (d, n) in enumerate(LANES) if s < len(n)]

        s_tot, s_b, s_e, s_qk, s_am, s_ams, s_zin = (
            sem("gla_totals_ready"), sem("gla_cumulated_ready"), sem("gla_exps_ready"), sem("gla_operands_ready"),
            sem("gla_matrices_ready"), sem("gla_matrices_stored"), sem("gla_state_in"))
        s_go, s_gz, s_goc, s_gzc = (sem("gla_chunk_ready"), sem("gla_state_products_ready"), sem("gla_chunk_stored"),
                                    sem("gla_state_updated"))
        with nc.Block() as block:
            def flat(v):
                return v.rearrange("p r d t -> p (r d t)")

            @block.sync
            def _(sp):
                for r in range(2):
                    sp.dma_start(ZG[:, r, 0:2], zgla[r]).then_inc(s_zin, 16)
                sp.wait_ge(s_zin, 32)

            @block.vector
            def _(dve):
                dve_o.inc(dve.memset(ZG[:, :, 2:4], 0.0))
                for r in range(2):
                    for d in range(2):
                        dve_o.inc(dve.tensor_tensor_scan(B[:, r, d, :], C[:, C_KEEP:C_KEEP + T], LD[:, r, d, :], 0.0,
                                                         ALU.mult, ALU.add))
                dve_o.wait()
                Bc = B.rearrange("p r d (n i) -> p r d n i", i=CH)
                for r in range(2):
                    dve_o.inc(dve.tensor_copy(TOT[:, r], Bc[:, r, :, :, CH - 1]))
                dve_o.wait()
                dve.sem_inc(s_tot, 1)
                for r in range(2):
                    dve_o(dve.scalar_tensor_tensor(out=B[:, r, 1, :], in0=B[:, r, 1, :], scalar=-1.0,
                                                   in1=LD[:, r, 1, :], op0=ALU.mult, op1=ALU.add))
                    dve_o.inc(dve.tensor_tensor(Bc[:, r, 1], Bc[:, r, 1],
                                                TOT[:, r, 1].unsqueeze(2).broadcast_to([P, NCH, CH]), ALU.add))
                dve_o.wait()
                for r in range(2):
                    kd = KD[:, r].rearrange("p d (n i) -> p d n i", i=CH)
                    dve_o.inc(dve.scalar_tensor_tensor(
                        out=KD[:, r].rearrange("p d (n i) -> p (d n) i", i=CH),
                        in0=B[:, r].rearrange("p d (n i) -> p (d n) i", i=CH), scalar=-1.0,
                        in1=TOT[:, r].rearrange("p d n -> p (d n)").unsqueeze(2).broadcast_to([P, 2 * NCH, CH]),
                        op0=ALU.mult, op1=ALU.add))
                dve_o.wait()
                dve.sem_inc(s_b, 1)
                dve.wait_ge(s_e, 1)
                for dst, src in ((QE, QG), (KN, KG), (KD, KG)):
                    for r in range(2):
                        dve_o.inc(dve.tensor_tensor(dst[:, r], dst[:, r], src[:, r].unsqueeze(1).broadcast_to([P, 2, T]),
                                                    ALU.mult))
                dve_o.wait()
                dve.sem_inc(s_qk, 1)
                for r in range(2):
                    dve.wait_ge(s_am, r + 1)
                    m = C[:, C_INCL:C_INCL + 2 * CH].rearrange("p (d i) -> p d i", d=2).unsqueeze(2)
                    dve.tensor_tensor(AT[:, r], ps[:, 1024 * r:1024 * r + 2 * T].rearrange("p (d n i) -> p d n i", d=2, n=NCH),
                                      m.broadcast_to([P, 2, NCH, CH]), ALU.mult).then_inc(s_ams, 1)
                    dve.tensor_copy(KDR[:, r], ps[:, 2048 + 1024 * r:2048 + 1024 * r + 2 * T].rearrange(
                        "p (d n i) -> p d n i", d=2, n=NCH)).then_inc(s_ams, 1)
                for s in range(4):
                    dve.wait_ge(s_gz, s + 1)
                    for r in range(2):
                        for a, d, n in lanes_at(s):
                            z = bank(2 + r, GV, a * GV)
                            dve_o.inc(dve.scalar_tensor_tensor(out=ZG[:, r, a], in0=ZG[:, r, a],
                                                               scalar=EBT[:, r, d, n:n + 1], in1=z,
                                                               op0=ALU.mult, op1=ALU.add))
                    dve_o.wait()
                    dve.sem_inc(s_gzc, 1)

            @block.scalar
            def _(act):
                act.wait_ge(s_tot, 1)
                act.activation(EBT.rearrange("p r d n -> p (r d n)"), TOT.rearrange("p r d n -> p (r d n)"), ACT.Exp)
                act.wait_ge(s_b, 1)
                act.activation(flat(QE), flat(B), ACT.Exp)
                act.activation(flat(KN), flat(B), ACT.Exp, scale=-1.0)
                act_o(act.activation(flat(KD), flat(KD), ACT.Exp))
                act.sem_inc(s_e, 1)
                for s in range(4):
                    act.wait_ge(s_go, s + 1)
                    for a, d, n in lanes_at(s):
                        src = ps[:, 0:1024].rearrange("p (x r a i) -> p r x a i", x=2, r=2, a=4)[:, :, :, a, :]
                        dst = OF[:, d].rearrange("p (r x) t -> p r x t", r=2)[:, :, :, CH * n:CH * n + CH]
                        act_o.inc(act.activation(dst, src, ACT.Copy))
                    act_o.wait()
                    act.sem_inc(s_goc, 1)
                act.wait_ge(s_gzc, 4)
                for r in range(2):
                    act.dma_start(gla_out[r], ZG[:, r, 2:4]).then_inc(out_sem, 16)
                n_out[0] += 32
                act.wait_ge(out_sem, n_out[0])

            @block.tensor
            def _(pe):
                pe.wait_ge(s_qk, 1)
                for r in range(2):
                    for which in range(2):
                        for d in range(2):
                            for n in range(NCH):
                                for hp in range(2):
                                    h = slice(HD * hp, HD * hp + HD)
                                    i = slice(CH * n, CH * n + CH)
                                    c = 1024 * r + 2048 * which + T * d + CH * n
                                    o = ps[h, c:c + CH]
                                    if which == 0:
                                        mm = pe.matmul(o, KN[h, r, d, i], QE[h, r, d, i], start=True, stop=True)
                                    else:
                                        mm = pe.matmul(o, KD[h, r, d, i], C[h, C_I64:C_I64 + CH], start=True, stop=True)
                    mm.then_inc(s_am, 1)
                pe.wait_ge(s_ams, 4)
                pe.wait_ge(s_zin, 32)
                for s in range(4):
                    if s:
                        pe.wait_ge(s_gzc, s)
                        pe.wait_ge(s_goc, s)
                    for r in range(2):
                        for hp in range(2):
                            h = slice(HD * hp, HD * hp + HD)
                            for a, d, n in lanes_at(s):
                                c = ((2 * hp + r) * 4 + a) * CH
                                o = ps[:, c:c + CH]
                                pe.matmul(o, ZG[h, r, a], QE[h, r, d, CH * n:CH * n + CH], start=True, stop=False)
                                mm = pe.matmul(o, GVR[h, r, n], AT[h, r, d, n], start=False, stop=True)
                    mm.then_inc(s_go, 1)
                    for r in range(2):
                        for hp in range(2):
                            h = slice(HD * hp, HD * hp + HD)
                            for a, d, n in lanes_at(s):
                                mm = pe.matmul(bank(2 + r, GV, a * GV)[h], KDR[h, r, d, n], GVR[h, r, n],
                                               start=True, stop=True)
                    mm.then_inc(s_gz, 1)

        s_go2, s_gsq, s_gss, s_gv, s_gsd = (sem("gla_sum_ready"), sem("gla_squares_ready"), sem("gla_square_sums_ready"),
                                            sem("gla_variance_ready"), sem("gla_std_ready"))
        O4 = area(at_aq, 4 * T)
        SQ4 = area(at_aq + 4 * T, 4 * T)
        with nc.Block() as block:
            @block.vector
            def _(dve):
                dve_o(dve.tensor_tensor(O4, OF[:, 0].rearrange("p h t -> p (h t)"), OF[:, 1].rearrange("p h t -> p (h t)"),
                                        ALU.add))
                dve.sem_inc(s_go2, 1)
                dve.wait_ge(s_gss, 1)
                dve.tensor_scalar(SQ4.rearrange("p (h t) -> p h t", h=4),
                                  ps[:, 0:2048].rearrange("p (h t) -> p h t", h=4)[:, :, 0:T],
                                  1.0 / GV, EPS, ALU.mult, ALU.add).then_inc(s_gv, 1)
                dve.wait_ge(s_gsd, 1)
                dve_o(dve.reciprocal(SQ4, SQ4))
                dve_o(dve.scalar_tensor_tensor(out=SQ4, in0=SQ4, scalar=V[:, V_GNORM:V_GNORM + 1], in1=O4,
                                               op0=ALU.mult, op1=ALU.mult))
                dve_o(dve.tensor_tensor(OT[:, 0:4].rearrange("p h t -> p (h t)"), SQ4, SG.rearrange("p h t -> p (h t)"),
                                        ALU.mult))

            @block.scalar
            def _(act):
                act.wait_ge(s_go2, 1)
                act.activation(SQ4, O4, ACT.Square).then_inc(s_gsq, 1)
                act.wait_ge(s_gv, 1)
                act.activation(SQ4, SQ4, ACT.Sqrt).then_inc(s_gsd, 1)

            @block.tensor
            def _(pe):
                pe.wait_ge(s_gsq, 1)
                for h in range(4):
                    mm = pe.matmul(bank(h), ones, SQ4[:, T * h:T * h + T], start=True, stop=True)
                mm.then_inc(s_gss, 1)

        def out_block(l, at, src, end, name):
            s_o, s_oc = sem(name + "_ready"), sem(name + "_added")
            with nc.Block() as block:
                @block.sync
                def _(sp):
                    stream(sp, end)

                @block.tensor
                def _(pe):
                    linear(pe, at, range(8), src, s_o, s_oc)

                @block.vector
                def _(dve):
                    for m in range(KC):
                        dve.wait_ge(s_o, m + 1)
                        for c, a, b in STREAMS:
                            last = dve.scalar_tensor_tensor(out=XT[:, m, a:b], in0=bank(m)[:, a:b],
                                                            scalar=mod[:, l, 2, m, c:c + 1], in1=XT[:, m, a:b],
                                                            op0=ALU.mult, op1=ALU.add)
                        last.then_inc(s_oc, 1)

        out_block(0, AT_OUT, OT, AT_OUT + N_OUT + RING, "mixer0_out")

        def moe_block(l, at, end):
            tag = f"moe{l}_"
            m0 = 2 * T
            ACC = area(m0, KC * T, k=KC, t=T)
            r0 = m0 + KC * T
            WR = area(r0, KC * 20, k=KC, e=20)
            BR = area(r0 + 160, 20)
            LG = area(r0 + 180, 60, a=3, e=20)
            RW = area(r0 + 240, 3 * 64, a=3, e=64)
            MK = area(r0 + 432, 3 * NE, a=3, e=NE)
            RKM = area(r0 + 480, 3 * (NE + 1), a=3, e=NE + 1)
            CNT = area(r0 + 531, 1)
            CNTI = A[:, r0 + 532:r0 + 533].bitcast(I32)
            RC = area(r0 + 533, CAP + P)
            b0 = r0 + 533 + CAP + P
            IOTA, BEFORE = RC[:, 0:CAP], RC[:, CAP:CAP + P]
            s_rw, s_lg, s_m, s_ex, s_mk, s_rk, s_gu, s_silu, s_hid, s_dn, s_acc, s_ord = (sem(tag + n) for n in (
                "router_weights_in", "logits_ready", "router_max_ready", "router_exps_ready", "assignment_ready",
                "ranks_ready", "gate_up_ready", "silu_ready", "hidden_ready", "products_to_add_ready", "products_added",
                "dve_order"))
            GATES = RW[:, :, 0:16]
            with nc.Block() as block:
                @block.sync
                def _(sp):
                    sp.dma_start(WR, wrt[l]).then_inc(s_rw, 16)
                    sp.dma_start(BR, brt[l].partition_broadcast(P)).then_inc(s_rw, 16)
                    sp.dma_start(RC, rcst).then_inc(s_rw, 16)
                    sp.wait_ge(s_rw, 48)

                @block.tensor
                def _(pe):
                    pe.wait_ge(s_rw, 48)
                    for a in range(3):
                        for k in range(KC):
                            mm = pe.matmul(bank(0, 20, 20 * a), HT[:, k, P * a:P * a + P], WR[:, k, :],
                                           start=k == 0, stop=k == KC - 1)
                    mm.then_inc(s_lg, 1)
                    pe.wait_ge(s_mk, 1)
                    for a in range(3):
                        for b in range(a + 1):
                            pe.matmul(bank(1, NE, NE * a), ones if b < a else BEFORE, MK[:, b], start=b == 0, stop=b == a)
                    for b in range(3):
                        mm = pe.matmul(bank(1, NE, NE * 3), ones, MK[:, b], start=b == 0, stop=b == 2)
                    mm.then_inc(s_rk, 1)

                @block.scalar
                def _(act):
                    act.wait_ge(s_m, 1)
                    for a in range(3):
                        act_o.inc(act.activation(RW[:, a, 44:48], LG[:, a, 0:4], ACT.Exp, bias=RW[:, a, 40:41],
                                                 accum_out=RW[:, a, 48:49]))
                        act_o.inc(act.activation(RW[:, a, 49:50], RW[:, a, 38:39], ACT.Exp, bias=RW[:, a, 39:40]))
                    act_o.wait()
                    act.sem_inc(s_ex, 1)

                @block.vector
                def _(dve):
                    dve_o.inc(dve.memset(ACC, 0.0))
                    dve_o.inc(dve.memset(RKM, 2.0 * T))
                    dve.wait_ge(s_rw, 48)
                    dve.wait_ge(s_lg, 1)
                    dve_o(dve.tensor_tensor(LG, bank(0, 60).rearrange("p (a e) -> p a e", a=3),
                                            BR.unsqueeze(1).broadcast_to([P, 3, 20]), ALU.add))

                    def first_max(x, one, mx, t):
                        dve_o(dve.tensor_reduce(mx, x, AX, ALU.max))
                        dve_o(dve.tensor_tensor(one, x, mx.broadcast_to([P, 3, 4]), ALU.is_equal))
                        dve_o(dve.tensor_scalar(t, one[:, :, 0:1], -1.0, 1.0, ALU.mult, ALU.add))
                        for j in range(1, 4):
                            dve_o(dve.tensor_tensor(one[:, :, j:j + 1], one[:, :, j:j + 1], t, ALU.mult))
                            if j < 3:
                                dve_o(dve.tensor_tensor(t, t, one[:, :, j:j + 1], ALU.subtract))

                    G = RW[:, :, 16:20]
                    first_max(LG[:, :, 0:4], G, RW[:, :, 50:51], RW[:, :, 51:52])
                    sel = RW[:, :, 20:24]
                    by_group = GATES.rearrange("p a (g j) -> p a g j", g=NG)
                    gb = G.unsqueeze(3).broadcast_to([P, 3, NG, EPG])
                    dve_o(dve.tensor_tensor(by_group, LG[:, :, 4:20].rearrange("p a (g j) -> p a g j", g=NG), gb, ALU.mult))
                    dve_o(dve.tensor_reduce(sel, GATES.rearrange("p a (g j) -> p a j g", g=NG), AX, ALU.add))
                    F1, F2 = RW[:, :, 24:28], RW[:, :, 28:32]
                    first_max(sel, F1, RW[:, :, 52:53], RW[:, :, 51:52])
                    sel2 = RW[:, :, 32:36]
                    dve_o(dve.tensor_scalar(sel2, F1, -3.0e38, None, ALU.mult))
                    dve_o(dve.tensor_tensor(sel2, sel2, sel, ALU.add))
                    first_max(sel2, F2, RW[:, :, 38:39], RW[:, :, 51:52])
                    dve_o(dve.tensor_scalar(RW[:, :, 39:40], RW[:, :, 52:53], -1.0, None, ALU.mult))
                    dve_o(dve.tensor_scalar(RW[:, :, 40:41], RW[:, :, 50:51], -1.0, None, ALU.mult))
                    dve.sem_inc(s_m, 1)
                    dve_o(dve.tensor_tensor(sel2, F1, F2, ALU.add))
                    mk4 = MK.rearrange("p a (g j) -> p a g j", g=NG)
                    dve_o(dve.tensor_tensor(mk4, gb, sel2.unsqueeze(2).broadcast_to([P, 3, NG, EPG]), ALU.mult))
                    dve.sem_inc(s_mk, 1)
                    dve.wait_ge(s_ex, 1)
                    x1, den = RW[:, :, 49:50], RW[:, :, 53:54]
                    dve_o(dve.tensor_scalar(den, x1, 1.0, None, ALU.add))
                    dve_o(dve.tensor_tensor(den, den, RW[:, :, 48:49], ALU.mult))
                    dve_o(dve.reciprocal(RW[:, :, 54:55], den))
                    dve_o(dve.tensor_tensor(RW[:, :, 55:56], RW[:, :, 54:55], x1, ALU.mult))
                    dve_o(dve.tensor_tensor(F1, F1, RW[:, :, 54:55].broadcast_to([P, 3, 4]), ALU.mult))
                    dve_o(dve.tensor_tensor(F2, F2, RW[:, :, 55:56].broadcast_to([P, 3, 4]), ALU.mult))
                    dve_o(dve.tensor_tensor(F1, F1, F2, ALU.add))
                    dve_o(dve.tensor_tensor(by_group, gb, F1.unsqueeze(2).broadcast_to([P, 3, NG, EPG]), ALU.mult))
                    dve.wait_ge(s_rk, 1)
                    dve_o(dve.tensor_reduce(CNT, bank(1, NE, NE * 3), AX, ALU.max))
                    dve_o(dve.tensor_copy(CNTI, CNT))
                    dve_o(dve.scalar_tensor_tensor(out=RKM[:, :, 0:NE], in0=MK, scalar=-2.0 * T,
                                                   in1=bank(1, 3 * NE).rearrange("p (a e) -> p a e", a=3),
                                                   op0=ALU.mult, op1=ALU.add))
                    dve_o(dve.tensor_scalar(RKM[:, :, 0:NE], RKM[:, :, 0:NE], 2.0 * T, None, ALU.add))

            HR = area(b0, 3 * D, a=3, d=D)
            HG = area(b0 + 3 * D, KC * CAP, k=KC, s=CAP)
            o1 = b0 + 3 * D + KC * CAP
            SEL = area(o1, 3 * CAP, a=3, s=CAP)
            SELG = area(o1 + 3 * CAP, 3 * CAP, a=3, s=CAP)
            SGT = area(o1 + 6 * CAP, T)
            HIDG = area(o1 + 6 * CAP + T, 4 * CAP, f=4, s=CAP)
            SLG = area(o1 + 10 * CAP + T, 2 * CAP, b=2, s=CAP)
            OUTR = area(o1 + 12 * CAP + T, D)
            assert o1 + 12 * CAP + T + D <= 30880
            GB = area(b0, NE * T, e=NE, t=T)
            HID = area(b0 + NE * T, 4 * T, f=4, t=T)
            SL = area(b0 + (NE + 4) * T, 2 * T, b=2, t=T)
            GT = area(b0 + (NE + 6) * T, T)
            s_hr, s_sl, s_ga, s_hg, s_tr, s_sgt, s_ou, s_ous = (sem(tag + n) for n in (
                "token_rows_stored", "slots_ready", "gather_ready", "gather_stored", "gates_turned",
                "turned_gates_stored", "expert_out_ready", "expert_out_stored"))

            with nc.Block() as block:
                @block.sync
                def _(sp):
                    stream(sp, end)

                def gathered_pe(pe):
                    for j in range(6):
                        for i in range(4):
                            k = 4 * (j % 2) + i
                            mm = pe.transpose(bank(j, P, P * i), HT[:, k, P * (j // 2):P * (j // 2) + P], ident)
                        if j % 2:
                            mm.then_inc(s_ga, 1)
                    pe.wait_ge(s_hr, 3)

                    def gather():
                        for k in range(KC):
                            for a in range(3):
                                mm = pe.matmul(bank(3 + k // 4, CAP, CAP * (k % 4)), HR[:, a, P * k:P * k + P], SEL[:, a, :],
                                               start=a == 0, stop=a == 2)
                        mm.then_inc(s_ga, 1)

                    def scatter(e):
                        pe.wait_ge(s_ous, e * 2 + 2)
                        pe.wait_ge(s_sgt, e + 1)
                        for m in range(KC):
                            pe.wait_ge(s_acc, e * 8 + (m + 1))
                            pe.matmul(bank(4 + m % 4), OUTR[0:CAP, P * m:P * m + P], SGT[0:CAP, :],
                                      start=True, stop=True).then_inc(s_dn, 1)

                    pe.wait_ge(s_sl, 1)
                    gather()
                    with pe.Fori(0, NE) as e:
                        pe.wait_ge(s_hg, e + 1)
                        for f in range(4):
                            pe.wait_ge(s_hid, e * 4 + (f + 1))
                            for w in range(2):
                                n = at + 2 * (f // 2) + w
                                if f % 2 == 0:
                                    tile_in(pe, n, e)
                                wt = tile(n, k=KC, c=256)
                                for k in range(KC):
                                    mm = pe.matmul(bank(f % 2, CAP, CAP * w), wt[:, k, f % 2 * P:f % 2 * P + P],
                                                   HG[:, k, :], start=k == 0, stop=k == KC - 1)
                            mm.then_inc(s_gu, 1)
                            if f % 2 == 1:
                                pe.wait_ge(s_gu, e * 4 + (f + 1))
                                pe.sem_inc(w_used, 2)
                        scatter(e)
                        pe.wait_ge(s_sl, e + 2)
                        for a in range(3):
                            mm = pe.transpose(bank(2, P, P * a)[0:CAP], SELG[:, a, :], ident)
                        mm.then_inc(s_tr, 1)
                        pe.wait_ge(s_acc, e * 8 + 9)
                        gather()
                        pe.wait_ge(s_hid, e * 4 + 6)
                        pe.wait_ge(s_acc, e * 8 + 12)
                        for j in range(2):
                            n = at + 4 + j
                            tile_in(pe, n, e)
                            wt = tile(n, f=4, c=512)
                            for f in range(4):
                                mm = pe.matmul(bank(6 + j, 512)[0:CAP], HIDG[:, f, :], wt[:, f, :], start=f == 0, stop=f == 3)
                            mm.then_inc(s_ou, 1)
                            pe.wait_ge(s_ou, e * 2 + (j + 1))
                            pe.sem_inc(w_used, 1)
                    scatter(NE)

                def gathered_act(act):
                    for a in range(3):
                        act.wait_ge(s_ga, a + 1)
                        act.activation(HR[:, a, :], ps[:, 1024 * a:1024 * a + 1024], ACT.Copy).then_inc(s_hr, 1)

                    def store_gathered(ready):
                        act.wait_ge(s_ga, ready)
                        act.activation(HG[:, 0:4], bank(3, 4 * CAP).rearrange("p (k s) -> p k s", k=4), ACT.Copy)
                        act.activation(HG[:, 4:8], bank(4, 4 * CAP).rearrange("p (k s) -> p k s", k=4),
                                       ACT.Copy).then_inc(s_hg, 1)

                    store_gathered(4)
                    with act.Fori(0, NE) as e:
                        for f in range(4):
                            act.wait_ge(s_gu, e * 4 + (f + 1))
                            act.wait_ge(s_hid, e * 4 + (f + 1))
                            act.activation(SLG[:, f % 2, :], bank(f % 2, CAP), ACT.Silu).then_inc(s_silu, 1)
                        act.wait_ge(s_tr, e + 1)
                        act.activation(SGT[0:CAP, :], bank(2)[0:CAP], ACT.Copy).then_inc(s_sgt, 1)
                        store_gathered(e + 5)
                        for j in range(2):
                            act.wait_ge(s_ou, e * 2 + (j + 1))
                            act.activation(OUTR[0:CAP, 512 * j:512 * j + 512], bank(6 + j, 512)[0:CAP],
                                           ACT.Copy).then_inc(s_ous, 1)

                def gathered_dve(dve):
                    order = Order(dve, s_ord)
                    order.inc(dve.memset(OUTR, 0.0))
                    order.inc(dve.memset(SGT, 0.0))
                    for a in range(3):
                        order.inc(dve.tensor_scalar(SEL[:, a, :], IOTA, RKM[:, a, 0:1], None, ALU.is_equal))
                    order.wait()
                    dve.sem_inc(s_sl, 1)
                    dve.sem_inc(s_ous, 2)
                    dve.sem_inc(s_sgt, 1)
                    dve.sem_inc(s_hid, 2)
                    dve.sem_inc(s_acc, 4)

                    def add(e):
                        for m in range(KC):
                            dve.wait_ge(s_dn, e * 8 + (m + 1))
                            dve.wait_ge(s_acc, e * 8 + (m + 1))
                            dve.tensor_tensor(ACC[:, m, :], ACC[:, m, :], bank(4 + m % 4), ALU.add).then_inc(s_acc, 1)

                    with dve.Fori(0, NE) as e:
                        order.enter(e, 6)
                        dve.wait_ge(s_ga, e + 4)
                        for a in range(3):
                            order.inc(dve.tensor_scalar(SEL[:, a, :], IOTA, RKM[:, a, bass.ds(e + 1, 1)], None, ALU.is_equal))
                            order.inc(dve.tensor_scalar(SELG[:, a, :], IOTA, RKM[:, a, bass.ds(e, 1)],
                                                        GATES[:, a, bass.ds(e, 1)], ALU.is_equal, ALU.mult))
                        order.wait()
                        dve.sem_inc(s_sl, 1)
                        for f in range(4):
                            dve.wait_ge(s_silu, e * 4 + (f + 1))
                            dve.tensor_tensor(HIDG[:, f, :], SLG[:, f % 2, :], bank(f % 2, CAP, CAP),
                                              ALU.mult).then_inc(s_hid, 1)
                        add(e)
                        order.leave(NE)
                    add(NE)
                    dve.wait_ge(s_acc, 4 + 8 * (NE + 1))

                def general_pe(pe):
                    for a in range(3):
                        mm = pe.transpose(bank(1, P, P * a)[0:NE], GATES[:, a, :], ident)
                    mm.then_inc(s_tr, 1)
                    pe.wait_ge(s_sgt, 1)
                    for e in range(NE):
                        if e >= 4:
                            pe.wait_ge(s_hg, e - 3)
                        pe.matmul(bank(4 + e % 4), ident[0:NE, e:e + 1].broadcast_to([NE, P]), GT[0:NE, :],
                                  start=True, stop=True).then_inc(s_ga, 1)
                    pe.wait_ge(s_hg, NE)
                    with pe.Fori(0, NE) as e:
                        for f in range(4):
                            pe.wait_ge(s_hid, e * 4 + (f + 1))
                            for w in range(2):
                                n = at + 2 * (f // 2) + w
                                if f % 2 == 0:
                                    tile_in(pe, n, e)
                                wt = tile(n, k=KC, c=256)
                                for k in range(KC):
                                    mm = pe.matmul(bank(2 * (f % 2) + w), wt[:, k, f % 2 * P:f % 2 * P + P], HT[:, k, :],
                                                   start=k == 0, stop=k == KC - 1)
                            mm.then_inc(s_gu, 1)
                            if f % 2 == 1:
                                pe.wait_ge(s_gu, e * 4 + (f + 1))
                                pe.sem_inc(w_used, 2)
                        pe.wait_ge(s_hid, e * 4 + 6)
                        for m in range(8):
                            n = at + 4 + m // 4
                            if m % 4 == 0:
                                tile_in(pe, n, e)
                            pe.wait_ge(s_acc, e * 8 + (m + 1))
                            wt = tile(n, f=4, c=512)
                            for f in range(4):
                                mm = pe.matmul(bank(4 + m % 4), wt[:, f, m % 4 * P:m % 4 * P + P], HID[:, f, :],
                                               start=f == 0, stop=f == 3)
                            mm.then_inc(s_dn, 1)
                            if m % 4 == 3:
                                pe.wait_ge(s_dn, e * 8 + (m + 1))
                                pe.sem_inc(w_used, 1)

                def general_act(act):
                    act.wait_ge(s_tr, 1)
                    act.activation(GT[0:NE, :], bank(1)[0:NE], ACT.Copy).then_inc(s_sgt, 1)
                    for e in range(NE):
                        act.wait_ge(s_ga, e + 1)
                        act.activation(GB[:, e, :], bank(4 + e % 4), ACT.Copy).then_inc(s_hg, 1)
                    with act.Fori(0, NE) as e:
                        for f in range(4):
                            act.wait_ge(s_gu, e * 4 + (f + 1))
                            act.wait_ge(s_hid, e * 4 + (f + 1))
                            act.activation(SL[:, f % 2, :], bank(2 * (f % 2)), ACT.Silu).then_inc(s_silu, 1)

                def general_dve(dve):
                    order = Order(dve, s_ord)
                    dve.sem_inc(s_hid, 2)
                    dve.sem_inc(s_acc, 4)
                    dve.wait_ge(s_hg, NE)
                    with dve.Fori(0, NE) as e:
                        order.enter(e, 4)
                        for f in range(4):
                            dve.wait_ge(s_silu, e * 4 + (f + 1))
                            order(dve.tensor_tensor(SL[:, f % 2, :], SL[:, f % 2, :], bank(2 * (f % 2) + 1), ALU.mult))
                            dve.tensor_tensor(HID[:, f, :], SL[:, f % 2, :],
                                              GB[:, bass.ds(e, 1), :].rearrange("p a t -> p (a t)"),
                                              ALU.mult).then_inc(s_hid, 1)
                        order.leave(NE)
                        for m in range(8):
                            dve.wait_ge(s_dn, e * 8 + (m + 1))
                            dve.wait_ge(s_acc, e * 8 + (m + 1))
                            dve.tensor_tensor(ACC[:, m, :], ACC[:, m, :], bank(4 + m % 4), ALU.add).then_inc(s_acc, 1)
                    dve.wait_ge(s_acc, 4 + 8 * NE)

                def by_load(eng, gathered, general):
                    most = eng.value_load(CNTI[0:1, 0:1])
                    with eng.If(most < CAP + 1):
                        gathered(eng)
                    with eng.Else():
                        general(eng)

                @block.tensor
                def _(pe):
                    by_load(pe, gathered_pe, general_pe)

                @block.scalar
                def _(act):
                    by_load(act, gathered_act, general_act)

                @block.vector
                def _(dve):
                    by_load(dve, gathered_dve, general_dve)
                    for m in range(KC):
                        for c, a, b in STREAMS:
                            dve_o.inc(dve.scalar_tensor_tensor(out=XT[:, m, a:b], in0=ACC[:, m, a:b],
                                                               scalar=mod[:, l, 5, m, c:c + 1], in1=XT[:, m, a:b],
                                                               op0=ALU.mult, op1=ALU.add))
                    dve_o.wait()


        norm_block(0, 1, AT_MOE0 + RING)
        moe_block(0, AT_MOE0, AT_RKV + RING)

        norm_block(1, 0, AT_RKV + RING)
        a_[0] = 0
        XX = area(take(KC * T), KC * T, k=KC, t=T)
        XM = [area(take(KC * T), KC * T, k=KC, t=T) for _ in range(2)]
        RT, KT, VT, GG = (area(take(KC * T), KC * T, k=KC, t=T) for _ in range(4))
        LH = area(take(2 * T), 2 * T, d=2, t=T)
        WA2 = area(take(2 * D), 2 * D, d=2, k=KC, c=P)
        GHID = area(take(T), T)
        at_top = a_[0]
        assert at_top <= 30880
        WO_EARLY = 2
        s_xx, s_xm, s_pj, s_pjc, s_wa = (sem("shift_ready"), sem("mixed_input_ready"), sem("rwkv_product_ready"),
                                         sem("rwkv_product_stored"), sem("second_factors_in"))
        with nc.Block() as block:
            MIX = (0, 2, 3, 1, 4, 5)

            @block.sync
            def _(sp):
                sp.dma_start(WA2, wa2).then_inc(s_wa, 16)
                stream(sp, AT_WO + WO_EARLY)
                sp.wait_ge(s_wa, 16)

            @block.vector
            def _(dve):
                for _, a, b in STREAMS:
                    dve_o.inc(dve.tensor_tensor(XX[:, :, a + 1:b - 1], HT[:, :, a:b - 2], HT[:, :, a + 2:b], ALU.add))
                    dve_o.inc(dve.tensor_copy(XX[:, :, a:a + 1], HT[:, :, a + 1:a + 2]))
                    dve_o.inc(dve.tensor_copy(XX[:, :, b - 1:b], HT[:, :, b - 2:b - 1]))
                dve_o.wait()
                dve_o(dve.scalar_tensor_tensor(out=XX.rearrange("p k t -> p (k t)"), in0=XX.rearrange("p k t -> p (k t)"),
                                               scalar=0.5, in1=HT_[:, :], op0=ALU.mult, op1=ALU.subtract))
                done = (0, 0, 8, 16, 24, 26)
                for x, mu in enumerate(MIX):
                    if x >= 2:
                        dve.wait_ge(s_pj, done[x])
                    for k in range(KC):
                        last = dve.scalar_tensor_tensor(out=XM[x % 2][:, k, :], in0=XX[:, k, :],
                                                        scalar=V[:, V_MU + KC * mu + k:V_MU + KC * mu + k + 1],
                                                        in1=HT[:, k, :], op0=ALU.mult, op1=ALU.add)
                        dve_o.inc(last)
                    dve_o.wait()
                    dve.sem_inc(s_xm, 1)

            @block.tensor
            def _(pe):
                for x in range(3):
                    pe.wait_ge(s_xm, x + 1)
                    linear(pe, AT_RKV, range(8 * x, 8 * x + 8), XM[x % 2], s_pj, s_pjc)
                tile_in(pe, AT_LORA)
                w = tile(AT_LORA, k=KC, c=256)
                for x in range(3, 5):
                    pe.wait_ge(s_xm, x + 1)
                    for d in range(2):
                        u = 2 * (x - 3) + d
                        pe.wait_ge(s_pjc, 24 + u - 7)
                        o = bank(u)[HD * (x - 3):HD * (x - 3) + HD]
                        for k in range(KC):
                            mm = pe.matmul(o, w[:, k, HD * u:HD * u + HD], XM[x % 2][:, k, :], start=k == 0, stop=k == KC - 1)
                        mm.then_inc(s_pj, 1)
                pe.wait_ge(s_pj, 28)
                pe.sem_inc(w_used, 1)
                tile_in(pe, AT_GATE)
                pe.wait_ge(s_xm, 6)
                g1 = ring[:, AT_GATE % RING * TILE:AT_GATE % RING * TILE + D].rearrange("p (k c) -> p k c", k=KC)
                g2 = ring[:, AT_GATE % RING * TILE + D:AT_GATE % RING * TILE + 2 * D]
                pe.wait_ge(s_pjc, 21)
                for k in range(KC):
                    mm = pe.matmul(bank(4), g1[:, k, :], XM[1][:, k, :], start=k == 0, stop=k == KC - 1)
                mm.then_inc(s_pj, 1)
                pe.wait_ge(s_pjc, 29)
                for m in range(KC):
                    pe.matmul(bank(m), g2[:, P * m:P * m + P], GHID, start=True, stop=True).then_inc(s_pj, 1)
                pe.wait_ge(s_pj, 37)
                pe.sem_inc(w_used, 1)

            @block.scalar
            def _(act):
                for m in range(37):
                    act.wait_ge(s_pj, m + 1)
                    if m < 24:
                        last = act.activation((RT, KT, VT)[m // 8][:, m % 8, :], bank(m % 8), ACT.Copy)
                    elif m < 26:
                        last = act.activation(LH[0:HD, m - 24, :], bank(m - 24)[0:HD], ACT.Tanh)
                    elif m < 28:
                        last = act.activation(LH[HD:P, m - 26, :], bank(m - 24)[HD:P], ACT.Copy)
                    elif m == 28:
                        last = act.activation(GHID, bank(4), ACT.Sigmoid)
                    else:
                        last = act.activation(GG[:, m - 29, :], bank(m - 29), ACT.Copy)
                    last.then_inc(s_pjc, 1)

        U2 = 2 * T
        low = 3 * KC * T
        a_[0] = 0
        LDF, BF, ALF, RHOF, BEF, KAF, BCF, KCF, KKAF, KDF, ATF, BTF = (area(take(U2), U2) for _ in range(12))
        assert a_[0] <= low
        a_[0] = at_top
        AB, BK = (area(take(2 * U2), 2 * U2, g=2, d=2, n=NCH, i=CH) for _ in range(2))
        RKV = area(take(3 * T), 3 * T, x=3, t=T)
        PV = area(take(PAIR_VECS), PAIR_VECS)
        LNV = area(take(2), 2)
        W2C = area(take(2 * P), 2 * P, d=2, c=P)
        KK = area(take(T), T)
        TW = area(take(2 * NCH), 2 * NCH, d=2, n=NCH)
        EW = area(take(2 * NCH), 2 * NCH, d=2, n=NCH)
        EWC = area(take(2 * NCH), 2 * NCH)
        ZF = area(take(2 * HD), 2 * HD, d=2, v=HD)
        BON = GHID
        assert a_[0] <= 30880, a_[0]
        spare = (AT_WO + WO_EARLY) % RING
        assert AT_WO % RING == (spare + RING - WO_EARLY) % RING
        b_ = [spare * TILE]

        def spare_ring(words):
            b_[0] += words
            assert b_[0] <= (spare + RING - WO_EARLY) * TILE <= RING * TILE
            return ring[:, b_[0] - words:b_[0]]

        AF, DTF, PF, SF, M1F = (spare_ring(U2) for _ in range(5))
        DF = AF
        DC, DTC = (SF[:, x * T:x * T + T].rearrange("p (d n j) -> p d n j", d=2, j=32) for x in range(2))
        RM = spare_ring(2 * U2).rearrange("p (g d n i) -> p g d n i", g=2, d=2, i=CH)
        RH = spare_ring(4 * HD).rearrange("p (a v) -> p a v", a=4)
        FIRST = (0, 4, 8, 10)
        ZV = spare_ring(2 * U2).rearrange("p (g x v) -> p g x v", g=2, v=HD)

        def dt(v):
            return v.rearrange("p (d t) -> p d t", d=2)

        def dn(v):
            return v.rearrange("p (d n i) -> p d n i", d=2, n=NCH)

        OD = dt(PF)
        KK2 = KDF[:, 0:T]
        NLEV = len(LEVELS) - 1
        (s_ic, s_si, s_lo, s_sg, s_ldr, s_cum, s_ksq, s_kss, s_kr, s_krr, s_cu, s_ex2, s_op, s_ma, s_ms, s_bon, s_rt, s_rst, s_cc, s_inv,
         s_ll, s_ls, s_lr, s_rh, s_rhs, s_so, s_sos, s_st, s_out, s_os, s_zu, s_osum, s_mean, s_osq, s_var2, s_vs, s_or, s_pd,
         s_po) = (
            sem("rw_" + name) for name in (
                "pair_inputs_copied", "pair_state_in", "lora_products_ready", "lora_sigmoids_ready",
                "log_decay_scaled", "log_decay_summed", "kk_squares_ready",
                "kk_square_sums_ready", "kk_root_ready", "kk_scale_ready", "cumulated_ready", "decay_exps_ready",
                "operands_ready", "matrices_ready", "matrices_stored", "bonus_stored", "rows_ready", "rows_stored",
                "operands_kept", "inverse_level_ready", "level_left_ready", "level_left_stored", "level_right_ready",
                "rhs_ready", "rhs_stored", "solved_ready", "solved_stored", "step_state_products_ready", "step_out_ready", "step_out_stored",
                "state_updated", "out_sum_ready", "out_mean_ready", "out_squares_ready", "out_square_sums_ready",
                "out_variance_ready", "out_root_ready", "pair_done", "pair_state_out"))

        s_past = sem("rw_products_past_a_wait")
        pool_o = Order(nc.gpsimd, s_pool, sem("rw_pool_past_a_wait"))
        POOL_PER, DVE_PER = 22, 41
        NMA, NMS, NINV, NLL = 6, 5, 2 * (NLEV + 1), 2 * NLEV

        def two_banks(b):
            return ps[:, 512 * b:512 * b + 1024].rearrange("p (d w) -> p d w", d=2)[:, :, 0:T]

        def by_chunk(v):
            return v.rearrange("p d (n i) -> p d n i", i=CH)

        def msk(at):
            return C[:, at:at + 2 * CH].rearrange("p (d i) -> p d i", d=2).unsqueeze(2).broadcast_to([P, 2, NCH, CH])

        def msk1(at, d):
            return C[:, at + d * CH:at + d * CH + CH].unsqueeze(1).broadcast_to([P, NCH, CH])

        def each_pair(eng, core, prep):
            prep(eng, 0)
            with eng.Fori(0, KC - 1) as c:
                core(eng, c, prep)
            core(eng, KC - 1, None)

        halves = (slice(0, HD), slice(HD, P))
        with nc.Block() as block:
            @block.sync
            def _(sp):
                sp.sem_inc(s_po, 16)
                with sp.Fori(0, KC) as c:
                    sp.wait_ge(s_pd, c + 1)
                    for g, h in enumerate(halves):
                        sp.dma_start(ZV[h, g, 0:2], zrwkv[bass.ds(c, 1)].rearrange("r p d v -> (r p) d v")[h]
                                     ).then_inc(s_si, 16)
                    sp.wait_ge(s_zu, c * 3 + 2)
                    sp.dma_start(rwkv_out[bass.ds(c, 1)].rearrange("r p d v -> (r p) d v"), ZF).then_inc(s_po, 16)
                sp.wait_ge(s_po, 16 * KC + 16)

            def prep_act(act, j):
                for x, src in enumerate((RT, KT, VT)):
                    act.activation(RKV[:, x, :], src[:, bass.ds(j, 1), :].rearrange("p a t -> p (a t)"), ACT.Copy)
                act.activation(W2C, WA2[:, :, bass.ds(j, 1), :].rearrange("p d a c -> p d (a c)"), ACT.Copy)
                act.activation(PV, V[:, bass.ds(j * PAIR_VECS + V_PAIR, PAIR_VECS)], ACT.Copy).then_inc(s_ic, 1)
                act.wait_ge(s_ic, j + 1)
                act.wait_ge(s_lo, j + 1)
                for d in range(2):
                    act.activation(dt(LDF)[:, d], bank(4 + d), ACT.Sigmoid, bias=PV[:, d:d + 1])
                    last = act.activation(dt(KKAF)[:, d], bank(6 + d), ACT.Sigmoid, bias=PV[:, 2 + d:3 + d])
                last.then_inc(s_sg, 1)
                act.wait_ge(s_kss, j + 1)
                act.activation(KK2, bank(4), ACT.Sqrt, bias=C[:, C_TINY:C_TINY + 1]).then_inc(s_kr, 1)
                act.wait_ge(s_cu, j + 1)
                act.activation(EW, TW, ACT.Exp)
                act.activation(ALF, ALF, ACT.Exp)
                act.activation(RHOF, BF, ACT.Exp)
                act.activation(BEF, BF, ACT.Exp, scale=-1.0)
                act.activation(BCF, BCF, ACT.Exp).then_inc(s_ex2, 1)

            def prep_pool(pool, j):
                r_, k_ = RKV[:, 0, :], RKV[:, 1, :]
                b, ld = dt(BF), dt(LDF)
                kb, kkb, rb = (v.unsqueeze(1).broadcast_to([P, 2, T]) for v in (k_, KK, r_))
                pool.wait_ge(s_ic, j + 1)
                pool.sem_inc(pool_o.past, 1)
                pool_o(pool.tensor_scalar(KK, k_, PV[:, 4:5], None, ALU.mult))
                pool_o(pool.tensor_tensor(KK2, KK, KK, ALU.mult))
                pool.sem_inc(s_ksq, 1)
                pool.wait_ge(s_sg, j + 1)
                pool.sem_inc(pool_o.past, 1)
                pool_o(pool.tensor_scalar(LDF, LDF, -HALF_DECAY, None, ALU.mult))
                pool.sem_inc(s_ldr, 1)
                pool.wait_ge(s_cum, j + 1)
                pool.sem_inc(pool_o.past, 1)
                pool_o(pool.tensor_copy(TW, dn(BF)[:, :, :, CH - 1]))
                pool_o(pool.tensor_tensor(b[:, 1], ld[:, 1], b[:, 1], ALU.subtract))
                pool_o(pool.tensor_tensor(dn(BF)[:, 1], dn(BF)[:, 1],
                                          TW[:, 1].unsqueeze(2).broadcast_to([P, NCH, CH]), ALU.add))
                pool.wait_ge(s_cc, j + 1)
                pool_o.inc(pool.tensor_tensor(ALF, BF, LDF, ALU.subtract))
                pool_o.inc(pool.tensor_tensor(BCF.rearrange("p (n i) -> p n i", i=CH),
                                              TW.rearrange("p d n -> p (d n)").unsqueeze(2).broadcast_to([P, 2 * NCH, CH]),
                                              BF.rearrange("p (n i) -> p n i", i=CH), ALU.subtract))
                pool_o.wait()
                pool.sem_inc(s_cu, 1)
                pool.wait_ge(s_krr, j + 1)
                pool_o(pool.tensor_tensor(KK, KK, KK2, ALU.mult))
                pool_o(pool.tensor_scalar(KDF, KKAF, -1.0, PV[:, 5:6], ALU.add, ALU.mult))
                pool_o(pool.tensor_scalar(KDF, KDF, 1.0, None, ALU.add))
                pool_o.inc(pool.tensor_tensor(dt(KDF), dt(KDF), kb, ALU.mult))
                pool_o.inc(pool.tensor_tensor(dt(KKAF), dt(KKAF), kkb, ALU.mult))
                pool_o.wait()
                pool.wait_ge(s_ex2, j + 1)
                pool_o.inc(pool.tensor_tensor(dt(ALF), dt(ALF), kkb, ALU.mult))
                pool_o.inc(pool.tensor_tensor(dt(RHOF), dt(RHOF), rb, ALU.mult))
                pool_o.inc(pool.tensor_tensor(KAF, KDF, BEF, ALU.mult))
                pool_o.inc(pool.tensor_tensor(KCF, KDF, BCF, ALU.mult))
                pool_o.wait()
                pool_o.inc(pool.tensor_tensor(BEF, KKAF, BEF, ALU.mult))
                pool_o.inc(pool.tensor_tensor(BCF, KKAF, BCF, ALU.mult))
                pool_o(pool.tensor_tensor(KK, dt(KDF)[:, 0], dt(KDF)[:, 1], ALU.add))
                pool_o(pool.tensor_scalar(KK, KK, 0.5, PV[:, 6:7], ALU.mult, ALU.mult))
                pool_o(pool.tensor_tensor(KK, KK, r_, ALU.mult))
                pool.sem_inc(s_op, 1)

            def prep_dve(dve, j):
                dve.wait_ge(s_ldr, j + 1)
                for d in range(2):
                    last = dve.tensor_tensor_scan(dt(BF)[:, d], C[:, C_KEEP:C_KEEP + T], dt(LDF)[:, d], 0.0,
                                                  ALU.mult, ALU.add)
                last.then_inc(s_cum, 1)

            def prep_dve_root(dve, j):
                dve.wait_ge(s_kr, j + 1)
                dve.reciprocal(KK2, KK2).then_inc(s_krr, 1)

            def wait(pe, s, value):
                pe.wait_ge(s, value)
                pe.sem_inc(s_past, 1)

            def prep_pe_lora(pe, j):
                wait(pe, s_ic, j + 1)
                for d in range(2):
                    for g in range(2):
                        mm = pe.matmul(bank(4 + 2 * g + d), W2C[halves[g], d], LH[halves[g], d], start=True, stop=True)
                mm.then_inc(s_lo, 1)

            def prep_pe_norm(pe, j):
                wait(pe, s_ksq, j + 1)
                wait(pe, s_sg, j + 1)
                pe.matmul(bank(4), heads, KK2, start=True, stop=True).then_inc(s_kss, 1)

            def prep_pe(pe, j):
                prep_pe_lora(pe, j)
                prep_pe_norm(pe, j)

            def core_act(act, c, prep):
                act.wait_ge(s_pd, c + 1)
                for x, b in enumerate((0, 3, 5)):
                    act.wait_ge(s_rt, c * 3 + (x + 1))
                    for g, h in enumerate(halves):
                        rows = ps[0:HD, 512 * b:512 * b + 2 * NCH * P].rearrange("p (n g k) -> p n g k", g=2, k=HD)[:, :, g, :]
                        dst = (BK[h, g].rearrange("p d n k -> p (d n) k"),
                               BK[halves[1 - g], g].rearrange("p d n k -> p (d n) k"), ZV[halves[1 - g], g])[x]
                        last = act.activation(dst, rows, ACT.Copy)
                    last.then_inc(s_rst, 1)
                for s in range(4):
                    for a, d, n in lanes_at(s):
                        act.activation(EWC[:, FIRST[s] + a:FIRST[s] + a + 1], EW[:, d, n:n + 1], ACT.Copy)
                act.activation(LNV, PV[:, 7:9], ACT.Copy)
                for g, h in enumerate(halves):
                    act.activation(AB[h, g], dn(ALF)[h], ACT.Copy)
                    last = act.activation(RM[h, g], dn(RHOF)[h], ACT.Copy)
                last.then_inc(s_cc, 1)
                if prep:
                    act.wait_ge(s_bon, c + 1)
                    act.wait_ge(s_cc, c + 2)
                    prep(act, c + 1)
                act.wait_ge(s_vs, c + 2)
                act.activation(OD[:, 1], OD[:, 1], ACT.Sqrt).then_inc(s_or, 1)

            def core_dve(dve, c, prep):
                v_ = RKV[:, 2, :]
                for g, h in enumerate(halves):
                    dve_o.inc(dve.memset(ZV[h, g, 2:4], 0.0))
                block32 = C[:, C_BLOCK:C_BLOCK + CH].unsqueeze(1).broadcast_to([P, NCH, CH])
                i32 = C[:, C_I32:C_I32 + 32].unsqueeze(1).broadcast_to([P, NCH, 32])

                def split(v):
                    return v.rearrange("p n (b j) -> p n b j", b=2)

                def twice(v):
                    return v.unsqueeze(2).broadcast_to([P, NCH, 2, 32])

                for d in range(2):
                    dve.wait_ge(s_ma, c * NMA + (d + 1))
                    a_t = by_chunk(two_banks(0))[:, d]
                    dve_o.inc(dve.tensor_tensor(dn(DTF)[:, d], a_t, msk1(C_LEV1T, d), ALU.mult))
                    dve_o(dve.tensor_tensor(dn(ATF)[:, d], a_t, msk1(C_STRICT, d), ALU.mult))
                    dve.sem_inc(s_ms, 1)
                    dve_o.inc(dve.tensor_tensor(DTC[:, d], dn(DTF)[:, d, :, 0:32], dn(DTF)[:, d, :, 32:64], ALU.add))
                    dve_o(dve.tensor_tensor(dn(AF)[:, d], dn(ATF)[:, d], block32, ALU.mult))
                    dve_o(dve.tensor_tensor(DTC[:, d], i32, DTC[:, d], ALU.subtract))
                    dve.transpose(DC[:, d].rearrange("p n j -> p (n j)"),
                                  DTC[:, d].rearrange("p n j -> p (n j)")).then_inc(s_inv, 1)
                for n, (v, bk, cm) in enumerate(((AB, 2, C_STRICT), (None, 6, None), (M1F, 4, C_INCL), (RM, 6, C_INCL))):
                    dve.wait_ge(s_ma, c * NMA + (3 + n))
                    if v is None:
                        dve.tensor_tensor(BON, bank(bk), v_, ALU.mult).then_inc(s_bon, 1)
                    elif v is M1F:
                        dve.tensor_tensor(dn(v), by_chunk(two_banks(bk)), msk(cm), ALU.mult).then_inc(s_ms, 1)
                    else:
                        for g in range(2):
                            h = halves[1 - g]
                            last = dve.tensor_tensor(v[h, g], by_chunk(two_banks(bk))[h], msk(cm)[h], ALU.mult)
                        last.then_inc(s_ms, 1)
                for n in range(1, NLEV + 1):
                    for d in range(2):
                        dve.wait_ge(s_ll, c * NLL + (2 * n - 1 + d))
                        mask = msk1(C_LEV + 2 * (n - 1) * CH, d)
                        if n < NLEV:
                            p_ = bank(d, NCH * 32).rearrange("p (n j) -> p n j", j=32)
                            dve.tensor_tensor(split(dn(PF)[:, d]), twice(p_), split(mask), ALU.mult).then_inc(s_ls, 1)
                        else:
                            dve.tensor_tensor(dn(PF)[:, d], by_chunk(two_banks(0))[:, d], mask, ALU.mult).then_inc(s_ls, 1)
                    for d in range(2):
                        dve.wait_ge(s_lr, c * NLL + (2 * n - 1 + d))
                        if n == NLEV:
                            dve.tensor_tensor(dt(DTF)[:, d], dt(DTF)[:, d], two_banks(2)[:, d],
                                              ALU.subtract).then_inc(s_inv, 1)
                            continue
                        dtc, dc = (v[:, d].rearrange("p n j -> p (n j)") for v in (DTC, DC))
                        dve_o(dve.tensor_tensor(dtc, dtc, bank(2 + d, NCH * 32), ALU.subtract))
                        last = dve.transpose(dc, dtc)
                        if n == NLEV - 1:
                            dve_o(last)
                            dve.tensor_tensor(split(dn(DF)[:, d]), twice(DC[:, d]), split(block32), ALU.mult)
                            last = dve.tensor_tensor(split(dn(DTF)[:, d]), twice(DTC[:, d]), split(block32), ALU.mult)
                        last.then_inc(s_inv, 1)
                    if n == 2 and prep:
                        prep(dve, c + 1)
                    if n == 3 and prep:
                        prep_dve_root(dve, c + 1)
                for s in range(4):
                    ln = lanes_at(s)
                    w = len(ln)
                    x = FIRST[s]

                    def lanes(b, h):
                        return bank(b, w * HD)[h].rearrange("p (a v) -> p a v", v=HD)

                    to = []
                    if s < 3:
                        more = len(lanes_at(s + 1))
                        for g, h in enumerate(halves):
                            to.append((h, g, 0, more, ZV[h, g, FIRST[s + 1]:FIRST[s + 1] + more]))
                            if more < w:
                                to.append((h, g, more, w, ZF[h]))
                    dve.wait_ge(s_rh, c * 4 + (s + 1))
                    dve.tensor_copy(RH[:, 0:w], lanes(0, slice(0, P))).then_inc(s_rhs, 1)
                    if s == 1:
                        dve.wait_ge(s_po, c * 16 + 16)
                    for h, g, a, b, new in to:
                        last = dve.tensor_tensor(new, ZV[h, g, x + a:x + b],
                                                 EWC[h, x + a:x + b].unsqueeze(2).broadcast_to([HD, b - a, HD]), ALU.mult)
                    if to:
                        dve_o(last)
                    dve.wait_ge(s_so, c * 4 + (s + 1))
                    for g, h in enumerate(halves):
                        last = dve.tensor_scalar(ZV[h, g, x:x + w], lanes(1, h), -1.0, None, ALU.mult)
                    last.then_inc(s_sos, 1)
                    if to:
                        dve.wait_ge(s_st, c * 3 + (s + 1))
                        for h, g, a, b, new in to:
                            last = dve.tensor_tensor(new, new, lanes(3, h)[:, a:b], ALU.add)
                        dve_o(last)
                        dve.sem_inc(s_zu, 1)
                    dve.wait_ge(s_out, c * 4 + (s + 1))
                    for a, d, n in ln:
                        last = dve.tensor_copy(OD[:, d, CH * n:CH * n + CH], bank(2, CH, CH * a))
                    dve_o(last)
                    for a, d, n in ln:
                        o = OD[:, d, CH * n:CH * n + CH]
                        last = dve.tensor_tensor(o, o, bank(7, CH, CH * a), ALU.add)
                    dve_o(last)
                    dve.sem_inc(s_os, 1)
                dve.tensor_tensor(OD[:, 0], OD[:, 0], OD[:, 1], ALU.add).then_inc(s_osum, 1)
                dve.wait_ge(s_mean, c + 1)
                dve_o(dve.scalar_tensor_tensor(out=OD[:, 0], in0=bank(4), scalar=-1.0 / HD, in1=OD[:, 0],
                                               op0=ALU.mult, op1=ALU.add))
                dve.tensor_tensor(OD[:, 1], OD[:, 0], OD[:, 0], ALU.mult).then_inc(s_osq, 1)
                dve.wait_ge(s_var2, c + 1)
                dve.tensor_scalar(OD[:, 1], bank(5), 1.0 / HD, LN_EPS, ALU.mult, ALU.add).then_inc(s_vs, 1)
                dve.wait_ge(s_or, c + 1)
                dve_o(dve.reciprocal(OD[:, 1], OD[:, 1]))
                dve_o(dve.tensor_tensor(OD[:, 0], OD[:, 0], OD[:, 1], ALU.mult))
                dve_o(dve.tensor_scalar(OD[:, 0], OD[:, 0], LNV[:, 0:1], LNV[:, 1:2], ALU.mult, ALU.add))
                dve_o(dve.tensor_tensor(OD[:, 0], OD[:, 0], BON, ALU.add))
                dve.tensor_tensor(OT[:, bass.ds(c, 1), :].rearrange("p a t -> p (a t)"), OD[:, 0],
                                  GG[:, bass.ds(c, 1), :].rearrange("p a t -> p (a t)"), ALU.mult).then_inc(s_pd, 1)

            def core_pe(pe, c, prep):
                chunks = [(d, n) for d in range(2) for n in range(NCH)]
                by_d = (chunks[:NCH], chunks[NCH:])
                al, rho, be, ka = (dt(v) for v in (ALF, RHOF, BEF, KAF))

                def each(bk, left, right, some=chunks, swap=0, wide=CH):
                    for d, n in some:
                        for g, h in enumerate(halves):
                            mm = pe.matmul(bank(bk + d, wide, wide * n)[halves[g ^ swap]], left(h, d, n), right(h, d, n),
                                           start=True, stop=True)
                    return mm

                def seg(v):
                    return lambda h, d, n: v[h, d, CH * n:CH * n + CH]

                def mat(v):
                    return lambda h, d, n: dn(v)[h, d, n]

                def turned(v, order, bk):
                    for x, n in enumerate(order):
                        mm = pe.transpose(ps[0:HD, 512 * bk + P * x:512 * bk + P * x + P], v[:, CH * n:CH * n + CH], ident)
                    mm.then_inc(s_rt, 1)

                wait(pe, s_op, c + 1)
                for d in range(2):
                    each(0, seg(be), seg(al), by_d[d]).then_inc(s_ma, 1)
                each(2, seg(ka), seg(al), swap=1).then_inc(s_ma, 1)
                pe.matmul(bank(6), heads, KK, start=True, stop=True).then_inc(s_ma, 1)
                wait(pe, s_vs, c + 1)
                each(4, seg(be), seg(rho)).then_inc(s_ma, 1)
                wait(pe, s_bon, c + 1)
                each(6, seg(ka), seg(rho), swap=1).then_inc(s_ma, 1)
                wait(pe, s_ms, c * NMS + 3)
                turned(BCF, range(2 * NCH), 0)
                wait(pe, s_ms, c * NMS + 4)
                turned(KCF, range(2 * NCH), 3)
                wait(pe, s_ms, c * NMS + 5)
                wait(pe, s_rst, c * 3 + 2)
                turned(RKV[:, 2, :], [n for s in range(4) for a, d, n in lanes_at(s)], 5)
                for n in range(1, NLEV + 1):
                    for d in range(2):
                        wait(pe, s_inv, c * NINV + (2 * n - 1 + d))
                        if n < NLEV:
                            mm = each(0, mat(AF), lambda h, d, n: DC[h, d, n], by_d[d], wide=32)
                        else:
                            mm = each(0, mat(ATF), mat(DF), by_d[d])
                        mm.then_inc(s_ll, 1)
                    for d in range(2):
                        wait(pe, s_ls, c * NLL + (2 * n - 1 + d))
                        if n < NLEV:
                            mm = each(2, mat(PF), lambda h, d, n: DTC[h, d, n], by_d[d], wide=32)
                        else:
                            mm = each(2, mat(PF), mat(DTF), by_d[d])
                        mm.then_inc(s_lr, 1)
                    if prep and n == 1:
                        wait(pe, s_rst, c * 3 + 3)
                        prep_pe_lora(pe, c + 1)
                    if prep and n == 2:
                        prep_pe_norm(pe, c + 1)
                wait(pe, s_inv, c * NINV + NINV)
                wait(pe, s_si, c * 32 + 32)
                wait(pe, s_cc, c + 2)
                if not prep:
                    pe.wait_ge(s_rst, c * 3 + 3)
                dT, m1 = dn(DTF), dn(M1F)
                for s in range(4):
                    ln = [(g, h, FIRST[s] + a, a, d, n) for g, h in enumerate(halves) for a, d, n in lanes_at(s)]
                    if s:
                        wait(pe, s_zu, c * 3 + s)
                    for g, h, x, a, d, n in ln:
                        mm = pe.matmul(bank(0, HD, HD * a)[h], AB[:, g, d, n], ZV[:, g, x], start=True, stop=True)
                    mm.then_inc(s_rh, 1)
                    if s:
                        wait(pe, s_os, c * 4 + s)
                    for g, h, x, a, d, n in ln:
                        pe.matmul(bank(2, CH, CH * a)[h], ZV[:, g, x], RM[:, g, d, n], start=True, stop=True)
                    wait(pe, s_rhs, c * 4 + (s + 1))
                    for g, h, x, a, d, n in ln:
                        mm = pe.matmul(bank(1, HD, HD * a)[h], dT[h, d, n], RH[h, a], start=True, stop=True)
                    mm.then_inc(s_so, 1)
                    wait(pe, s_sos, c * 4 + (s + 1))
                    if s < 3:
                        for g, h, x, a, d, n in ln:
                            mm = pe.matmul(bank(3, HD, HD * a)[h], BK[:, g, d, n], ZV[:, g, x], start=True, stop=True)
                        mm.then_inc(s_st, 1)
                    for g, h, x, a, d, n in ln:
                        mm = pe.matmul(bank(7, CH, CH * a)[h], ZV[h, g, x], m1[h, d, n], start=True, stop=True)
                    mm.then_inc(s_out, 1)
                wait(pe, s_osum, c + 1)
                if prep:
                    wait(pe, s_kr, c + 2)
                pe.matmul(bank(4), heads, OD[:, 0], start=True, stop=True).then_inc(s_mean, 1)
                wait(pe, s_osq, c + 1)
                pe.matmul(bank(5), heads, OD[:, 1], start=True, stop=True).then_inc(s_var2, 1)

            @block.scalar
            def _(act):
                each_pair(act, core_act, prep_act)

            @block.gpsimd
            def _(pool):
                prep_pool(pool, 0)
                with pool.Fori(0, KC - 1) as c:
                    pool_o.enter(c, POOL_PER)
                    prep_pool(pool, c + 1)
                    pool_o.leave(KC - 1)

            @block.vector
            def _(dve):
                dve.sem_inc(s_pd, 1)
                dve.sem_inc(s_vs, 1)
                dve.sem_inc(s_cc, 1)
                prep_dve(dve, 0)
                prep_dve_root(dve, 0)
                with dve.Fori(0, KC - 1) as c:
                    dve_o.enter(c, DVE_PER)
                    core_dve(dve, c, prep_dve)
                    dve_o.leave(KC - 1)
                core_dve(dve, KC - 1, None)

            @block.tensor
            def _(pe):
                each_pair(pe, core_pe, prep_pe)

        out_block(1, AT_WO, OT, AT_MOE1 + RING, "mixer1_out")
        norm_block(1, 1, AT_MOE1 + RING)
        moe_block(1, AT_MOE1, N_TILES)
        norm_block(None, 0, N_TILES)


_INS = ["xT", "cst", "rcst", "vec", "sinkr", "ckT", "cv", "zgla", "zrwkv", "wrt", "brt", "dec2", "wa2", "wstream"]
_OUTS = [("yT", (P, KC * T)), ("kT_out", (HD, 2, CTX)), ("vT_out", (P, CTX)), ("gla_out", (2, P, 2, GV)),
         ("rwkv_out", (KC, P, 2, HD))]


def cols(v):
    return np.asarray(v, np.float32).reshape(-1, P).T


def tiles_of(w, width=256):
    k, n = w.shape
    return w.reshape(k // P, P, n // width, width).transpose(2, 1, 0, 3).reshape(n // width, P, -1)


def lay_out(i):
    f = {k: np.asarray(v) for k, v in i.items()}
    h = {}
    x = np.concatenate([f["x_prompt"][0], f["x_sample"][0]], 0)
    h["xT"] = np.ascontiguousarray(x.T.reshape(KC, P, T).transpose(1, 0, 2).reshape(P, KC * T))
    h["cst"] = constants()
    h["rcst"] = router_constants()
    v = np.zeros((P, V_N), np.float32)
    v[:, V_COND:V_COND + 2 * KC] = np.stack([cols(f["c_ctx"]), cols(f["c"][0])], 2).reshape(P, -1)
    v[:, V_ADA_B:V_NMIX] = cols(f["ada_b"].ravel())
    v[:, V_NMIX:V_NFFN] = cols(f["norm_mix"].ravel())
    v[:, V_NFFN:V_NOUT] = cols(f["norm_ffn"].ravel())
    v[:, V_NOUT:V_MU] = cols(f["norm_out"])
    v[:, V_MU:V_PAIR] = cols(f["rw_mu"][0].ravel())
    pair = [f["rw_w0"][0, 0], f["rw_w0"][0, 1], f["rw_a0"][0, 0], f["rw_a0"][0, 1], f["rw_kk"][0], f["rw_ka"][0],
            f["rw_rk"][0].ravel(), f["rw_lnx_w"][0], f["rw_lnx_b"][0]]
    v[:, V_PAIR:V_GNORM] = np.stack([cols(a) for a in pair], 2).reshape(P, -1)
    v[:, V_GNORM] = f["gla_norm"][0]
    v[:, V_DECB:V_DECB + 4] = f["gla_dec_b"][0].reshape(2, 2, P).transpose(2, 1, 0).reshape(P, 4)
    h["vec"] = v
    h["sinkr"] = f["att_sink"][0].copy()
    h["ckT"] = np.ascontiguousarray(f["cache_attn_k"][0, 0].transpose(2, 1, 0))
    h["cv"] = np.ascontiguousarray(f["cache_attn_v"][0, 0])
    h["zgla"] = np.ascontiguousarray(f["state_gla"][0, 0].reshape(2, 2, P, GV).transpose(1, 2, 0, 3))
    h["zrwkv"] = np.ascontiguousarray(
        f["state_rwkv"][0, 0].reshape(2, KC, 2, HD, HD).transpose(1, 2, 4, 0, 3).reshape(KC, P, 2, HD))
    wr = np.concatenate([f["moe_w_grp"], f["moe_w_exp"]], 2)
    h["wrt"] = np.ascontiguousarray(wr.reshape(2, KC, P, 20).transpose(0, 2, 1, 3))
    h["brt"] = np.concatenate([f["moe_b_grp"], f["moe_b_exp"]], 1)
    dec = np.zeros((2 * LR, 4 * P), np.float32)
    dec[:LR, :256] = f["gla_dec_w"][0, 0]
    dec[LR:, 256:] = f["gla_dec_w"][0, 1]
    h["dec2"] = dec
    h["wa2"] = np.concatenate([f["rw_w2"][0].transpose(1, 0, 2), f["rw_a2"][0].transpose(1, 0, 2)], 0
                              ).reshape(P, 2, KC, P)
    w = np.zeros((N_TILES, P, TILE), np.float32)
    for l in range(2):
        w[AT_ADA + l * MC // 2:AT_ADA + (l + 1) * MC // 2] = tiles_of(f["ada_w"][l])
    w_in = np.zeros((D, 2560), np.float32)
    w_in[:, :IN_W] = f["ev_w_in"][0]
    w[AT_IN:AT_OUT] = tiles_of(w_in)
    w[AT_OUT:AT_MOE0] = tiles_of(f["ev_w_out"][0])
    for l, at in ((0, AT_MOE0), (1, AT_MOE1)):
        for e in range(NE):
            t = at + 6 * e
            w[t:t + 4:2] = tiles_of(f["moe_w_gate"][l, e])
            w[t + 1:t + 4:2] = tiles_of(f["moe_w_up"][l, e])
            w[t + 4:t + 6] = tiles_of(f["moe_w_down"][l, e], 512)
    for n, name in enumerate(("rw_wr", "rw_wk", "rw_wv")):
        w[AT_RKV + 4 * n:AT_RKV + 4 * n + 4] = tiles_of(f[name][0])
    lora = np.concatenate([f["rw_w1"][0, 0], f["rw_w1"][0, 1], f["rw_a1"][0, 0], f["rw_a1"][0, 1]], 1)
    w[AT_LORA] = tiles_of(lora)[0]
    w[AT_GATE, :, :D] = tiles_of(f["rw_g1"][0], P)[0]
    w[AT_GATE, :, D:] = f["rw_g2"][0]
    w[AT_WO:AT_MOE1] = tiles_of(f["rw_wo"][0])
    h["wstream"] = w
    return h


def kernel(**inputs):
    import concourse.bacc as bacc
    from concourse.bass_utils import run_bass_kernel_spmd

    nc = bacc.Bacc("TRN2", target_bir_lowering=False, num_devices=1)
    arrays = lay_out(inputs)
    args = [nc.dram_tensor(n, arrays[n].shape, F32, kind="ExternalInput").ap() for n in _INS]
    args += [nc.dram_tensor(n, shape, F32, kind="ExternalOutput").ap() for n, shape in _OUTS]
    build(nc, *args)
    r = run_bass_kernel_spmd(nc, [arrays], core_ids=[0]).results[0]
    y = r["yT"].reshape(P, KC, T).transpose(2, 1, 0).reshape(1, T, D)
    k = r["kT_out"].transpose(2, 1, 0).reshape(1, 1, CTX, AKV, HD)
    v = r["vT_out"].T.reshape(1, 1, CTX, AKV, HD)
    g = r["gla_out"].reshape(2, 2, HD, 2, GV).transpose(3, 0, 1, 2, 4).reshape(1, 1, 2, GH, HD, GV)
    s = r["rwkv_out"].reshape(KC, 2, HD, 2, HD).transpose(3, 0, 1, 4, 2).reshape(1, 1, 2, 2 * KC, HD, HD)
    c = np.ascontiguousarray
    return c(y[:, :CTX]), c(y[:, CTX:]), c(k), c(v), c(g), c(s)
```

```python
from contextlib import ExitStack

import numpy as np

import concourse.bass as bass
from concourse import mybir

F32 = mybir.dt.float32
I32 = mybir.dt.int32
ALU = mybir.AluOpType
ACT = mybir.ActivationFunctionType
AX = mybir.AxisListType.X

P = 128
D = 1024
KC = D // P
CTX, LAT = 128, 256
T = CTX + LAT
STREAMS = ((0, 0, CTX), (1, CTX, T))
TILE = 2048
RING = 6
MC = 6 * KC
HD = 64
CH = 64
NCH = T // CH
GH, GV = 4, 128
AH, AKV = 8, 2
LR = 16
IN_W = 2336
NE, NG, EPG, FE = 16, 4, 4, 512
CAP = 96
SLOTS = 2 * T
EPS = 1e-6
LN_EPS = 64e-5
HALF_DECAY = float(np.exp(-0.5))

N_ADA = 2 * MC // 2
N_IN = 10
N_OUT = 4
N_MOE = NE * 6
AT_ADA = 0
AT_IN = AT_ADA + N_ADA
AT_OUT = AT_IN + N_IN
AT_MOE0 = AT_OUT + N_OUT
AT_RKV = AT_MOE0 + N_MOE
AT_LORA = AT_RKV + 12
AT_GATE = AT_LORA + 1
AT_WO = AT_GATE + 1
AT_MOE1 = AT_WO + 4
N_TILES = AT_MOE1 + N_MOE

V_COND = 0
V_ADA_B = V_COND + 2 * KC
V_NMIX = V_ADA_B + 2 * MC
V_NFFN = V_NMIX + 2 * KC
V_NOUT = V_NFFN + 2 * KC
V_MU = V_NOUT + KC
V_PAIR = V_MU + 6 * KC
PAIR_VECS = 9
V_GNORM = V_PAIR + PAIR_VECS * KC
V_DECB = V_GNORM + 1
V_N = V_DECB + 4

LEVELS = (1, 2, 4, 8, 16, 32)
C_ID = 0
C_ONES = C_ID + P
C_HEADS = C_ONES + P
C_INCL = C_HEADS + P
C_STRICT = C_INCL + 2 * CH
C_LEV = C_STRICT + 2 * CH
C_LEV1T = C_LEV + (len(LEVELS) - 1) * 2 * CH
C_BLOCK = C_LEV1T + 2 * CH
C_I32 = C_BLOCK + CH
C_I64 = C_I32 + 32
C_KEEP = C_I64 + CH
C_MASK = C_KEEP + T
C_COS = C_MASK + 2 * T
C_SIN = C_COS + LAT
C_PERM = C_SIN + LAT
C_TINY = C_PERM + HD
C_N = C_TINY + 1


def constants():
    c = np.zeros((P, C_N), np.float32)
    c[:, C_ID:C_ID + P] = np.eye(P)
    c[:, C_ONES:C_ONES + P] = 1.0
    c[:64, C_HEADS:C_HEADS + 64] = 1.0
    c[64:, C_HEADS + 64:C_HEADS + 128] = 1.0
    p = np.arange(CH)[:, None]
    f = np.arange(CH)[None, :]

    def put(at, m):
        c[:64, at:at + CH] = m
        c[64:, at:at + CH] = m

    put(C_INCL, p <= f)
    put(C_INCL + CH, p >= f)
    put(C_STRICT, p < f)
    put(C_STRICT + CH, p > f)
    for n, s in enumerate(LEVELS):
        lower = (p // (2 * s) == f // (2 * s)) & (p % (2 * s) >= s) & (f % (2 * s) < s)
        if s == 1:
            put(C_LEV1T, lower.T)
            put(C_LEV1T + CH, lower)
        else:
            put(C_LEV + 2 * (n - 1) * CH, lower)
            put(C_LEV + (2 * n - 1) * CH, lower.T)
    put(C_BLOCK, p // 32 == f // 32)
    put(C_I64, p == f)
    c[:, C_I32:C_I32 + 32] = np.arange(P)[:, None] % 32 == np.arange(32)[None, :]
    c[:, C_KEEP:C_KEEP + T] = np.arange(T) % CH != 0
    for b in range(2):
        q = b * P + np.arange(P)[:, None]
        k = np.arange(LAT)[None, :]
        c[:, C_MASK + b * T + CTX:C_MASK + (b + 1) * T] = np.where(np.abs(q - k) <= 128, 0.0, -1e30)
    freqs = (np.float32(10000.0) ** (-np.arange(0, 32, 2, dtype=np.float32) / np.float32(32))).astype(np.float32)
    t = np.arange(LAT)
    row = (t // 64).astype(np.float32)[None, :] * freqs[:, None]
    col = (t % 64).astype(np.float32)[None, :] * freqs[:, None]
    ang = np.concatenate([row, row, col, col], 0)
    put_at = slice(0, HD)
    c[put_at, C_COS:C_COS + LAT] = np.cos(ang)
    c[put_at, C_SIN:C_SIN + LAT] = np.sin(ang)
    perm = np.zeros((HD, HD), np.float32)
    for half in (0, 32):
        for i in range(16):
            perm[half + 16 + i, half + i] = -1.0
            perm[half + i, half + 16 + i] = 1.0
    c[:HD, C_PERM:C_PERM + HD] = perm
    c[:, C_TINY] = 1e-12
    return c


def router_constants():
    c = np.zeros((P, SLOTS + P), np.float32)
    c[:, :SLOTS] = np.arange(SLOTS)
    c[:, SLOTS:] = np.arange(P)[:, None] < np.arange(P)[None, :]
    return c


class Order:

    def __init__(self, eng, sem, past=None):
        self.eng, self.sem, self.past, self.n, self.at = eng, sem, past, 0, 0

    def __call__(self, ins):
        self.inc(ins)
        self.wait()

    def inc(self, ins):
        ins.then_inc(self.sem, 1)
        self.n += 1

    def wait(self):
        self.eng.wait_ge(self.sem, self.at + self.n)
        if self.past is not None:
            self.eng.sem_inc(self.past, 1)

    def enter(self, i, per):
        self.start, self.per = self.n, per
        self.at = i * per

    def leave(self, turns):
        assert self.n - self.start == self.per, self.n - self.start
        self.n = self.start + self.per * turns
        self.at = 0


def build(nc, xT, cst, rcst, vec, sinkr, ckT, cv, zgla, zrwkv, wrt, brt, dec2, wa2, wstream,
          yT, kT_out, vT_out, gla_out, rwkv_out):
    ctx = ExitStack()

    def sb(name, words):
        return ctx.enter_context(nc.sbuf_tensor(name, [P, words], F32))

    def sem(name):
        return ctx.enter_context(nc.semaphore(name))

    with ctx:
        ring = sb("ring", RING * TILE)
        XT_ = sb("XT", KC * T)
        HT_ = sb("HT", KC * T)
        C = sb("consts", C_N)
        V = sb("vecs", V_N)
        MOD = sb("mod", 2 * MC * 2)
        GAIN = sb("gain", 2 * 2 * KC * 2)
        SINK = sb("sink", AH)
        A = sb("arena", 30880)
        ps = ctx.enter_context(nc.psum_tensor("ps", [P, 8 * 512], F32))

        XT = XT_[:, :].rearrange("p (k t) -> p k t", k=KC)
        HT = HT_[:, :].rearrange("p (k t) -> p k t", k=KC)
        mod = MOD[:, :].rearrange("p (l a k c) -> p l a k c", l=2, a=6, k=KC)
        gain = GAIN[:, :].rearrange("p (l w k c) -> p l w k c", l=2, w=2, k=KC)
        ident = C[:, C_ID:C_ID + P]
        ones = C[:, C_ONES:C_ONES + P]
        heads = C[:, C_HEADS:C_HEADS + P]

        def bank(b, cols=T, at=0):
            return ps[:, b * 512 + at:b * 512 + at + cols]

        def area(at, words, **dims):
            v = A[:, at:at + words]
            if not dims:
                return v
            names = " ".join(dims)
            return v.rearrange(f"p ({names}) -> p {names}", **dims)

        w_in = [sem(f"weight_tile_in_slot{i}") for i in range(RING)]
        w_used = sem("weight_tiles_used")
        out_sem = sem("outputs_written")
        n_out = [0]

        issued = [0]

        def stream(sp, end):
            n = issued[0]
            while n < end:
                if n >= RING and n + RING <= end:
                    turns = (end - n) // RING
                    with sp.Fori(0, turns) as i:
                        for j in range(RING):
                            m = n + j
                            sp.wait_ge(w_used, i * RING + (m - RING + 1))
                            sp.dma_start(ring[:, m % RING * TILE:(m % RING + 1) * TILE],
                                         wstream[bass.ds(i * RING + m, 1)].rearrange("a p n -> (a p) n")
                                         ).then_inc(w_in[m % RING], 16)
                    n += turns * RING
                    continue
                if n >= RING:
                    sp.wait_ge(w_used, n - RING + 1)
                sp.dma_start(ring[:, n % RING * TILE:(n % RING + 1) * TILE], wstream[n]).then_inc(w_in[n % RING], 16)
                n += 1
            issued[0] = n

        def tile_in(pe, n, i=0):
            pe.wait_ge(w_in[n % RING], i * 16 + 16 * (n // RING + 1))

        def tile(n, **dims):
            names = " ".join(dims)
            return ring[:, n % RING * TILE:(n % RING + 1) * TILE].rearrange(f"p ({names}) -> p {names}", **dims)

        def linear(pe, at, chunks, rhs, ready, freed, rhs_wait=None, last_of=2, first=0):
            if rhs_wait is not None:
                pe.wait_ge(*rhs_wait)
            for m in chunks:
                n = at + m // 2
                if m % 2 == 0:
                    tile_in(pe, n)
                if m - first >= 8:
                    pe.wait_ge(freed, m - 7)
                w = tile(n, k=KC, c=256)
                for k in range(KC):
                    mm = pe.matmul(bank(m % 8), w[:, k, m % 2 * P:m % 2 * P + P], rhs[:, k, :],
                                   start=k == 0, stop=k == KC - 1)
                mm.then_inc(ready, 1)

        s_small, s_state = sem("small_inputs_in"), sem("x_in")
        s_cond, s_ada, s_ada_ev = sem("cond_silu_ready"), sem("ada_products_ready"), sem("ada_chunks_stored")
        s_dve, s_act, s_pool = sem("dve_order"), sem("act_order"), sem("pool_order")
        dve_o, act_o = Order(nc.vector, s_dve), Order(nc.scalar, s_act)
        SC = area(0, 2 * KC, k=KC, c=2)
        ROWS = area(2 * KC, N_ADA * 256)
        with nc.Block() as block:
            @block.sync
            def _(sp):
                stream(sp, AT_IN + RING)

            @block.scalar
            def _(act):
                act.dma_start(V[:, :], vec).then_inc(s_small, 16)
                act.dma_start(C[:, :], cst).then_inc(s_small, 16)
                act.dma_start(SINK[:, :], sinkr.partition_broadcast(P)).then_inc(s_small, 16)
                act.dma_start(XT_[:, :], xT).then_inc(s_state, 16)
                act.wait_ge(s_small, 48)
                act.activation(SC, V[:, V_COND:V_COND + 2 * KC].rearrange("p (k c) -> p k c", c=2),
                               ACT.Silu).then_inc(s_cond, 1)
                act.wait_ge(s_state, 16)

                with act.Fori(0, N_ADA // RING) as i:
                    for b in range(RING // 2):
                        act.wait_ge(w_used, i * RING + (2 * b + 2))
                        act.activation(ROWS[0:2, bass.ds(i * (RING * 256) + b * 512, 512)], bank(b, 512)[0:2],
                                       ACT.Copy).then_inc(s_ada_ev, 1)

            @block.tensor
            def _(pe):
                pe.wait_ge(s_cond, 1)
                with pe.Fori(0, N_ADA // RING) as i:
                    for j in range(RING):
                        if j % 2 == 0:
                            pe.wait_ge(s_ada_ev, i * (RING // 2) + (j // 2 + 1))
                        tile_in(pe, j, i)
                        w = tile(j, k=KC, c=256)
                        for k in range(KC):
                            mm = pe.matmul(bank(j // 2, 256, j % 2 * 256)[0:2], SC[:, k, :], w[:, k, :],
                                           start=k == 0, stop=k == KC - 1)
                        mm.then_inc(w_used, 1)
                pe.wait_ge(s_ada_ev, N_ADA // 2 + RING // 2)
                for m in range(2 * MC):
                    mm = pe.transpose(bank(4, 2, 2 * m), ROWS[0:2, P * m:P * m + P], ident[0:2, 0:2])
                mm.then_inc(s_ada, 1)

            @block.vector
            def _(dve):
                dve.wait_ge(s_small, 48)
                dve.sem_inc(s_ada_ev, RING // 2)
                dve.wait_ge(s_ada, 1)
                b = V[:, V_ADA_B:V_ADA_B + 2 * MC].unsqueeze(2).broadcast_to([P, 2 * MC, 2])
                dve_o(dve.tensor_tensor(MOD[:, :].rearrange("p (m c) -> p m c", c=2),
                                        bank(4, 4 * MC).rearrange("p (m c) -> p m c", c=2), b, ALU.add))
                for l in range(2):
                    for w, vn in ((0, V_NMIX), (1, V_NFFN)):
                        nw = V[:, vn + l * KC:vn + (l + 1) * KC].unsqueeze(2).broadcast_to([P, KC, 2])
                        last = dve.scalar_tensor_tensor(out=gain[:, l, w], in0=mod[:, l, 3 * w + 1], scalar=1.0,
                                                        in1=nw, op0=ALU.add, op1=ALU.mult)
                        dve_o(last)

        s_sqs = sem("squares_of_chunks_added")
        s_sq, s_ss, s_var, s_sd, s_rs, s_xn = (sem("squares_ready"), sem("square_sums_ready"), sem("variance_ready"),
                                               sem("std_ready"), sem("rstd_ready"), sem("normalised_ready"))
        norms = [0]

        def norm_block(l, w, end, save=None):
            n = norms[0]
            norms[0] += 1
            RS, VAR = area(0, T), area(T, T)
            with nc.Block() as block:
                @block.sync
                def _(sp):
                    stream(sp, end)

                @block.scalar
                def _(act):
                    for k in range(KC):
                        act.activation(HT[:, k, :], XT[:, k, :], ACT.Square).then_inc(s_sq, 1)
                    act.wait_ge(s_var, n + 1)
                    act.activation(VAR, VAR, ACT.Sqrt).then_inc(s_sd, 1)
                    for k in range(KC):
                        act.wait_ge(s_xn, n * KC + k + 1)
                        if l is None:
                            act_o(act.activation(HT[:, k, :], HT[:, k, :], ACT.Copy,
                                                 scale=V[:, V_NOUT + k:V_NOUT + k + 1]))
                            continue
                        for c, a, b in STREAMS:
                            act_o.inc(act.activation(HT[:, k, a:b], HT[:, k, a:b], ACT.Identity,
                                                     bias=mod[:, l, 3 * w, k, c:c + 1],
                                                     scale=gain[:, l, w, k, c:c + 1]))
                    act_o.wait()
                    if l is None:
                        act.dma_start(yT, HT_[:, :]).then_inc(out_sem, 16)
                        n_out[0] += 16
                        act.wait_ge(out_sem, n_out[0])

                @block.tensor
                def _(pe):
                    pe.wait_ge(s_sqs, n + 1)
                    pe.matmul(bank(0), ones, RS, start=True, stop=True).then_inc(s_ss, 1)

                @block.vector
                def _(dve):
                    for k in range(1, KC):
                        dve.wait_ge(s_sq, n * KC + k + 1)
                        dve_o(dve.tensor_tensor(RS, HT[:, 0, :] if k == 1 else RS, HT[:, k, :], ALU.add))
                    dve.sem_inc(s_sqs, 1)
                    dve.wait_ge(s_ss, n + 1)
                    dve.tensor_scalar(VAR, bank(0), 1.0 / D, EPS, ALU.mult, ALU.add).then_inc(s_var, 1)
                    dve.wait_ge(s_sd, n + 1)
                    dve_o(dve.reciprocal(RS, VAR))
                    for k in range(KC):
                        dve.tensor_tensor(HT[:, k, :], XT[:, k, :], RS, ALU.mult).then_inc(s_xn, 1)

        norm_block(0, 0, AT_IN + RING)

        a_ = [0]

        def take(words):
            a_[0] += words
            return a_[0] - words

        QG = area(take(2 * T), 2 * T, c=2, t=T)
        KG = area(take(2 * T), 2 * T, c=2, t=T)
        GVT = area(take(4 * T), 4 * T, h=4, t=T)
        SG = area(take(4 * T), 4 * T, h=4, t=T)
        at_aq = take(8 * T)
        AQK = area(at_aq, 8 * T, h=8, t=T)
        AK = area(take(2 * T), 2 * T, h=2, t=T)
        AVT = area(take(T), T)
        LRT = area(take(T), T)
        VR = area(take(T), T, a=3, d=P)
        GVR = area(take(2 * NCH * GV), 2 * NCH * GV, r=2, n=NCH, v=GV)
        LD = area(take(4 * T), 4 * T, r=2, d=2, t=T)
        CK = area(take(2 * P), 2 * P, h=2, t=P)
        CV = area(take(P), P, h=2, e=HD)
        DEC = area(take(4 * P), 4 * P)
        at_tmp = a_[0]
        OT = HT
        s_in, s_in_ev, s_side = sem("projection_ready"), sem("projection_stored"), sem("side_inputs_in")
        with nc.Block() as block:
            @block.sync
            def _(sp):
                sp.dma_start(CK[0:HD], ckT).then_inc(s_side, 16)
                sp.dma_start(CV, cv).then_inc(s_side, 16)
                sp.dma_start(DEC[0:2 * LR, :], dec2).then_inc(s_side, 16)
                stream(sp, AT_OUT + N_OUT)
                sp.wait_ge(s_side, 48)

            @block.tensor
            def _(pe):
                linear(pe, AT_IN, range(18), HT, s_in, s_in_ev)
                tile_in(pe, AT_IN + 9)
                pe.wait_ge(s_in_ev, 11)
                w = tile(AT_IN + 9, k=KC, c=256)
                for k in range(KC):
                    mm = pe.matmul(bank(2)[0:2 * LR, :], w[:, k, 0:2 * LR], HT[:, k, :], start=k == 0, stop=k == KC - 1)
                mm.then_inc(s_in, 1)

            @block.scalar
            def _(act):
                for m in range(19):
                    act.wait_ge(s_in, m + 1)
                    if m % 2 == 1 or m == 18:
                        act.sem_inc(w_used, 1)
                    o = bank(m % 8)
                    if m < 2:
                        last = act.activation(QG[:, m, :], o, ACT.Copy, scale=HD ** -0.5)
                    elif m < 4:
                        last = act.activation(KG[:, m - 2, :], o, ACT.Copy)
                    elif m < 8:
                        last = act.activation(GVT[:, m - 4, :], o, ACT.Copy)
                    elif m < 12:
                        last = act.activation(SG[:, m - 8, :], o, ACT.Silu)
                    elif m < 16:
                        h = 2 * (m - 12)
                        act.activation(AQK[0:HD, h, :], o[0:HD], ACT.Copy, scale=HD ** -0.5)
                        last = act.activation(AQK[0:HD, h + 1, :], o[HD:P], ACT.Copy, scale=HD ** -0.5)
                    elif m == 16:
                        act.activation(AK[0:HD, 0, :], o[0:HD], ACT.Copy)
                        last = act.activation(AK[0:HD, 1, :], o[HD:P], ACT.Copy)
                    elif m == 17:
                        last = act.activation(AVT, o, ACT.Copy)
                    else:
                        last = act.activation(LRT[0:2 * LR, :], o[0:2 * LR], ACT.Copy)
                    last.then_inc(s_in_ev, 1)

        ROT = area(at_tmp, 10 * LAT, h=10, t=LAT)
        Z_ = area(at_tmp + 10 * LAT, 4 * T, r=2, d=2, t=T)
        E_ = area(at_tmp + 10 * LAT + 4 * T, 4 * T, r=2, d=2, t=T)
        assert at_tmp + 10 * LAT + 8 * T <= 30880
        s_rows, s_ldp, s_rope, s_free = sem("value_rows_ready"), sem("decay_products_ready"), sem("rotated_ready"), sem("rope_banks_read")
        s_z, s_l = sem("decay_argument_ready"), sem("decay_log_ready")
        with nc.Block() as block:
            @block.scalar
            def _(act):
                act.dma_start(kT_out, AK[0:HD, :, 0:CTX]).then_inc(out_sem, 16)
                act.dma_start(vT_out, AVT[:, 0:CTX]).then_inc(out_sem, 16)
                n_out[0] += 32
                for r in range(2):
                    act.wait_ge(s_rows, r + 1)
                    act_o.inc(act.activation(GVR[:, r], ps[:, 1024 * r:1024 * r + NCH * GV].rearrange(
                        "p (n v) -> p n v", v=GV), ACT.Copy))
                act.wait_ge(s_rows, 3)
                act_o(act.activation(VR, bank(4).rearrange("p (a d) -> p a d", d=P), ACT.Copy))
                act.sem_inc(s_free, 1)
                for r in range(2):
                    for d in range(2):
                        u = 2 * r + d
                        act.wait_ge(s_ldp, u + 1)
                        o = bank(5 + u) if u < 3 else bank(4)
                        act_o.inc(act.activation(Z_[:, r, d, :], o, ACT.Identity,
                                                 bias=V[:, V_DECB + u:V_DECB + u + 1]))
                        if u == 0:
                            act_o.wait()
                            act.sem_inc(s_free, 1)
                act_o.wait()
                act.sem_inc(s_z, 1)
                zf, ef = Z_.rearrange("p r d t -> p (r d t)"), E_.rearrange("p r d t -> p (r d t)")
                act_o(act.activation(ef, zf, ACT.Abs))
                act_o(act.activation(ef, ef, ACT.Exp, scale=-1.0))
                act.activation(ef, ef, ACT.Ln, bias=1.0).then_inc(s_l, 1)

            @block.tensor
            def _(pe):
                for r in range(2):
                    for n in range(NCH):
                        for hp in range(2):
                            mm = pe.matmul(ps[HD * (1 - hp):HD * (2 - hp), 1024 * r + GV * n:1024 * r + GV * (n + 1)],
                                           GVT[:, 2 * r + hp, CH * n:CH * (n + 1)], ident, start=True, stop=True)
                    mm.then_inc(s_rows, 1)
                for a in range(3):
                    mm = pe.matmul(bank(4, P, P * a), AVT[:, P * a:P * a + P], ident, start=True, stop=True)
                mm.then_inc(s_rows, 1)
                for u in range(4):
                    if u == 3:
                        pe.wait_ge(s_free, 1)
                    r, d = divmod(u, 2)
                    pe.matmul(bank(5 + u) if u < 3 else bank(4), DEC[0:2 * LR, 256 * d + P * r:256 * d + P * r + P],
                              LRT[0:2 * LR, :], start=True, stop=True).then_inc(s_ldp, 1)
                for h in range(10):
                    if h == 8:
                        pe.wait_ge(s_free, 2)
                    src = AQK[0:HD, h, CTX:T] if h < 8 else AK[0:HD, h - 8, CTX:T]
                    b = h // 2 if h < 8 else 5
                    mm = pe.matmul(bank(b, LAT, LAT * (h % 2))[0:HD], C[0:HD, C_PERM:C_PERM + HD], src,
                                   start=True, stop=True)
                    mm.then_inc(s_rope, 1)

            @block.vector
            def _(dve):
                cos = C[0:HD, C_COS:C_COS + LAT]
                sin = C[0:HD, C_SIN:C_SIN + LAT]
                for h in range(10):
                    dve.wait_ge(s_rope, h // 2 * 2 + 2)
                    b = h // 2 if h < 8 else 5
                    x = AQK[0:HD, h, CTX:T] if h < 8 else AK[0:HD, h - 8, CTX:T]
                    dve.tensor_tensor(ROT[0:HD, h, :], bank(b, LAT, LAT * (h % 2))[0:HD], sin, ALU.mult)
                    dve_o(dve.tensor_tensor(x, x, cos, ALU.mult))
                    dve_o.inc(dve.tensor_tensor(x, x, ROT[0:HD, h, :], ALU.add))
                dve_o.wait()
                dve.wait_ge(s_l, 1)
                zf, ef, lf = (v.rearrange("p r d t -> p (r d t)") for v in (Z_, E_, LD))
                dve_o(dve.tensor_scalar(zf, zf, 0.0, 1.0 / 16.0, ALU.min, ALU.mult))
                dve_o(dve.scalar_tensor_tensor(out=lf, in0=ef, scalar=-1.0 / 16.0, in1=zf,
                                               op0=ALU.mult, op1=ALU.add))

        units = [(h, -1) for h in range(AH)] + [(h, b) for h in range(AH) for b in range(2)]
        NU = len(units)
        S = area(at_tmp, 3 * T, b=3, t=T)
        PR = area(at_tmp + 3 * T, 3 * T, b=3, t=T)
        PTR = area(at_tmp + 6 * T, 2 * T, b=2, t=T)
        ST = area(at_tmp + 8 * T, 8 * NU, u=NU, v=8)
        s_sc, s_scr, s_nm, s_p, s_pn = (sem("scores_ready"), sem("scores_read"), sem("row_max_ready"), sem("probs_ready"),
                                        sem("probs_normalised"))
        s_pt, s_ptc, s_ao, s_aoc = sem("probs_turned"), sem("turned_probs_stored"), sem("attention_ready"), sem("attention_stored")
        with nc.Block() as block:
            def keys(b):
                return CTX if b < 0 else T

            @block.tensor
            def _(pe):
                def scores(u):
                    h, b = units[u]
                    kv = h // (AH // AKV)
                    if u >= 3:
                        pe.wait_ge(s_scr, u - 2)
                    if b < 0:
                        mm = pe.matmul(bank(u % 3, CTX), AQK[0:HD, h, 0:CTX], AK[0:HD, kv, 0:CTX], start=True, stop=True)
                    else:
                        q = AQK[0:HD, h, CTX + P * b:CTX + P * b + P]
                        pe.matmul(bank(u % 3, P), q, CK[0:HD, kv, :], start=True, stop=True)
                        mm = pe.matmul(bank(u % 3, LAT, P), q, AK[0:HD, kv, CTX:T], start=True, stop=True)
                    mm.then_inc(s_sc, 1)

                def turn(u):
                    pe.wait_ge(s_pn, u + 1)
                    if u >= 2:
                        pe.wait_ge(s_ptc, u - 1)
                    for a in range(keys(units[u][1]) // P):
                        mm = pe.transpose(bank(3 + u % 2, P, P * a), PR[:, u % 3, P * a:P * a + P], ident)
                    mm.then_inc(s_pt, 1)

                def mix(u):
                    h, b = units[u]
                    kv = h // (AH // AKV)
                    pe.wait_ge(s_ptc, u + 1)
                    if u >= 2:
                        pe.wait_ge(s_aoc, u - 1)
                    vs = [VR[:, 0, HD * kv:HD * kv + HD]] if b < 0 else \
                        [CV[:, kv, :], VR[:, 1, HD * kv:HD * kv + HD], VR[:, 2, HD * kv:HD * kv + HD]]
                    o = bank(5 + u % 2, P)[HD * (h % 2):HD * (h % 2) + HD]
                    for a, v in enumerate(vs):
                        mm = pe.matmul(o, v, PTR[:, u % 2, P * a:P * a + P], start=a == 0, stop=a == len(vs) - 1)
                    mm.then_inc(s_ao, 1)

                scores(0)
                for u in range(NU + 2):
                    if u + 1 < NU:
                        scores(u + 1)
                    if 1 <= u <= NU:
                        turn(u - 1)
                    if u >= 2:
                        mix(u - 2)

            @block.scalar
            def _(act):
                def exps(u):
                    h, b = units[u]
                    n = keys(b)
                    act.wait_ge(s_nm, u + 1)
                    if u >= 3:
                        act.wait_ge(s_pt, u - 2)
                    act.activation(ST[:, u, 3:4], SINK[:, h:h + 1], ACT.Exp, bias=ST[:, u, 1:2])
                    act.activation(PR[:, u % 3, 0:n], S[:, u % 3, 0:n], ACT.Exp, bias=ST[:, u, 1:2],
                                   accum_out=ST[:, u, 2:3]).then_inc(s_p, 1)

                def store_turned(u):
                    n = keys(units[u][1])
                    act.wait_ge(s_pt, u + 1)
                    if u >= 2:
                        act.wait_ge(s_ao, u - 1)
                    act.activation(PTR[:, u % 2, 0:n], bank(3 + u % 2, n), ACT.Copy).then_inc(s_ptc, 1)

                def store_out(u):
                    h, b = units[u]
                    act.wait_ge(s_ao, u + 1)
                    p0, t0 = HD * (h % 2), 0 if b < 0 else CTX + P * b
                    act.activation(OT[p0:p0 + HD, 4 + h // 2, t0:t0 + P], bank(5 + u % 2, P)[p0:p0 + HD],
                                   ACT.Copy).then_inc(s_aoc, 1)

                for u in range(NU + 2):
                    if u < NU:
                        exps(u)
                    if 1 <= u <= NU:
                        store_turned(u - 1)
                    if u >= 2:
                        store_out(u - 2)

            @block.vector
            def _(dve):
                def front(u):
                    h, b = units[u]
                    n = keys(b)
                    dve.wait_ge(s_sc, u + 1)
                    if u >= 3:
                        dve.wait_ge(s_p, u - 2)
                    if b < 0:
                        dve.tensor_copy(S[:, u % 3, 0:n], bank(u % 3, n)).then_inc(s_scr, 1)
                    else:
                        dve.tensor_tensor(S[:, u % 3, :], bank(u % 3), C[:, C_MASK + T * b:C_MASK + T * (b + 1)],
                                          ALU.add).then_inc(s_scr, 1)
                    dve.wait_ge(s_scr, u + 1)
                    dve_o(dve.reduce_max(ST[:, u, 0:1], S[:, u % 3, 0:n], AX))
                    dve.tensor_scalar(ST[:, u, 1:2], ST[:, u, 0:1], SINK[:, h:h + 1], -1.0,
                                      ALU.max, ALU.mult).then_inc(s_nm, 1)

                def back(u):
                    n = keys(units[u][1])
                    dve.wait_ge(s_p, u + 1)
                    dve_o(dve.tensor_tensor(ST[:, u, 4:5], ST[:, u, 2:3], ST[:, u, 3:4], ALU.add))
                    dve_o(dve.reciprocal(ST[:, u, 5:6], ST[:, u, 4:5]))
                    dve.tensor_scalar(PR[:, u % 3, 0:n], PR[:, u % 3, 0:n], ST[:, u, 5:6], None,
                                      ALU.mult).then_inc(s_pn, 1)

                front(0)
                for u in range(NU):
                    if u + 1 < NU:
                        front(u + 1)
                    back(u)

        a_[0] = at_aq
        B = area(take(4 * T), 4 * T, r=2, d=2, t=T)
        at_qa0 = take(4 * T)
        assert a_[0] <= at_aq + 8 * T
        a_[0] = at_tmp
        KN = area(take(4 * T), 4 * T, r=2, d=2, t=T)
        KD = area(take(4 * T), 4 * T, r=2, d=2, t=T)
        KDR = area(take(4 * T), 4 * T, r=2, d=2, n=NCH, k=HD)
        QA = [area(at, 4 * T, r=2, d=2, n=NCH, i=CH) for at in (at_qa0, take(4 * T))]
        TOT = area(take(4 * NCH), 4 * NCH, r=2, d=2, n=NCH)
        EBT = area(take(4 * NCH), 4 * NCH, r=2, d=2, n=NCH)
        ZVG = area(take(4 * 2 * NCH * GV), 4 * 2 * NCH * GV, g=2, r=2, x=2 * NCH, v=GV)
        ZFG = area(take(4 * GV), 4 * GV, r=2, d=2, v=GV)
        OF = area(take(8 * T), 8 * T, d=2, h=4, t=T)
        assert a_[0] <= 30880
        LANES = ((0, (2, 3, 4, 5)), (1, (5, 4, 3, 2)), (0, (0, 1)), (1, (1, 0)))

        def lanes_at(s):
            return [(a, d, n[s]) for a, (d, n) in enumerate(LANES) if s < len(n)]

        FIRST = (0, 4, 8, 10)
        halves = (slice(0, HD), slice(HD, P))
        s_zv = sem("gla_values_placed")
        pool_g = Order(nc.gpsimd, s_zv)
        s_tot, s_b, s_e, s_qk, s_am, s_ams, s_zin = (
            sem("gla_totals_ready"), sem("gla_cumulated_ready"), sem("gla_exps_ready"), sem("gla_operands_ready"),
            sem("gla_matrices_ready"), sem("gla_matrices_stored"), sem("gla_state_in"))
        s_go, s_gz, s_goc, s_gzc = (sem("gla_chunk_ready"), sem("gla_state_products_ready"), sem("gla_chunk_stored"),
                                    sem("gla_state_updated"))
        with nc.Block() as block:
            def flat(v):
                return v.rearrange("p r d t -> p (r d t)")

            @block.sync
            def _(sp):
                for r in range(2):
                    for g, h in enumerate(halves):
                        sp.dma_start(ZVG[h, g, r, 0:2], zgla[r][h]).then_inc(s_zin, 16)
                sp.wait_ge(s_zin, 64)

            @block.gpsimd
            def _(pool):
                for s in range(4):
                    for a, d, n in lanes_at(s):
                        for g in range(2):
                            h = halves[1 - g]
                            pool_g(pool.tensor_copy(ZVG[h, g, :, FIRST[s] + a], GVR[h, :, n]))

            @block.vector
            def _(dve):
                for g, h in enumerate(halves):
                    dve_o.inc(dve.memset(ZVG[h, g, :, 2:4], 0.0))
                for r in range(2):
                    for d in range(2):
                        dve_o.inc(dve.tensor_tensor_scan(B[:, r, d, :], C[:, C_KEEP:C_KEEP + T], LD[:, r, d, :], 0.0,
                                                         ALU.mult, ALU.add))
                dve_o.wait()
                Bc = B.rearrange("p r d (n i) -> p r d n i", i=CH)
                for r in range(2):
                    dve_o.inc(dve.tensor_copy(TOT[:, r], Bc[:, r, :, :, CH - 1]))
                dve_o.wait()
                dve.sem_inc(s_tot, 1)
                for r in range(2):
                    dve_o(dve.scalar_tensor_tensor(out=B[:, r, 1, :], in0=B[:, r, 1, :], scalar=-1.0,
                                                   in1=LD[:, r, 1, :], op0=ALU.mult, op1=ALU.add))
                    dve_o.inc(dve.tensor_tensor(Bc[:, r, 1], Bc[:, r, 1],
                                                TOT[:, r, 1].unsqueeze(2).broadcast_to([P, NCH, CH]), ALU.add))
                dve_o.wait()
                for r in range(2):
                    kd = KD[:, r].rearrange("p d (n i) -> p d n i", i=CH)
                    dve_o.inc(dve.scalar_tensor_tensor(
                        out=KD[:, r].rearrange("p d (n i) -> p (d n) i", i=CH),
                        in0=B[:, r].rearrange("p d (n i) -> p (d n) i", i=CH), scalar=-1.0,
                        in1=TOT[:, r].rearrange("p d n -> p (d n)").unsqueeze(2).broadcast_to([P, 2 * NCH, CH]),
                        op0=ALU.mult, op1=ALU.add))
                dve_o.wait()
                dve.sem_inc(s_b, 1)
                dve.wait_ge(s_e, 1)
                for r in range(2):
                    for g, h in enumerate(halves):
                        q = QA[g][h, r].rearrange("p d n i -> p d (n i)")
                        dve_o.inc(dve.tensor_tensor(q, q, QG[h, r].unsqueeze(1).broadcast_to([HD, 2, T]), ALU.mult))
                for dst, src in ((KN, KG), (KD, KG)):
                    for r in range(2):
                        dve_o.inc(dve.tensor_tensor(dst[:, r], dst[:, r], src[:, r].unsqueeze(1).broadcast_to([P, 2, T]),
                                                    ALU.mult))
                dve_o.wait()
                dve.sem_inc(s_qk, 1)
                for r in range(2):
                    dve.wait_ge(s_am, r + 1)
                    m = C[:, C_INCL:C_INCL + 2 * CH].rearrange("p (d i) -> p d i", d=2).unsqueeze(2)
                    for g in range(2):
                        h = halves[1 - g]
                        last = dve.tensor_tensor(
                            QA[g][h, r], ps[h, 1024 * r:1024 * r + 2 * T].rearrange("p (d n i) -> p d n i", d=2, n=NCH),
                            m[h].broadcast_to([HD, 2, NCH, CH]), ALU.mult)
                    last.then_inc(s_ams, 1)
                    dve.tensor_copy(KDR[:, r], ps[:, 2048 + 1024 * r:2048 + 1024 * r + 2 * T].rearrange(
                        "p (d n i) -> p d n i", d=2, n=NCH)).then_inc(s_ams, 1)
                for s in range(3):
                    dve.wait_ge(s_gz, s + 1)
                    more = len(lanes_at(s + 1))
                    for r in range(2):
                        for a, d, n in lanes_at(s):
                            for g, h in enumerate(halves):
                                new = ZVG[h, g, r, FIRST[s + 1] + a] if a < more else ZFG[h, r, a - more]
                                dve_o.inc(dve.scalar_tensor_tensor(
                                    out=new, in0=ZVG[h, g, r, FIRST[s] + a], scalar=EBT[h, r, d, n:n + 1],
                                    in1=bank(2 + r, GV, a * GV)[h], op0=ALU.mult, op1=ALU.add))
                    dve_o.wait()
                    dve.sem_inc(s_gzc, 1)

            @block.scalar
            def _(act):
                act.wait_ge(s_tot, 1)
                act.activation(EBT.rearrange("p r d n -> p (r d n)"), TOT.rearrange("p r d n -> p (r d n)"), ACT.Exp)
                act.wait_ge(s_b, 1)
                for g, h in enumerate(halves):
                    act.activation(QA[g][h].rearrange("p r d n i -> p (r d n i)"), flat(B)[h], ACT.Exp)
                act.activation(flat(KN), flat(B), ACT.Exp, scale=-1.0)
                act_o(act.activation(flat(KD), flat(KD), ACT.Exp))
                act.sem_inc(s_e, 1)
                for s in range(4):
                    act.wait_ge(s_go, s + 1)
                    for a, d, n in lanes_at(s):
                        src = ps[:, 0:1024].rearrange("p (x r a i) -> p r x a i", x=2, r=2, a=4)[:, :, :, a, :]
                        dst = OF[:, d].rearrange("p (r x) t -> p r x t", r=2)[:, :, :, CH * n:CH * n + CH]
                        act_o.inc(act.activation(dst, src, ACT.Copy))
                    act_o.wait()
                    act.sem_inc(s_goc, 1)
                act.wait_ge(s_gzc, 3)
                for r in range(2):
                    act.dma_start(gla_out[r], ZFG[:, r]).then_inc(out_sem, 16)
                n_out[0] += 32
                act.wait_ge(out_sem, n_out[0])

            @block.tensor
            def _(pe):
                pe.wait_ge(s_qk, 1)
                for r in range(2):
                    for which in range(2):
                        for d in range(2):
                            for n in range(NCH):
                                for hp in range(2):
                                    h = slice(HD * hp, HD * hp + HD)
                                    i = slice(CH * n, CH * n + CH)
                                    c = 1024 * r + 2048 * which + T * d + CH * n
                                    o = ps[halves[1 - hp], c:c + CH]
                                    if which == 0:
                                        mm = pe.matmul(o, KN[h, r, d, i], QA[hp][h, r, d, n], start=True, stop=True)
                                    else:
                                        mm = pe.matmul(o, KD[h, r, d, i], C[h, C_I64:C_I64 + CH], start=True, stop=True)
                    mm.then_inc(s_am, 1)
                pe.wait_ge(s_ams, 4)
                pe.wait_ge(s_zin, 64)
                pe.wait_ge(s_zv, 4 * NCH)
                for s in range(4):
                    if s:
                        pe.wait_ge(s_gzc, s)
                        pe.wait_ge(s_goc, s)
                    if s < 3:
                        for r in range(2):
                            for g, h in enumerate(halves):
                                for a, d, n in lanes_at(s):
                                    other = halves[1 - g]
                                    mm = pe.matmul(bank(2 + r, GV, a * GV)[h], KDR[other, r, d, n],
                                                   ZVG[other, g, r, FIRST[s] + a], start=True, stop=True)
                        mm.then_inc(s_gz, 1)
                    for r in range(2):
                        for g in range(2):
                            for a, d, n in lanes_at(s):
                                c = ((2 * g + r) * 4 + a) * CH
                                mm = pe.matmul(ps[:, c:c + CH], ZVG[:, g, r, FIRST[s] + a], QA[g][:, r, d, n],
                                               start=True, stop=True)
                    mm.then_inc(s_go, 1)

        s_go2, s_gsq, s_gss, s_gv, s_gsd = (sem("gla_sum_ready"), sem("gla_squares_ready"), sem("gla_square_sums_ready"),
                                            sem("gla_variance_ready"), sem("gla_std_ready"))
        O4 = area(at_aq, 4 * T)
        SQ4 = area(at_aq + 4 * T, 4 * T)
        with nc.Block() as block:
            @block.vector
            def _(dve):
                dve_o(dve.tensor_tensor(O4, OF[:, 0].rearrange("p h t -> p (h t)"), OF[:, 1].rearrange("p h t -> p (h t)"),
                                        ALU.add))
                dve.sem_inc(s_go2, 1)
                dve.wait_ge(s_gss, 1)
                dve.tensor_scalar(SQ4.rearrange("p (h t) -> p h t", h=4),
                                  ps[:, 0:2048].rearrange("p (h t) -> p h t", h=4)[:, :, 0:T],
                                  1.0 / GV, EPS, ALU.mult, ALU.add).then_inc(s_gv, 1)
                dve.wait_ge(s_gsd, 1)
                dve_o(dve.reciprocal(SQ4, SQ4))
                dve_o(dve.scalar_tensor_tensor(out=SQ4, in0=SQ4, scalar=V[:, V_GNORM:V_GNORM + 1], in1=O4,
                                               op0=ALU.mult, op1=ALU.mult))
                dve_o(dve.tensor_tensor(OT[:, 0:4].rearrange("p h t -> p (h t)"), SQ4, SG.rearrange("p h t -> p (h t)"),
                                        ALU.mult))

            @block.scalar
            def _(act):
                act.wait_ge(s_go2, 1)
                act.activation(SQ4, O4, ACT.Square).then_inc(s_gsq, 1)
                act.wait_ge(s_gv, 1)
                act.activation(SQ4, SQ4, ACT.Sqrt).then_inc(s_gsd, 1)

            @block.tensor
            def _(pe):
                pe.wait_ge(s_gsq, 1)
                for h in range(4):
                    mm = pe.matmul(bank(h), ones, SQ4[:, T * h:T * h + T], start=True, stop=True)
                mm.then_inc(s_gss, 1)

        def out_block(l, at, src, end, name):
            s_o, s_oc = sem(name + "_ready"), sem(name + "_added")
            with nc.Block() as block:
                @block.sync
                def _(sp):
                    stream(sp, end)

                @block.tensor
                def _(pe):
                    linear(pe, at, range(8), src, s_o, s_oc)

                @block.vector
                def _(dve):
                    for m in range(KC):
                        dve.wait_ge(s_o, m + 1)
                        if m % 2 == 1:
                            dve.sem_inc(w_used, 1)
                        for c, a, b in STREAMS:
                            last = dve.scalar_tensor_tensor(out=XT[:, m, a:b], in0=bank(m)[:, a:b],
                                                            scalar=mod[:, l, 2, m, c:c + 1], in1=XT[:, m, a:b],
                                                            op0=ALU.mult, op1=ALU.add)
                        last.then_inc(s_oc, 1)

        out_block(0, AT_OUT, OT, AT_OUT + N_OUT + RING, "mixer0_out")

        def moe_block(l, at, end):
            tag = f"moe{l}_"
            m0 = 2 * T
            ACC = area(m0, KC * T, k=KC, t=T)
            r0 = m0 + KC * T
            WR = area(r0, KC * 20, k=KC, e=20)
            BR = area(r0 + 160, 20)
            LG = area(r0 + 180, 60, a=3, e=20)
            RW = area(r0 + 240, 3 * 64, a=3, e=64)
            MK = area(r0 + 432, 3 * NE, a=3, e=NE)
            SLOT = area(r0 + 480, 3 * NE, a=3, e=NE)
            CNT = area(r0 + 531, 1)
            CNTI = A[:, r0 + 532:r0 + 533].bitcast(I32)
            OFF = area(r0 + 533, NE)
            OFFI = A[:, r0 + 549:r0 + 549 + NE].bitcast(I32)
            ONE = area(r0 + 565, 3 * NE, a=3, e=NE)
            S12 = area(r0 + 613, 6, x=2, a=3)
            RC = area(r0 + 619, SLOTS + P)
            b0 = r0 + 619 + SLOTS + P
            IOTA, BEFORE = RC[:, 0:SLOTS], RC[:, SLOTS:SLOTS + P]
            s_rw, s_lg, s_m, s_ex, s_mk, s_rk, s_gu, s_silu, s_hid, s_dn, s_acc, s_ord = (sem(tag + n) for n in (
                "router_weights_in", "logits_ready", "router_max_ready", "router_exps_ready", "assignment_ready",
                "ranks_ready", "gate_up_ready", "silu_ready", "hidden_ready", "products_to_add_ready", "products_added",
                "dve_order"))
            GATES = RW[:, :, 0:16]
            with nc.Block() as block:
                @block.sync
                def _(sp):
                    sp.dma_start(WR, wrt[l]).then_inc(s_rw, 16)
                    sp.dma_start(BR, brt[l].partition_broadcast(P)).then_inc(s_rw, 16)
                    sp.dma_start(RC, rcst).then_inc(s_rw, 16)
                    sp.wait_ge(s_rw, 48)

                @block.tensor
                def _(pe):
                    pe.wait_ge(s_rw, 48)
                    for a in range(3):
                        for k in range(KC):
                            mm = pe.matmul(bank(0, 20, 20 * a), HT[:, k, P * a:P * a + P], WR[:, k, :],
                                           start=k == 0, stop=k == KC - 1)
                    mm.then_inc(s_lg, 1)
                    pe.wait_ge(s_mk, 1)
                    for a in range(3):
                        for b in range(a + 1):
                            pe.matmul(bank(1, NE, NE * a), ones if b < a else BEFORE, MK[:, b], start=b == 0, stop=b == a)
                    for b in range(3):
                        mm = pe.matmul(bank(1, NE, NE * 3), ones, MK[:, b], start=b == 0, stop=b == 2)
                    mm.then_inc(s_rk, 1)

                @block.scalar
                def _(act):
                    act.wait_ge(s_m, 1)
                    for a in range(3):
                        act_o.inc(act.activation(RW[:, a, 44:48], LG[:, a, 0:4], ACT.Exp, bias=RW[:, a, 40:41],
                                                 accum_out=RW[:, a, 48:49]))
                        act_o.inc(act.activation(RW[:, a, 49:50], RW[:, a, 38:39], ACT.Exp, bias=RW[:, a, 39:40]))
                    act_o.wait()
                    act.sem_inc(s_ex, 1)

                @block.vector
                def _(dve):
                    dve_o.inc(dve.memset(ACC, 0.0))
                    dve.wait_ge(s_rw, 48)
                    dve.wait_ge(s_lg, 1)
                    dve_o(dve.tensor_tensor(LG, bank(0, 60).rearrange("p (a e) -> p a e", a=3),
                                            BR.unsqueeze(1).broadcast_to([P, 3, 20]), ALU.add))

                    def first_max(x, one, mx, t):
                        dve_o(dve.tensor_reduce(mx, x, AX, ALU.max))
                        dve_o(dve.tensor_tensor(one, x, mx.broadcast_to([P, 3, 4]), ALU.is_equal))
                        dve_o(dve.tensor_scalar(t, one[:, :, 0:1], -1.0, 1.0, ALU.mult, ALU.add))
                        for j in range(1, 4):
                            dve_o(dve.tensor_tensor(one[:, :, j:j + 1], one[:, :, j:j + 1], t, ALU.mult))
                            if j < 3:
                                dve_o(dve.tensor_tensor(t, t, one[:, :, j:j + 1], ALU.subtract))

                    G = RW[:, :, 16:20]
                    first_max(LG[:, :, 0:4], G, RW[:, :, 50:51], RW[:, :, 51:52])
                    sel = RW[:, :, 20:24]
                    by_group = GATES.rearrange("p a (g j) -> p a g j", g=NG)
                    gb = G.unsqueeze(3).broadcast_to([P, 3, NG, EPG])
                    dve_o(dve.tensor_tensor(by_group, LG[:, :, 4:20].rearrange("p a (g j) -> p a g j", g=NG), gb, ALU.mult))
                    dve_o(dve.tensor_reduce(sel, GATES.rearrange("p a (g j) -> p a j g", g=NG), AX, ALU.add))
                    F1, F2 = RW[:, :, 24:28], RW[:, :, 28:32]
                    first_max(sel, F1, RW[:, :, 52:53], RW[:, :, 51:52])
                    sel2 = RW[:, :, 32:36]
                    dve_o(dve.tensor_scalar(sel2, F1, -3.0e38, None, ALU.mult))
                    dve_o(dve.tensor_tensor(sel2, sel2, sel, ALU.add))
                    first_max(sel2, F2, RW[:, :, 38:39], RW[:, :, 51:52])
                    dve_o(dve.tensor_scalar(RW[:, :, 39:40], RW[:, :, 52:53], -1.0, None, ALU.mult))
                    dve_o(dve.tensor_scalar(RW[:, :, 40:41], RW[:, :, 50:51], -1.0, None, ALU.mult))
                    dve.sem_inc(s_m, 1)
                    dve_o(dve.tensor_tensor(sel2, F1, F2, ALU.add))
                    mk4 = MK.rearrange("p a (g j) -> p a g j", g=NG)
                    dve_o(dve.tensor_tensor(mk4, gb, sel2.unsqueeze(2).broadcast_to([P, 3, NG, EPG]), ALU.mult))
                    dve.sem_inc(s_mk, 1)
                    chosen = (RW[:, :, 56:60], RW[:, :, 60:64])
                    for f, kept in zip((F1, F2), chosen):
                        dve_o.inc(dve.tensor_copy(kept, f))
                    dve.wait_ge(s_ex, 1)
                    x1, den = RW[:, :, 49:50], RW[:, :, 53:54]
                    dve_o(dve.tensor_scalar(den, x1, 1.0, None, ALU.add))
                    dve_o(dve.tensor_tensor(den, den, RW[:, :, 48:49], ALU.mult))
                    dve_o(dve.reciprocal(RW[:, :, 54:55], den))
                    dve_o(dve.tensor_tensor(RW[:, :, 55:56], RW[:, :, 54:55], x1, ALU.mult))
                    dve_o(dve.tensor_tensor(F1, F1, RW[:, :, 54:55].broadcast_to([P, 3, 4]), ALU.mult))
                    dve_o(dve.tensor_tensor(F2, F2, RW[:, :, 55:56].broadcast_to([P, 3, 4]), ALU.mult))
                    dve_o(dve.tensor_tensor(F1, F1, F2, ALU.add))
                    dve_o(dve.tensor_tensor(by_group, gb, F1.unsqueeze(2).broadcast_to([P, 3, NG, EPG]), ALU.mult))
                    dve.wait_ge(s_rk, 1)
                    totals = bank(1, NE, NE * 3)
                    dve_o(dve.tensor_reduce(CNT, totals, AX, ALU.max))
                    dve_o(dve.tensor_copy(CNTI, CNT))
                    dve_o(dve.tensor_tensor_scan(OFF, C[:, C_ONES:C_ONES + NE], totals, 0.0, ALU.mult, ALU.add))
                    dve_o(dve.tensor_tensor(OFF, OFF, totals, ALU.subtract))
                    dve_o.inc(dve.tensor_copy(OFFI, OFF))
                    dve_o(dve.tensor_tensor(SLOT, bank(1, 3 * NE).rearrange("p (a e) -> p a e", a=3),
                                            OFF.unsqueeze(1).broadcast_to([P, 3, NE]), ALU.add))
                    for x, kept in enumerate(chosen):
                        one4 = ONE.rearrange("p a (g j) -> p a g j", g=NG)
                        dve_o(dve.tensor_tensor(one4, gb, kept.unsqueeze(2).broadcast_to([P, 3, NG, EPG]), ALU.mult))
                        dve_o(dve.tensor_tensor(ONE, ONE, SLOT, ALU.mult))
                        dve_o(dve.tensor_reduce(S12[:, x, :].unsqueeze(2), ONE, AX, ALU.add))

            TOK = area(b0, KC * (SLOTS + CAP), k=KC, s=SLOTS + CAP)
            o1 = b0 + KC * (SLOTS + CAP)
            OUTT = area(o1, KC * (SLOTS + CAP), k=KC, s=SLOTS + CAP)
            o2 = o1 + KC * (SLOTS + CAP)
            HR = area(o2, 3 * D, a=3, d=D)
            SEL = area(o2 + 3 * D, 3 * SLOTS, a=3, s=SLOTS)
            SELG = area(o2 + 3 * D + 3 * SLOTS, 3 * SLOTS, a=3, s=SLOTS)
            NST = SLOTS // P
            OUTR = area(o2, NST * D, s=NST, d=D)
            o3 = o2 + 3 * D + 6 * SLOTS
            SGT = area(o3, NST * T, s=NST, t=T)
            HIDG = area(o3 + NST * T, 4 * CAP, f=4, s=CAP)
            SLG = area(o3 + NST * T + 4 * CAP, 2 * CAP, b=2, s=CAP)
            assert o3 + NST * T + 6 * CAP <= 30880 and NST * D <= 3 * D + 6 * SLOTS
            GB = area(b0, NE * T, e=NE, t=T)
            HID = area(b0 + NE * T, 4 * T, f=4, t=T)
            SL = area(b0 + (NE + 4) * T, 2 * T, b=2, t=T)
            GT = area(b0 + (NE + 6) * T, T)
            s_hr, s_sl, s_ga, s_hg, s_tr, s_sgt, s_tr2, s_ou, s_ous = (sem(tag + n) for n in (
                "token_rows_stored", "slots_ready", "gather_ready", "gather_stored", "turned_ready",
                "turned_gates_stored", "turned_outputs_stored", "expert_out_ready", "expert_out_stored"))

            with nc.Block() as block:
                @block.sync
                def _(sp):
                    stream(sp, end)

                def gathered_pe(pe):
                    for j in range(6):
                        for i in range(4):
                            k = 4 * (j % 2) + i
                            mm = pe.transpose(bank(j, P, P * i), HT[:, k, P * (j // 2):P * (j // 2) + P], ident)
                        if j % 2:
                            mm.then_inc(s_ga, 1)
                    pe.wait_ge(s_hr, 3)
                    pe.wait_ge(s_sl, 1)
                    for g in range(2 * KC):
                        if g >= 8:
                            pe.wait_ge(s_hg, g - 7)
                        for a in range(3):
                            mm = pe.matmul(bank(g % 8), HR[:, a, P * (g // 2):P * (g // 2) + P],
                                           SEL[:, a, T * (g % 2):T * (g % 2) + T], start=a == 0, stop=a == 2)
                        mm.then_inc(s_ga, 1)
                    pe.wait_ge(s_sl, 2)
                    for s in range(NST):
                        pe.wait_ge(s_hg, 9 + s)
                        for a in range(3):
                            mm = pe.transpose(bank(s, P, P * a), SELG[:, a, P * s:P * s + P], ident)
                        mm.then_inc(s_tr, 1)
                    pe.wait_ge(s_hg, 2 * KC)
                    pe.wait_ge(s_sgt, NST)
                    with pe.Fori(0, NE // 2) as i:
                        firsts = [pe.value_load(OFFI[0:1, bass.ds(i * 2 + u, 1)], min_val=0, max_val=SLOTS)
                                  for u in range(2)]
                        for u, first in enumerate(firsts):
                            e = i * 2 + u
                            for f in range(4):
                                pe.wait_ge(s_hid, e * 4 + (f + 1))
                                for w in range(2):
                                    n = at + 2 * (f // 2) + w
                                    if f % 2 == 0:
                                        tile_in(pe, n, e)
                                    wt = tile(n, k=KC, c=256)
                                    for k in range(KC):
                                        mm = pe.matmul(bank(f % 2, CAP, CAP * w), wt[:, k, f % 2 * P:f % 2 * P + P],
                                                       TOK[:, k, bass.ds(first, CAP)], start=k == 0, stop=k == KC - 1)
                                mm.then_inc(s_gu, 1)
                            pe.wait_ge(s_hid, e * 4 + 5)
                            for j in range(2):
                                n = at + 4 + j
                                tile_in(pe, n, e)
                                wt = tile(n, f=4, c=512)
                                pe.wait_ge(s_ous, e * 2 + (j + 1))
                                for m in range(4):
                                    for f in range(4):
                                        if j == 0 and m == 0 and f == 3:
                                            pe.wait_ge(s_hid, e * 4 + 6)
                                        mm = pe.matmul(bank(4 + j, CAP, CAP * m), wt[:, f, P * m:P * m + P], HIDG[:, f, :],
                                                       start=f == 0, stop=f == 3)
                                mm.then_inc(s_ou, 1)
                    pe.wait_ge(s_ous, 2 * NE + 2)
                    for g in range(2 * NST):
                        if g >= 8:
                            pe.wait_ge(s_tr2, g - 7)
                        for i in range(4):
                            k = 4 * (g % 2) + i
                            mm = pe.transpose(bank(g % 8, P, P * i), OUTT[:, k, P * (g // 2):P * (g // 2) + P], ident)
                        mm.then_inc(s_tr, 1)
                    pe.wait_ge(s_tr2, 2 * NST)
                    for m in range(KC):
                        for s in range(NST):
                            mm = pe.matmul(bank(m), OUTR[:, s, P * m:P * m + P], SGT[:, s, :], start=s == 0, stop=s == NST - 1)
                        mm.then_inc(s_dn, 1)

                def gathered_act(act):
                    for a in range(3):
                        act.wait_ge(s_ga, a + 1)
                        act.activation(HR[:, a, :], ps[:, 1024 * a:1024 * a + 1024], ACT.Copy).then_inc(s_hr, 1)
                    for g in range(2 * KC):
                        act.wait_ge(s_ga, 4 + g)
                        act.activation(TOK[:, g // 2, T * (g % 2):T * (g % 2) + T], bank(g % 8), ACT.Copy).then_inc(s_hg, 1)
                    for s in range(NST):
                        act.wait_ge(s_tr, s + 1)
                        act.activation(SGT[:, s, :], bank(s), ACT.Copy).then_inc(s_sgt, 1)
                    with act.Fori(0, NE) as e:
                        for f in range(4):
                            act.wait_ge(s_gu, e * 4 + (f + 1))
                            act.wait_ge(s_hid, e * 4 + (f + 1))
                            act.activation(SLG[:, f % 2, :], bank(f % 2, CAP), ACT.Silu).then_inc(s_silu, 1)
                            if f % 2 == 1:
                                act.sem_inc(w_used, 2)
                        for j in range(2):
                            act.wait_ge(s_ou, e * 2 + (j + 1))
                            act.sem_inc(w_used, 1)
                    for g in range(2 * NST):
                        act.wait_ge(s_tr, NST + g + 1)
                        act.activation(OUTR[:, g // 2, 512 * (g % 2):512 * (g % 2) + 512], bank(g % 8, 512),
                                       ACT.Copy).then_inc(s_tr2, 1)

                def gathered_dve(dve):
                    order = Order(dve, s_ord)
                    for a in range(3):
                        order.inc(dve.tensor_scalar(SEL[:, a, :], IOTA, S12[:, 0, a:a + 1], None, ALU.is_equal))
                    order.wait()
                    for a in range(3):
                        order.inc(dve.scalar_tensor_tensor(out=SEL[:, a, :], in0=IOTA, scalar=S12[:, 1, a:a + 1],
                                                           in1=SEL[:, a, :], op0=ALU.is_equal, op1=ALU.add))
                    order.wait()
                    dve.sem_inc(s_sl, 1)
                    GTMP = OUTT[:, 0:3, 0:SLOTS]
                    for a in range(3):
                        order.inc(dve.tensor_scalar(SELG[:, a, :], IOTA, S12[:, 0, a:a + 1], RW[:, a, 54:55],
                                                    ALU.is_equal, ALU.mult))
                        order.inc(dve.tensor_scalar(GTMP[:, a, :], IOTA, S12[:, 1, a:a + 1], RW[:, a, 55:56],
                                                    ALU.is_equal, ALU.mult))
                    order.wait()
                    for a in range(3):
                        order.inc(dve.tensor_tensor(SELG[:, a, :], SELG[:, a, :], GTMP[:, a, :], ALU.add))
                    order.inc(dve.memset(TOK[:, :, SLOTS:SLOTS + CAP], 0.0))
                    order.wait()
                    dve.sem_inc(s_sl, 1)
                    dve.sem_inc(s_hid, 2)
                    dve.sem_inc(s_ous, 2)
                    with dve.Fori(0, NE) as e:
                        first = dve.value_load(OFFI[0:1, bass.ds(e, 1)], min_val=0, max_val=SLOTS)
                        for f in range(4):
                            dve.wait_ge(s_silu, e * 4 + (f + 1))
                            dve.tensor_tensor(HIDG[:, f, :], SLG[:, f % 2, :], bank(f % 2, CAP, CAP),
                                              ALU.mult).then_inc(s_hid, 1)
                        for j in range(2):
                            dve.wait_ge(s_ou, e * 2 + (j + 1))
                            dve.wait_ge(s_ous, e * 2 + (j + 1))
                            dve.tensor_copy(OUTT[:, 4 * j:4 * j + 4, bass.ds(first, CAP)],
                                            bank(4 + j, 4 * CAP).rearrange("p (m s) -> p m s", m=4)).then_inc(s_ous, 1)
                    for m in range(KC):
                        dve.wait_ge(s_dn, m + 1)
                        for c, a, b in STREAMS:
                            order.inc(dve.scalar_tensor_tensor(out=XT[:, m, a:b], in0=bank(m)[:, a:b],
                                                               scalar=mod[:, l, 5, m, c:c + 1], in1=XT[:, m, a:b],
                                                               op0=ALU.mult, op1=ALU.add))
                    order.wait()

                def general_pe(pe):
                    for a in range(3):
                        mm = pe.transpose(bank(1, P, P * a)[0:NE], GATES[:, a, :], ident)
                    mm.then_inc(s_tr, 1)
                    pe.wait_ge(s_sgt, 1)
                    for e in range(NE):
                        if e >= 4:
                            pe.wait_ge(s_hg, e - 3)
                        pe.matmul(bank(4 + e % 4), ident[0:NE, e:e + 1].broadcast_to([NE, P]), GT[0:NE, :],
                                  start=True, stop=True).then_inc(s_ga, 1)
                    pe.wait_ge(s_hg, NE)
                    with pe.Fori(0, NE) as e:
                        for f in range(4):
                            pe.wait_ge(s_hid, e * 4 + (f + 1))
                            for w in range(2):
                                n = at + 2 * (f // 2) + w
                                if f % 2 == 0:
                                    tile_in(pe, n, e)
                                wt = tile(n, k=KC, c=256)
                                for k in range(KC):
                                    mm = pe.matmul(bank(2 * (f % 2) + w), wt[:, k, f % 2 * P:f % 2 * P + P], HT[:, k, :],
                                                   start=k == 0, stop=k == KC - 1)
                            mm.then_inc(s_gu, 1)
                            if f % 2 == 1:
                                pe.wait_ge(s_gu, e * 4 + (f + 1))
                                pe.sem_inc(w_used, 2)
                        pe.wait_ge(s_hid, e * 4 + 6)
                        for m in range(8):
                            n = at + 4 + m // 4
                            if m % 4 == 0:
                                tile_in(pe, n, e)
                            pe.wait_ge(s_acc, e * 8 + (m + 1))
                            wt = tile(n, f=4, c=512)
                            for f in range(4):
                                mm = pe.matmul(bank(4 + m % 4), wt[:, f, m % 4 * P:m % 4 * P + P], HID[:, f, :],
                                               start=f == 0, stop=f == 3)
                            mm.then_inc(s_dn, 1)
                            if m % 4 == 3:
                                pe.wait_ge(s_dn, e * 8 + (m + 1))
                                pe.sem_inc(w_used, 1)

                def general_act(act):
                    act.wait_ge(s_tr, 1)
                    act.activation(GT[0:NE, :], bank(1)[0:NE], ACT.Copy).then_inc(s_sgt, 1)
                    for e in range(NE):
                        act.wait_ge(s_ga, e + 1)
                        act.activation(GB[:, e, :], bank(4 + e % 4), ACT.Copy).then_inc(s_hg, 1)
                    with act.Fori(0, NE) as e:
                        for f in range(4):
                            act.wait_ge(s_gu, e * 4 + (f + 1))
                            act.wait_ge(s_hid, e * 4 + (f + 1))
                            act.activation(SL[:, f % 2, :], bank(2 * (f % 2)), ACT.Silu).then_inc(s_silu, 1)

                def general_dve(dve):
                    order = Order(dve, s_ord)
                    dve.sem_inc(s_hid, 2)
                    dve.sem_inc(s_acc, 4)
                    dve.wait_ge(s_hg, NE)
                    with dve.Fori(0, NE) as e:
                        order.enter(e, 4)
                        for f in range(4):
                            dve.wait_ge(s_silu, e * 4 + (f + 1))
                            order(dve.tensor_tensor(SL[:, f % 2, :], SL[:, f % 2, :], bank(2 * (f % 2) + 1), ALU.mult))
                            dve.tensor_tensor(HID[:, f, :], SL[:, f % 2, :],
                                              GB[:, bass.ds(e, 1), :].rearrange("p a t -> p (a t)"),
                                              ALU.mult).then_inc(s_hid, 1)
                        order.leave(NE)
                        for m in range(8):
                            dve.wait_ge(s_dn, e * 8 + (m + 1))
                            dve.wait_ge(s_acc, e * 8 + (m + 1))
                            dve.tensor_tensor(ACC[:, m, :], ACC[:, m, :], bank(4 + m % 4), ALU.add).then_inc(s_acc, 1)
                    dve.wait_ge(s_acc, 4 + 8 * NE)
                    for m in range(KC):
                        for c, a, b in STREAMS:
                            order.inc(dve.scalar_tensor_tensor(out=XT[:, m, a:b], in0=ACC[:, m, a:b],
                                                               scalar=mod[:, l, 5, m, c:c + 1], in1=XT[:, m, a:b],
                                                               op0=ALU.mult, op1=ALU.add))
                    order.wait()

                def by_load(eng, gathered, general):
                    most = eng.value_load(CNTI[0:1, 0:1])
                    with eng.If(most < CAP + 1):
                        gathered(eng)
                    with eng.Else():
                        general(eng)

                @block.tensor
                def _(pe):
                    by_load(pe, gathered_pe, general_pe)

                @block.scalar
                def _(act):
                    by_load(act, gathered_act, general_act)

                @block.vector
                def _(dve):
                    by_load(dve, gathered_dve, general_dve)

        norm_block(0, 1, AT_MOE0 + RING)
        moe_block(0, AT_MOE0, AT_RKV + RING)

        norm_block(1, 0, AT_RKV + RING)
        a_[0] = 0
        XX = area(take(KC * T), KC * T, k=KC, t=T)
        XM = [area(take(KC * T), KC * T, k=KC, t=T) for _ in range(2)]
        RT, KT, VT, GG = (area(take(KC * T), KC * T, k=KC, t=T) for _ in range(4))
        LH = area(take(2 * T), 2 * T, d=2, t=T)
        WA2 = area(take(2 * D), 2 * D, d=2, k=KC, c=P)
        GHID = area(take(T), T)
        at_top = a_[0]
        assert at_top <= 30880
        WO_EARLY = 2
        s_xx, s_xm, s_pj, s_pjc, s_wa = (sem("shift_ready"), sem("mixed_input_ready"), sem("rwkv_product_ready"),
                                         sem("rwkv_product_stored"), sem("second_factors_in"))
        with nc.Block() as block:
            MIX = (0, 2, 3, 1, 4, 5)

            @block.sync
            def _(sp):
                sp.dma_start(WA2, wa2).then_inc(s_wa, 16)
                stream(sp, AT_WO + WO_EARLY)
                sp.wait_ge(s_wa, 16)

            @block.vector
            def _(dve):
                for _, a, b in STREAMS:
                    dve_o.inc(dve.tensor_tensor(XX[:, :, a + 1:b - 1], HT[:, :, a:b - 2], HT[:, :, a + 2:b], ALU.add))
                    dve_o.inc(dve.tensor_copy(XX[:, :, a:a + 1], HT[:, :, a + 1:a + 2]))
                    dve_o.inc(dve.tensor_copy(XX[:, :, b - 1:b], HT[:, :, b - 2:b - 1]))
                dve_o.wait()
                dve_o(dve.scalar_tensor_tensor(out=XX.rearrange("p k t -> p (k t)"), in0=XX.rearrange("p k t -> p (k t)"),
                                               scalar=0.5, in1=HT_[:, :], op0=ALU.mult, op1=ALU.subtract))
                done = (0, 0, 8, 16, 24, 26)
                for x, mu in enumerate(MIX):
                    if x >= 2:
                        dve.wait_ge(s_pj, done[x])
                    for k in range(KC):
                        last = dve.scalar_tensor_tensor(out=XM[x % 2][:, k, :], in0=XX[:, k, :],
                                                        scalar=V[:, V_MU + KC * mu + k:V_MU + KC * mu + k + 1],
                                                        in1=HT[:, k, :], op0=ALU.mult, op1=ALU.add)
                        dve_o.inc(last)
                    dve_o.wait()
                    dve.sem_inc(s_xm, 1)

            @block.tensor
            def _(pe):
                for x in range(3):
                    pe.wait_ge(s_xm, x + 1)
                    linear(pe, AT_RKV, range(8 * x, 8 * x + 8), XM[x % 2], s_pj, s_pjc)
                tile_in(pe, AT_LORA)
                w = tile(AT_LORA, k=KC, c=256)
                for x in range(3, 5):
                    pe.wait_ge(s_xm, x + 1)
                    for d in range(2):
                        u = 2 * (x - 3) + d
                        pe.wait_ge(s_pjc, 24 + u - 7)
                        o = bank(u)[HD * (x - 3):HD * (x - 3) + HD]
                        for k in range(KC):
                            mm = pe.matmul(o, w[:, k, HD * u:HD * u + HD], XM[x % 2][:, k, :], start=k == 0, stop=k == KC - 1)
                        mm.then_inc(s_pj, 1)
                tile_in(pe, AT_GATE)
                pe.wait_ge(s_xm, 6)
                g1 = ring[:, AT_GATE % RING * TILE:AT_GATE % RING * TILE + D].rearrange("p (k c) -> p k c", k=KC)
                g2 = ring[:, AT_GATE % RING * TILE + D:AT_GATE % RING * TILE + 2 * D]
                pe.wait_ge(s_pjc, 21)
                for k in range(KC):
                    mm = pe.matmul(bank(4), g1[:, k, :], XM[1][:, k, :], start=k == 0, stop=k == KC - 1)
                mm.then_inc(s_pj, 1)
                pe.wait_ge(s_pjc, 29)
                for m in range(KC):
                    pe.matmul(bank(m), g2[:, P * m:P * m + P], GHID, start=True, stop=True).then_inc(s_pj, 1)

            @block.scalar
            def _(act):
                for m in range(37):
                    act.wait_ge(s_pj, m + 1)
                    if (m % 2 == 1 and m < 24) or m in (27, 36):
                        act.sem_inc(w_used, 1)
                    if m < 24:
                        last = act.activation((RT, KT, VT)[m // 8][:, m % 8, :], bank(m % 8), ACT.Copy)
                    elif m < 26:
                        last = act.activation(LH[0:HD, m - 24, :], bank(m - 24)[0:HD], ACT.Tanh)
                    elif m < 28:
                        last = act.activation(LH[HD:P, m - 26, :], bank(m - 24)[HD:P], ACT.Copy)
                    elif m == 28:
                        last = act.activation(GHID, bank(4), ACT.Sigmoid)
                    else:
                        last = act.activation(GG[:, m - 29, :], bank(m - 29), ACT.Copy)
                    last.then_inc(s_pjc, 1)

        U2 = 2 * T
        low = 3 * KC * T
        a_[0] = 0
        LDF, BF, BCF, KCF, KKAF, KDF, ATF, PF = (area(take(U2), U2) for _ in range(8))
        AR = area(take(2 * U2), 2 * U2, d=2, n=NCH, x=2, i=CH)
        BEB = area(take(2 * U2), 2 * U2, d=2, n=NCH, g=2, i=CH)
        assert a_[0] <= low
        a_[0] = at_top
        AB, BK = (area(take(2 * U2), 2 * U2, g=2, d=2, n=NCH, i=CH) for _ in range(2))
        RKV = area(take(3 * T), 3 * T, x=3, t=T)
        PV = area(take(PAIR_VECS), PAIR_VECS)
        LNV = area(take(2), 2)
        W2C = area(take(2 * P), 2 * P, d=2, c=P)
        KK = area(take(T), T)
        TW = area(take(2 * NCH), 2 * NCH, d=2, n=NCH)
        EW = area(take(2 * NCH), 2 * NCH, d=2, n=NCH)
        EWC = area(take(2 * NCH), 2 * NCH)
        ZF = area(take(2 * HD), 2 * HD, d=2, v=HD)
        BON = GHID
        assert a_[0] <= 30880, a_[0]
        spare = (AT_WO + WO_EARLY) % RING
        assert AT_WO % RING == (spare + RING - WO_EARLY) % RING
        b_ = [spare * TILE]

        def spare_ring(words):
            b_[0] += words
            assert b_[0] <= (spare + RING - WO_EARLY) * TILE <= RING * TILE
            return ring[:, b_[0] - words:b_[0]]

        AF, DTF, SF, M1F = (spare_ring(U2) for _ in range(4))
        KAB = spare_ring(2 * U2).rearrange("p (d n g i) -> p d n g i", d=2, n=NCH, g=2)
        DF = AF
        DC, DTC = (SF[:, x * T:x * T + T].rearrange("p (d n j) -> p d n j", d=2, j=32) for x in range(2))
        RM = spare_ring(2 * U2).rearrange("p (g d n i) -> p g d n i", g=2, d=2, i=CH)
        RH = spare_ring(4 * HD).rearrange("p (a v) -> p a v", a=4)
        ZV = spare_ring(2 * U2).rearrange("p (g x v) -> p g x v", g=2, v=HD)

        def dt(v):
            return v.rearrange("p (d t) -> p d t", d=2)

        def dn(v):
            return v.rearrange("p (d n i) -> p d n i", d=2, n=NCH)

        OD = dt(PF)
        KK2 = KCF[:, 0:T]
        NLEV = len(LEVELS) - 1
        (s_ic, s_si, s_lo, s_sg, s_ldr, s_cum, s_ksq, s_kss, s_kr, s_krr, s_cu, s_ex2, s_op, s_ma, s_ms, s_bon, s_rt, s_rst, s_cc, s_inv,
         s_ll, s_ls, s_lr, s_rh, s_rhs, s_so, s_sos, s_st, s_out, s_os, s_zu, s_osum, s_mean, s_osq, s_var2, s_vs, s_or, s_rstd, s_ln, s_pd,
         s_po) = (
            sem("rw_" + name) for name in (
                "pair_inputs_copied", "pair_state_in", "lora_products_ready", "lora_sigmoids_ready",
                "log_decay_scaled", "log_decay_summed", "kk_squares_ready",
                "kk_square_sums_ready", "kk_root_ready", "kk_scale_ready", "cumulated_ready", "decay_exps_ready",
                "operands_ready", "matrices_ready", "matrices_stored", "bonus_stored", "rows_ready", "rows_stored",
                "operands_kept", "inverse_level_ready", "level_left_ready", "level_left_stored", "level_right_ready",
                "rhs_ready", "rhs_stored", "solved_ready", "solved_stored", "step_state_products_ready", "step_out_ready", "step_out_stored",
                "state_updated", "out_sum_ready", "out_mean_ready", "out_squares_ready", "out_square_sums_ready",
                "out_variance_ready", "out_root_ready", "out_scale_ready", "norm_vectors_kept", "pair_done", "pair_state_out"))

        s_past = sem("rw_products_past_a_wait")
        pool_o = Order(nc.gpsimd, s_pool, sem("rw_pool_past_a_wait"))
        POOL_PER, DVE_PER = 27, 38
        NMA, NMS, NINV, NLL = 3, 5, 2 * (NLEV + 1), 2 * NLEV

        def chunk_products(b):
            return ps[:, 512 * b:512 * b + 2 * U2].rearrange("p (d n x i) -> p d n x i", d=2, n=NCH, x=2)

        LEFT_BANKS, RIGHT_BANKS = (3, 0), (1, 2)

        def msk(at):
            return C[:, at:at + 2 * CH].rearrange("p (d i) -> p d i", d=2).unsqueeze(2).broadcast_to([P, 2, NCH, CH])

        def msk1(at, d):
            return C[:, at + d * CH:at + d * CH + CH].unsqueeze(1).broadcast_to([P, NCH, CH])

        def each_pair(eng, core, prep):
            prep(eng, 0)
            with eng.Fori(0, KC - 1) as c:
                core(eng, c, prep)
            core(eng, KC - 1, None)

        halves = (slice(0, HD), slice(HD, P))
        with nc.Block() as block:
            @block.sync
            def _(sp):
                sp.sem_inc(s_po, 16)
                with sp.Fori(0, KC) as c:
                    sp.wait_ge(s_pd, c + 1)
                    for g, h in enumerate(halves):
                        sp.dma_start(ZV[h, g, 0:2], zrwkv[bass.ds(c, 1)].rearrange("r p d v -> (r p) d v")[h]
                                     ).then_inc(s_si, 16)
                    sp.wait_ge(s_zu, c * 3 + 2)
                    sp.dma_start(rwkv_out[bass.ds(c, 1)].rearrange("r p d v -> (r p) d v"), ZF).then_inc(s_po, 16)
                sp.wait_ge(s_po, 16 * KC + 16)

            def prep_act(act, j):
                for x, src in enumerate((RT, KT, VT)):
                    act.activation(RKV[:, x, :], src[:, bass.ds(j, 1), :].rearrange("p a t -> p (a t)"), ACT.Copy)
                act.activation(W2C, WA2[:, :, bass.ds(j, 1), :].rearrange("p d a c -> p d (a c)"), ACT.Copy)
                act.activation(PV, V[:, bass.ds(j * PAIR_VECS + V_PAIR, PAIR_VECS)], ACT.Copy).then_inc(s_ic, 1)

            def prep_act_rest(act, j):
                act.wait_ge(s_ic, j + 1)
                act.wait_ge(s_lo, j + 1)
                for d in range(2):
                    act.activation(dt(LDF)[:, d], bank(4 + d), ACT.Sigmoid, bias=PV[:, d:d + 1])
                    last = act.activation(dt(KKAF)[:, d], bank(6 + d), ACT.Sigmoid, bias=PV[:, 2 + d:3 + d])
                last.then_inc(s_sg, 1)
                act.wait_ge(s_kss, j + 1)
                act.activation(KK2, bank(4), ACT.Sqrt, bias=C[:, C_TINY:C_TINY + 1]).then_inc(s_kr, 1)
                act.wait_ge(s_cu, j + 1)
                act.activation(EW, TW, ACT.Exp)
                al, rho = (AR[:, :, :, x, :] for x in range(2))
                act.activation(al, al, ACT.Exp)
                act.activation(rho, dn(BF), ACT.Exp)
                act.activation(LDF, BF, ACT.Exp, scale=-1.0)
                act.activation(BCF, BCF, ACT.Exp).then_inc(s_ex2, 1)

            def prep_act_all(act, j):
                prep_act(act, j)
                prep_act_rest(act, j)

            def prep_pool(pool, j):
                r_, k_ = RKV[:, 0, :], RKV[:, 1, :]
                b, ld = dt(BF), dt(LDF)
                kb, kkb = (v.unsqueeze(1).broadcast_to([P, 2, T]) for v in (k_, KK))
                kkc, rc = (v.rearrange("p (n i) -> p n i", i=CH).unsqueeze(1).broadcast_to([P, 2, NCH, CH])
                           for v in (KK, r_))
                al, rho = (AR[:, :, :, x, :] for x in range(2))
                pool.wait_ge(s_ic, j + 1)
                pool.sem_inc(pool_o.past, 1)
                pool_o(pool.tensor_scalar(KK, k_, PV[:, 4:5], None, ALU.mult))
                pool_o(pool.tensor_tensor(KK2, KK, KK, ALU.mult))
                pool.sem_inc(s_ksq, 1)
                pool.wait_ge(s_sg, j + 1)
                pool.sem_inc(pool_o.past, 1)
                pool_o(pool.tensor_scalar(LDF, LDF, -HALF_DECAY, None, ALU.mult))
                pool.sem_inc(s_ldr, 1)
                pool_o(pool.tensor_scalar(KDF, KKAF, -1.0, PV[:, 5:6], ALU.add, ALU.mult))
                pool_o(pool.tensor_scalar(KDF, KDF, 1.0, None, ALU.add))
                pool_o.inc(pool.tensor_tensor(dt(KDF), dt(KDF), kb, ALU.mult))
                pool.wait_ge(s_cum, j + 1)
                pool.sem_inc(pool_o.past, 1)
                pool_o(pool.tensor_copy(TW, dn(BF)[:, :, :, CH - 1]))
                pool_o(pool.tensor_tensor(b[:, 1], ld[:, 1], b[:, 1], ALU.subtract))
                pool_o(pool.tensor_tensor(dn(BF)[:, 1], dn(BF)[:, 1],
                                          TW[:, 1].unsqueeze(2).broadcast_to([P, NCH, CH]), ALU.add))
                pool.wait_ge(s_cc, j + 1)
                pool_o.inc(pool.tensor_tensor(al, dn(BF), dn(LDF), ALU.subtract))
                pool_o.inc(pool.tensor_tensor(BCF.rearrange("p (n i) -> p n i", i=CH),
                                              TW.rearrange("p d n -> p (d n)").unsqueeze(2).broadcast_to([P, 2 * NCH, CH]),
                                              BF.rearrange("p (n i) -> p n i", i=CH), ALU.subtract))
                pool_o.wait()
                pool.sem_inc(s_cu, 1)
                pool.wait_ge(s_ex2, j + 1)
                pool_o(pool.tensor_tensor(rho, rho, rc, ALU.mult))
                for g, h in enumerate(halves):
                    pool_o(pool.tensor_tensor(KAB[h, :, :, 1 - g, :], dn(KDF)[h], dn(LDF)[h], ALU.mult))
                pool.wait_ge(s_krr, j + 1)
                pool_o(pool.tensor_tensor(KK, KK, KK2, ALU.mult))
                pool_o.inc(pool.tensor_tensor(dt(KKAF), dt(KKAF), kkb, ALU.mult))
                pool_o.inc(pool.tensor_tensor(al, al, kkc, ALU.mult))
                pool_o.wait()
                for g, h in enumerate(halves):
                    pool_o(pool.tensor_tensor(BEB[h, :, :, g, :], dn(KKAF)[h], dn(LDF)[h], ALU.mult))
                pool_o.inc(pool.tensor_tensor(KCF, KDF, BCF, ALU.mult))
                pool_o.wait()
                pool_o.inc(pool.tensor_tensor(BCF, KKAF, BCF, ALU.mult))
                pool_o(pool.tensor_tensor(KK, dt(KDF)[:, 0], dt(KDF)[:, 1], ALU.add))
                pool_o(pool.tensor_scalar(KK, KK, 0.5, PV[:, 6:7], ALU.mult, ALU.mult))
                pool_o(pool.tensor_tensor(KK, KK, r_, ALU.mult))
                pool.sem_inc(s_op, 1)

            def prep_dve(dve, j):
                dve.wait_ge(s_ldr, j + 1)
                for d in range(2):
                    last = dve.tensor_tensor_scan(dt(BF)[:, d], C[:, C_KEEP:C_KEEP + T], dt(LDF)[:, d], 0.0,
                                                  ALU.mult, ALU.add)
                last.then_inc(s_cum, 1)

            def prep_dve_root(dve, j):
                dve.wait_ge(s_kr, j + 1)
                dve.reciprocal(KK2, KK2).then_inc(s_krr, 1)

            def wait(pe, s, value):
                pe.wait_ge(s, value)
                pe.sem_inc(s_past, 1)

            def prep_pe_lora(pe, j):
                wait(pe, s_ic, j + 1)
                for d in range(2):
                    for g in range(2):
                        mm = pe.matmul(bank(4 + 2 * g + d), W2C[halves[g], d], LH[halves[g], d], start=True, stop=True)
                mm.then_inc(s_lo, 1)

            def prep_pe_norm(pe, j):
                wait(pe, s_ksq, j + 1)
                wait(pe, s_sg, j + 1)
                pe.matmul(bank(4), heads, KK2, start=True, stop=True).then_inc(s_kss, 1)

            def prep_pe(pe, j):
                prep_pe_lora(pe, j)
                prep_pe_norm(pe, j)

            def core_act(act, c, prep):
                act.wait_ge(s_pd, c + 1)
                for x in range(3):
                    act.wait_ge(s_rt, c * 3 + (x + 1))
                    for g, h in enumerate(halves):
                        rows = ps[0:HD, 2048:2048 + 2 * NCH * P].rearrange("p (n g k) -> p n g k", g=2, k=HD)[:, :, g, :]
                        dst = (BK[h, g].rearrange("p d n k -> p (d n) k"),
                               BK[halves[1 - g], g].rearrange("p d n k -> p (d n) k"), ZV[halves[1 - g], g])[x]
                        last = act.activation(dst, rows, ACT.Copy)
                    last.then_inc(s_rst, 1)
                act.activation(LNV, PV[:, 7:9], ACT.Copy).then_inc(s_ln, 1)
                if prep:
                    act.wait_ge(s_bon, c + 1)
                    act.wait_ge(s_ln, c + 1)
                    prep_act(act, c + 1)
                for s in range(4):
                    for a, d, n in lanes_at(s):
                        act.activation(EWC[:, FIRST[s] + a:FIRST[s] + a + 1], EW[:, d, n:n + 1], ACT.Copy)
                for g, h in enumerate(halves):
                    act.activation(AB[h, g], AR[h, :, :, 0, :], ACT.Copy)
                    last = act.activation(RM[h, g], AR[h, :, :, 1, :], ACT.Copy)
                last.then_inc(s_cc, 1)
                if prep:
                    act.wait_ge(s_cc, c + 2)
                    prep_act_rest(act, c + 1)
                act.wait_ge(s_vs, c + 2)
                act.activation(OD[:, 1], OD[:, 1], ACT.Sqrt).then_inc(s_or, 1)

            def core_dve(dve, c, prep):
                v_ = RKV[:, 2, :]
                for g, h in enumerate(halves):
                    dve_o.inc(dve.memset(ZV[h, g, 2:4], 0.0))
                block32 = C[:, C_BLOCK:C_BLOCK + CH].unsqueeze(1).broadcast_to([P, NCH, CH])
                i32 = C[:, C_I32:C_I32 + 32].unsqueeze(1).broadcast_to([P, NCH, 32])

                def split(v):
                    return v.rearrange("p n (b j) -> p n b j", b=2)

                def twice(v):
                    return v.unsqueeze(2).broadcast_to([P, NCH, 2, 32])

                for d in range(2):
                    if d:
                        dve.tensor_tensor(dn(M1F), chunk_products(0)[:, :, :, 1, :], msk(C_INCL), ALU.mult
                                          ).then_inc(s_ms, 1)
                    dve.wait_ge(s_ma, c * NMA + 1)
                    a_t = chunk_products(0)[:, d, :, 0, :]
                    dve_o.inc(dve.tensor_tensor(dn(DTF)[:, d], a_t, msk1(C_LEV1T, d), ALU.mult))
                    dve_o(dve.tensor_tensor(dn(ATF)[:, d], a_t, msk1(C_STRICT, d), ALU.mult))
                    dve.sem_inc(s_ms, 1)
                    dve_o.inc(dve.tensor_tensor(DTC[:, d], dn(DTF)[:, d, :, 0:32], dn(DTF)[:, d, :, 32:64], ALU.add))
                    dve_o(dve.tensor_tensor(dn(AF)[:, d], dn(ATF)[:, d], block32, ALU.mult))
                    dve_o(dve.tensor_tensor(DTC[:, d], i32, DTC[:, d], ALU.subtract))
                    dve.transpose(DC[:, d].rearrange("p n j -> p (n j)"),
                                  DTC[:, d].rearrange("p n j -> p (n j)")).then_inc(s_inv, 1)
                for n in range(1, NLEV + 1):
                    if n == 1:
                        dve.wait_ge(s_pd, c + 1)
                    if n == 2:
                        dve.wait_ge(s_ma, c * NMA + 3)
                        dve.tensor_tensor(BON, bank(7), v_, ALU.mult).then_inc(s_bon, 1)
                    for d in range(2):
                        dve.wait_ge(s_ll, c * NLL + (2 * n - 1 + d))
                        mask = msk1(C_LEV + 2 * (n - 1) * CH, d)
                        if n < NLEV:
                            p_ = bank(LEFT_BANKS[d], NCH * 32).rearrange("p (n j) -> p n j", j=32)
                            dve.tensor_tensor(split(dn(PF)[:, d]), twice(p_), split(mask), ALU.mult).then_inc(s_ls, 1)
                        else:
                            dve.tensor_tensor(dn(PF)[:, d], bank(LEFT_BANKS[d]).rearrange("p (n i) -> p n i", i=CH), mask, ALU.mult).then_inc(s_ls, 1)
                    if n == 1:
                        dve.wait_ge(s_ma, c * NMA + 2)
                        for x, (v, cm) in enumerate(((AB, C_STRICT), (RM, C_INCL))):
                            for g in range(2):
                                h = halves[1 - g]
                                last = dve.tensor_tensor(v[h, g], chunk_products(4)[h, :, :, x, :], msk(cm)[h], ALU.mult)
                            last.then_inc(s_ms, 1)
                    for d in range(2):
                        dve.wait_ge(s_lr, c * NLL + (2 * n - 1 + d))
                        if n == NLEV:
                            dve.tensor_tensor(dt(DTF)[:, d], dt(DTF)[:, d], bank(RIGHT_BANKS[d]),
                                              ALU.subtract).then_inc(s_inv, 1)
                            continue
                        dtc, dc = (v[:, d].rearrange("p n j -> p (n j)") for v in (DTC, DC))
                        dve_o(dve.tensor_tensor(dtc, dtc, bank(RIGHT_BANKS[d], NCH * 32), ALU.subtract))
                        last = dve.transpose(dc, dtc)
                        if n == NLEV - 1:
                            dve_o(last)
                            dve.tensor_tensor(split(dn(DF)[:, d]), twice(DC[:, d]), split(block32), ALU.mult)
                            last = dve.tensor_tensor(split(dn(DTF)[:, d]), twice(DTC[:, d]), split(block32), ALU.mult)
                        last.then_inc(s_inv, 1)
                    if n == 4 and prep:
                        prep(dve, c + 1)
                    if n == 5 and prep:
                        prep_dve_root(dve, c + 1)
                for s in range(4):
                    ln = lanes_at(s)
                    w = len(ln)
                    x = FIRST[s]

                    def lanes(b, h):
                        return bank(b, w * HD)[h].rearrange("p (a v) -> p a v", v=HD)

                    to = []
                    if s < 3:
                        more = len(lanes_at(s + 1))
                        for g, h in enumerate(halves):
                            to.append((h, g, 0, more, ZV[h, g, FIRST[s + 1]:FIRST[s + 1] + more]))
                            if more < w:
                                to.append((h, g, more, w, ZF[h]))
                    dve.wait_ge(s_rh, c * 4 + (s + 1))
                    dve.tensor_copy(RH[:, 0:w], lanes(0, slice(0, P))).then_inc(s_rhs, 1)
                    if s == 1:
                        dve.wait_ge(s_po, c * 16 + 16)
                    for h, g, a, b, new in to:
                        last = dve.tensor_tensor(new, ZV[h, g, x + a:x + b],
                                                 EWC[h, x + a:x + b].unsqueeze(2).broadcast_to([HD, b - a, HD]), ALU.mult)
                    if to:
                        dve_o(last)
                    dve.wait_ge(s_so, c * 4 + (s + 1))
                    for g, h in enumerate(halves):
                        last = dve.tensor_scalar(ZV[h, g, x:x + w], lanes(1, h), -1.0, None, ALU.mult)
                    last.then_inc(s_sos, 1)
                    if to:
                        dve.wait_ge(s_st, c * 3 + (s + 1))
                        for h, g, a, b, new in to:
                            last = dve.tensor_tensor(new, new, lanes(3, h)[:, a:b], ALU.add)
                        dve_o(last)
                        dve.sem_inc(s_zu, 1)
                    dve.wait_ge(s_out, c * 4 + (s + 1))
                    for a, d, n in ln:
                        last = dve.tensor_copy(OD[:, d, CH * n:CH * n + CH], bank(2, CH, CH * a))
                    dve_o(last)
                    for a, d, n in ln:
                        o = OD[:, d, CH * n:CH * n + CH]
                        last = dve.tensor_tensor(o, o, bank(7, CH, CH * a), ALU.add)
                    dve_o(last)
                    dve.sem_inc(s_os, 1)
                dve.tensor_tensor(OD[:, 0], OD[:, 0], OD[:, 1], ALU.add).then_inc(s_osum, 1)
                dve.wait_ge(s_mean, c + 1)
                dve_o(dve.scalar_tensor_tensor(out=OD[:, 0], in0=bank(4), scalar=-1.0 / HD, in1=OD[:, 0],
                                               op0=ALU.mult, op1=ALU.add))
                dve.tensor_tensor(OD[:, 1], OD[:, 0], OD[:, 0], ALU.mult).then_inc(s_osq, 1)
                dve.wait_ge(s_var2, c + 1)
                dve.tensor_scalar(OD[:, 1], bank(5), 1.0 / HD, LN_EPS, ALU.mult, ALU.add).then_inc(s_vs, 1)
                dve.wait_ge(s_or, c + 1)
                dve_o(dve.reciprocal(OD[:, 1], OD[:, 1]))
                dve.sem_inc(s_rstd, 1)

            def out_pool(pool, c):
                pool.wait_ge(s_rstd, c + 1)
                pool_o(pool.tensor_tensor(OD[:, 0], OD[:, 0], OD[:, 1], ALU.mult))
                pool_o(pool.tensor_scalar(OD[:, 0], OD[:, 0], LNV[:, 0:1], LNV[:, 1:2], ALU.mult, ALU.add))
                pool_o(pool.tensor_tensor(OD[:, 0], OD[:, 0], BON, ALU.add))
                pool.tensor_tensor(OT[:, bass.ds(c, 1), :].rearrange("p a t -> p (a t)"), OD[:, 0],
                                   GG[:, bass.ds(c, 1), :].rearrange("p a t -> p (a t)"), ALU.mult).then_inc(s_pd, 1)

            def core_pe(pe, c, prep):
                chunks = [(d, n) for d in range(2) for n in range(NCH)]
                by_d = (chunks[:NCH], chunks[NCH:])

                def each(banks, left, right, some, wide=CH):
                    for d, n in some:
                        for h in halves:
                            mm = pe.matmul(bank(banks[d], wide, wide * n)[h], left(h, d, n), right(h, d, n),
                                           start=True, stop=True)
                    return mm

                def mat(v):
                    return lambda h, d, n: dn(v)[h, d, n]

                def turned(v, order, bk):
                    for x, n in enumerate(order):
                        mm = pe.transpose(ps[0:HD, 512 * bk + P * x:512 * bk + P * x + P], v[:, CH * n:CH * n + CH], ident)
                    mm.then_inc(s_rt, 1)

                wait(pe, s_op, c + 1)
                for b, left in ((0, BEB), (4, KAB)):
                    if b:
                        wait(pe, s_vs, c + 1)
                    for d, n in chunks:
                        x = (d * NCH + n) * P
                        mm = pe.matmul(ps[:, 512 * b + x:512 * b + x + P], left[:, d, n], AR[:, d, n], start=True, stop=True)
                    mm.then_inc(s_ma, 1)
                pe.matmul(bank(7), heads, KK, start=True, stop=True).then_inc(s_ma, 1)
                for n in range(1, NLEV + 1):
                    for d in range(2):
                        wait(pe, s_inv, c * NINV + (2 * n - 1 + d))
                        if n == 1 and d == 1:
                            wait(pe, s_ms, c * NMS + 3)
                        if n < NLEV:
                            mm = each(LEFT_BANKS, mat(AF), lambda h, d, n: DC[h, d, n], by_d[d], wide=32)
                        else:
                            mm = each(LEFT_BANKS, mat(ATF), mat(DF), by_d[d])
                        mm.then_inc(s_ll, 1)
                    if n == 2:
                        wait(pe, s_rst, c * 3 + 1)
                        turned(KCF, range(2 * NCH), 4)
                    for d in range(2):
                        wait(pe, s_ls, c * NLL + (2 * n - 1 + d))
                        if n < NLEV:
                            mm = each(RIGHT_BANKS, mat(PF), lambda h, d, n: DTC[h, d, n], by_d[d], wide=32)
                        else:
                            mm = each(RIGHT_BANKS, mat(PF), mat(DTF), by_d[d])
                        mm.then_inc(s_lr, 1)
                    if n == 1:
                        wait(pe, s_ms, c * NMS + 5)
                        turned(BCF, range(2 * NCH), 4)
                    if n == 2:
                        wait(pe, s_rst, c * 3 + 2)
                        turned(RKV[:, 2, :], [n_ for s in range(4) for a, d, n_ in lanes_at(s)], 4)
                    if prep and n == 3:
                        wait(pe, s_rst, c * 3 + 3)
                        wait(pe, s_bon, c + 1)
                        prep_pe_lora(pe, c + 1)
                    if prep and n == 4:
                        prep_pe_norm(pe, c + 1)
                wait(pe, s_inv, c * NINV + NINV)
                wait(pe, s_si, c * 32 + 32)
                wait(pe, s_cc, c + 2)
                if not prep:
                    pe.wait_ge(s_rst, c * 3 + 3)
                    pe.wait_ge(s_bon, c + 1)
                dT, m1 = dn(DTF), dn(M1F)
                for s in range(4):
                    ln = [(g, h, FIRST[s] + a, a, d, n) for g, h in enumerate(halves) for a, d, n in lanes_at(s)]
                    if s:
                        wait(pe, s_zu, c * 3 + s)
                    for g, h, x, a, d, n in ln:
                        mm = pe.matmul(bank(0, HD, HD * a)[h], AB[:, g, d, n], ZV[:, g, x], start=True, stop=True)
                    mm.then_inc(s_rh, 1)
                    if s:
                        wait(pe, s_os, c * 4 + s)
                    for g, h, x, a, d, n in ln:
                        pe.matmul(bank(2, CH, CH * a)[h], ZV[:, g, x], RM[:, g, d, n], start=True, stop=True)
                    wait(pe, s_rhs, c * 4 + (s + 1))
                    for g, h, x, a, d, n in ln:
                        mm = pe.matmul(bank(1, HD, HD * a)[h], dT[h, d, n], RH[h, a], start=True, stop=True)
                    mm.then_inc(s_so, 1)
                    wait(pe, s_sos, c * 4 + (s + 1))
                    if s < 3:
                        for g, h, x, a, d, n in ln:
                            mm = pe.matmul(bank(3, HD, HD * a)[h], BK[:, g, d, n], ZV[:, g, x], start=True, stop=True)
                        mm.then_inc(s_st, 1)
                    for g, h, x, a, d, n in ln:
                        mm = pe.matmul(bank(7, CH, CH * a)[h], ZV[h, g, x], m1[h, d, n], start=True, stop=True)
                    mm.then_inc(s_out, 1)
                wait(pe, s_osum, c + 1)
                if prep:
                    wait(pe, s_kr, c + 2)
                pe.matmul(bank(4), heads, OD[:, 0], start=True, stop=True).then_inc(s_mean, 1)
                wait(pe, s_osq, c + 1)
                pe.matmul(bank(5), heads, OD[:, 1], start=True, stop=True).then_inc(s_var2, 1)

            @block.scalar
            def _(act):
                each_pair(act, core_act, prep_act_all)

            @block.gpsimd
            def _(pool):
                pool.sem_inc(s_pd, 1)
                pool_o.inc(pool.memset(BEB, 0.0))
                pool_o(pool.memset(KAB, 0.0))
                prep_pool(pool, 0)
                with pool.Fori(0, KC - 1) as c:
                    pool_o.enter(c, POOL_PER)
                    prep_pool(pool, c + 1)
                    out_pool(pool, c)
                    pool_o.leave(KC - 1)
                out_pool(pool, KC - 1)

            @block.vector
            def _(dve):
                dve.sem_inc(s_vs, 1)
                dve.sem_inc(s_cc, 1)
                prep_dve(dve, 0)
                prep_dve_root(dve, 0)
                with dve.Fori(0, KC - 1) as c:
                    dve_o.enter(c, DVE_PER)
                    core_dve(dve, c, prep_dve)
                    dve_o.leave(KC - 1)
                core_dve(dve, KC - 1, None)

            @block.tensor
            def _(pe):
                each_pair(pe, core_pe, prep_pe)

        out_block(1, AT_WO, OT, AT_MOE1 + RING, "mixer1_out")
        norm_block(1, 1, AT_MOE1 + RING)
        moe_block(1, AT_MOE1, N_TILES)
        norm_block(None, 0, N_TILES)


_INS = ["xT", "cst", "rcst", "vec", "sinkr", "ckT", "cv", "zgla", "zrwkv", "wrt", "brt", "dec2", "wa2", "wstream"]
_OUTS = [("yT", (P, KC * T)), ("kT_out", (HD, 2, CTX)), ("vT_out", (P, CTX)), ("gla_out", (2, P, 2, GV)),
         ("rwkv_out", (KC, P, 2, HD))]


def cols(v):
    return np.asarray(v, np.float32).reshape(-1, P).T


def tiles_of(w, width=256):
    k, n = w.shape
    return w.reshape(k // P, P, n // width, width).transpose(2, 1, 0, 3).reshape(n // width, P, -1)


def lay_out(i):
    f = {k: np.asarray(v) for k, v in i.items()}
    h = {}
    x = np.concatenate([f["x_prompt"][0], f["x_sample"][0]], 0)
    h["xT"] = np.ascontiguousarray(x.T.reshape(KC, P, T).transpose(1, 0, 2).reshape(P, KC * T))
    h["cst"] = constants()
    h["rcst"] = router_constants()
    v = np.zeros((P, V_N), np.float32)
    v[:, V_COND:V_COND + 2 * KC] = np.stack([cols(f["c_ctx"]), cols(f["c"][0])], 2).reshape(P, -1)
    v[:, V_ADA_B:V_NMIX] = cols(f["ada_b"].ravel())
    v[:, V_NMIX:V_NFFN] = cols(f["norm_mix"].ravel())
    v[:, V_NFFN:V_NOUT] = cols(f["norm_ffn"].ravel())
    v[:, V_NOUT:V_MU] = cols(f["norm_out"])
    v[:, V_MU:V_PAIR] = cols(f["rw_mu"][0].ravel())
    pair = [f["rw_w0"][0, 0], f["rw_w0"][0, 1], f["rw_a0"][0, 0], f["rw_a0"][0, 1], f["rw_kk"][0], f["rw_ka"][0],
            f["rw_rk"][0].ravel(), f["rw_lnx_w"][0], f["rw_lnx_b"][0]]
    v[:, V_PAIR:V_GNORM] = np.stack([cols(a) for a in pair], 2).reshape(P, -1)
    v[:, V_GNORM] = f["gla_norm"][0]
    v[:, V_DECB:V_DECB + 4] = f["gla_dec_b"][0].reshape(2, 2, P).transpose(2, 1, 0).reshape(P, 4)
    h["vec"] = v
    h["sinkr"] = f["att_sink"][0].copy()
    h["ckT"] = np.ascontiguousarray(f["cache_attn_k"][0, 0].transpose(2, 1, 0))
    h["cv"] = np.ascontiguousarray(f["cache_attn_v"][0, 0])
    h["zgla"] = np.ascontiguousarray(f["state_gla"][0, 0].reshape(2, 2, P, GV).transpose(1, 2, 0, 3))
    h["zrwkv"] = np.ascontiguousarray(
        f["state_rwkv"][0, 0].reshape(2, KC, 2, HD, HD).transpose(1, 2, 4, 0, 3).reshape(KC, P, 2, HD))
    wr = np.concatenate([f["moe_w_grp"], f["moe_w_exp"]], 2)
    h["wrt"] = np.ascontiguousarray(wr.reshape(2, KC, P, 20).transpose(0, 2, 1, 3))
    h["brt"] = np.concatenate([f["moe_b_grp"], f["moe_b_exp"]], 1)
    dec = np.zeros((2 * LR, 4 * P), np.float32)
    dec[:LR, :256] = f["gla_dec_w"][0, 0]
    dec[LR:, 256:] = f["gla_dec_w"][0, 1]
    h["dec2"] = dec
    h["wa2"] = np.concatenate([f["rw_w2"][0].transpose(1, 0, 2), f["rw_a2"][0].transpose(1, 0, 2)], 0
                              ).reshape(P, 2, KC, P)
    w = np.zeros((N_TILES, P, TILE), np.float32)
    for l in range(2):
        w[AT_ADA + l * MC // 2:AT_ADA + (l + 1) * MC // 2] = tiles_of(f["ada_w"][l])
    w_in = np.zeros((D, 2560), np.float32)
    w_in[:, :IN_W] = f["ev_w_in"][0]
    w[AT_IN:AT_OUT] = tiles_of(w_in)
    w[AT_OUT:AT_MOE0] = tiles_of(f["ev_w_out"][0])
    for l, at in ((0, AT_MOE0), (1, AT_MOE1)):
        for e in range(NE):
            t = at + 6 * e
            w[t:t + 4:2] = tiles_of(f["moe_w_gate"][l, e])
            w[t + 1:t + 4:2] = tiles_of(f["moe_w_up"][l, e])
            w[t + 4:t + 6] = tiles_of(f["moe_w_down"][l, e], 512)
    for n, name in enumerate(("rw_wr", "rw_wk", "rw_wv")):
        w[AT_RKV + 4 * n:AT_RKV + 4 * n + 4] = tiles_of(f[name][0])
    lora = np.concatenate([f["rw_w1"][0, 0], f["rw_w1"][0, 1], f["rw_a1"][0, 0], f["rw_a1"][0, 1]], 1)
    w[AT_LORA] = tiles_of(lora)[0]
    w[AT_GATE, :, :D] = tiles_of(f["rw_g1"][0], P)[0]
    w[AT_GATE, :, D:] = f["rw_g2"][0]
    w[AT_WO:AT_MOE1] = tiles_of(f["rw_wo"][0])
    h["wstream"] = w
    return h


def kernel(**inputs):
    import concourse.bacc as bacc
    from concourse.bass_utils import run_bass_kernel_spmd

    nc = bacc.Bacc("TRN2", target_bir_lowering=False, num_devices=1)
    arrays = lay_out(inputs)
    args = [nc.dram_tensor(n, arrays[n].shape, F32, kind="ExternalInput").ap() for n in _INS]
    args += [nc.dram_tensor(n, shape, F32, kind="ExternalOutput").ap() for n, shape in _OUTS]
    build(nc, *args)
    r = run_bass_kernel_spmd(nc, [arrays], core_ids=[0]).results[0]
    y = r["yT"].reshape(P, KC, T).transpose(2, 1, 0).reshape(1, T, D)
    k = r["kT_out"].transpose(2, 1, 0).reshape(1, 1, CTX, AKV, HD)
    v = r["vT_out"].T.reshape(1, 1, CTX, AKV, HD)
    g = r["gla_out"].reshape(2, 2, HD, 2, GV).transpose(3, 0, 1, 2, 4).reshape(1, 1, 2, GH, HD, GV)
    s = r["rwkv_out"].reshape(KC, 2, HD, 2, HD).transpose(3, 0, 1, 4, 2).reshape(1, 1, 2, 2 * KC, HD, HD)
    c = np.ascontiguousarray
    return c(y[:, :CTX]), c(y[:, CTX:]), c(k), c(v), c(g), c(s)
```
